# Optimizing a Trainium2 kernel written in Bass

```python
import math
import jax, jax.numpy as jnp
from jax import lax
import numpy as np
import math, functools

D_MODEL = 1024
BATCH = 1
SEQ = 512
DEPTH = 2

N_MIXERS = 2
N_SSM_LAYERS = (DEPTH + 1) // 2
N_ATT_LAYERS = DEPTH // 2
SSM_WIDTH = D_MODEL // 2
SSM_CH = 16
SSM_GROUPS = SSM_WIDTH // SSM_CH
SSM_STATE = 64
DT_MIN, DT_MAX = 1e-3, 1e-1
HEAD_DIM = 64
N_HEADS = D_MODEL // HEAD_DIM
N_KV_HEADS = N_HEADS // 4
KV_GROUP = N_HEADS // N_KV_HEADS
IDX_HEADS = max(4, D_MODEL // 128)
IDX_DIM = 64
TOPK_MAX = 256
Q_BLOCK = 128
ROPE_THETA = 10000.0
ATT_SPLITS = (N_HEADS * HEAD_DIM, N_KV_HEADS * HEAD_DIM, N_KV_HEADS * HEAD_DIM,
              IDX_HEADS * IDX_DIM, IDX_DIM, IDX_HEADS)
ATT_IN_COLS = sum(ATT_SPLITS)
D_FF = 4 * D_MODEL
NORM_EPS = 1e-6


def rms_norm(x, g):
    xf = x.astype(jnp.float32)
    y = xf * lax.rsqrt(jnp.mean(xf * xf, axis=-1, keepdims=True) + NORM_EPS)
    return (y * g.astype(jnp.float32)).astype(x.dtype)

def rope_tables(seq_len, dim, dtype):
    half = dim // 2
    inv_freq = ROPE_THETA ** (-jnp.arange(half, dtype=jnp.float32) * 2.0 / dim)
    ang = jnp.arange(seq_len, dtype=jnp.float32)[:, None] * inv_freq[None, :]
    cos = jnp.concatenate([jnp.cos(ang), jnp.cos(ang)], axis=-1)
    sin = jnp.concatenate([jnp.sin(ang), jnp.sin(ang)], axis=-1)
    return cos.astype(dtype), sin.astype(dtype)

def apply_rope(x, cos, sin):
    half = x.shape[-1] // 2
    rot = jnp.concatenate([-x[..., half:], x[..., :half]], axis=-1)
    return x * cos[None, :, None, :] + rot * sin[None, :, None, :]

def s5_mixer(h, w_in, lam_re, lam_im, log_dt, b_re, b_im, c_re, c_im, d_skip, w_glu, w_out):
    bsz, seq, _ = h.shape
    dt_ = h.dtype
    u = (h @ w_in).reshape(bsz, seq, SSM_GROUPS, SSM_CH)
    lr = lam_re.astype(jnp.float32); li = lam_im.astype(jnp.float32)
    dt = jnp.exp(log_dt.astype(jnp.float32))[:, None]
    mag = jnp.exp(lr * dt)
    abar_re = mag * jnp.cos(li * dt)
    abar_im = mag * jnp.sin(li * dt)
    den = lr * lr + li * li
    nr = abar_re - 1.0
    ni = abar_im
    fr = (nr * lr + ni * li) / den
    fi = (ni * lr - nr * li) / den
    br = b_re.astype(jnp.float32); bi = b_im.astype(jnp.float32)
    bbar_re = (fr[..., None] * br - fi[..., None] * bi).astype(dt_)
    bbar_im = (fr[..., None] * bi + fi[..., None] * br).astype(dt_)
    bu_re = jnp.einsum('bsgc,gpc->bsgp', u, bbar_re)
    bu_im = jnp.einsum('bsgc,gpc->bsgp', u, bbar_im)
    a_re = jnp.broadcast_to(abar_re.astype(dt_), bu_re.shape)
    a_im = jnp.broadcast_to(abar_im.astype(dt_), bu_im.shape)

    def combine(left, right):
        a1r, a1i, b1r, b1i = left
        a2r, a2i, b2r, b2i = right
        return (a2r * a1r - a2i * a1i,
                a2r * a1i + a2i * a1r,
                a2r * b1r - a2i * b1i + b2r,
                a2r * b1i + a2i * b1r + b2i)

    _, _, xs_re, xs_im = lax.associative_scan(combine, (a_re, a_im, bu_re, bu_im), axis=1)
    y = (jnp.einsum('bsgp,gcp->bsgc', xs_re, c_re)
         - jnp.einsum('bsgp,gcp->bsgc', xs_im, c_im)
         + d_skip[None, None] * u)
    z = jax.nn.gelu(y.reshape(bsz, seq, SSM_WIDTH))
    z = z * jax.nn.sigmoid(z @ w_glu)
    return z @ w_out

def dsa_mixer(h, w_in, w_out):
    bsz, seq, _ = h.shape
    dt_ = h.dtype
    proj = h @ w_in
    offs = np.cumsum(ATT_SPLITS)[:-1].tolist()
    q, k, v, qi, ki, wi = jnp.split(proj, offs, axis=-1)
    cos, sin = rope_tables(seq, HEAD_DIM, dt_)
    q = apply_rope(q.reshape(bsz, seq, N_HEADS, HEAD_DIM), cos, sin)
    k = apply_rope(k.reshape(bsz, seq, N_KV_HEADS, HEAD_DIM), cos, sin)
    v = v.reshape(bsz, seq, N_KV_HEADS, HEAD_DIM)
    qi = apply_rope(qi.reshape(bsz, seq, IDX_HEADS, IDX_DIM), cos, sin)
    ki = apply_rope(ki[:, :, None, :], cos, sin)[:, :, 0, :]
    wi = wi * (IDX_HEADS ** -0.5 * IDX_DIM ** -0.5)

    k_sel = min(TOPK_MAX, seq // 4)
    n_blk = seq // Q_BLOCK
    to_blocks = lambda a: jnp.swapaxes(a.reshape((bsz, n_blk, Q_BLOCK) + a.shape[2:]), 0, 1)
    q_b, qi_b, wi_b = to_blocks(q), to_blocks(qi), to_blocks(wi)
    starts = jnp.arange(n_blk, dtype=jnp.int32) * Q_BLOCK
    key_pos = jnp.arange(seq, dtype=jnp.int32)
    b_idx = jnp.arange(bsz)[:, None, None]
    scale = HEAD_DIM ** -0.5

    def block(args):
        q_blk, qi_blk, wi_blk, t0 = args
        t = t0 + jnp.arange(Q_BLOCK, dtype=jnp.int32)
        rel = jax.nn.relu(jnp.einsum('bthd,bsd->bths', qi_blk, ki).astype(jnp.float32))
        score = jnp.einsum('bths,bth->bts', rel, wi_blk.astype(jnp.float32))
        causal = key_pos[None, :] <= t[:, None]
        score = jnp.where(causal[None], score, -jnp.inf)
        _, idx = lax.top_k(score, k_sel)
        kg = k[b_idx, idx]
        vg = v[b_idx, idx]
        qg = q_blk.reshape(bsz, Q_BLOCK, N_KV_HEADS, KV_GROUP, HEAD_DIM)
        att = jnp.einsum('btngd,btknd->btngk', qg, kg).astype(jnp.float32) * scale
        valid = idx <= t[None, :, None]
        att = jnp.where(valid[:, :, None, None, :], att, -jnp.inf)
        p = jax.nn.softmax(att, axis=-1).astype(dt_)
        o = jnp.einsum('btngk,btknd->btngd', p, vg)
        return o.reshape(bsz, Q_BLOCK, N_HEADS * HEAD_DIM)

    out = lax.map(block, (q_b, qi_b, wi_b, starts))
    out = jnp.swapaxes(out, 0, 1).reshape(bsz, seq, N_HEADS * HEAD_DIM)
    return out @ w_out

def sq_relu_mlp(h, w1, w2):
    a = jax.nn.relu(h @ w1)
    return (a * a) @ w2

def first_inputs(seed: int = 0) -> dict:
    key = jax.random.key(seed)
    ks = jax.random.split(key, 20)
    nA, nB = N_SSM_LAYERS, N_ATT_LAYERS
    G, P, C, E = SSM_GROUPS, SSM_STATE, SSM_CH, SSM_WIDTH
    nrm = lambda k, shape, fan: jax.random.normal(k, shape, jnp.float32) * (fan ** -0.5)
    x = jax.random.normal(ks[0], (BATCH, SEQ, D_MODEL), jnp.float32)
    norm_g = 1.0 + 0.01 * jax.random.normal(ks[1], (DEPTH, 4, D_MODEL), jnp.float32)
    mlp_w1 = nrm(ks[2], (DEPTH, D_MODEL, D_FF), D_MODEL)
    mlp_w2 = nrm(ks[3], (DEPTH, D_FF, D_MODEL), D_FF)
    ssm_w_in = nrm(ks[4], (nA, D_MODEL, E), D_MODEL)
    n_idx = jnp.arange(P, dtype=jnp.float32)
    ssm_lam_re = -0.5 + 0.01 * jax.random.normal(ks[5], (nA, G, P), jnp.float32)
    ssm_lam_im = math.pi * n_idx[None, None, :] + 0.01 * jax.random.normal(ks[6], (nA, G, P), jnp.float32)
    ssm_log_dt = jax.random.uniform(ks[7], (nA, G), jnp.float32, math.log(DT_MIN), math.log(DT_MAX))
    ssm_b_re = nrm(ks[8], (nA, G, P, C), 2 * C)
    ssm_b_im = nrm(ks[9], (nA, G, P, C), 2 * C)
    ssm_c_re = nrm(ks[10], (nA, G, C, P), 2 * P)
    ssm_c_im = nrm(ks[11], (nA, G, C, P), 2 * P)
    ssm_d = jax.random.normal(ks[12], (nA, G, C), jnp.float32)
    ssm_w_glu = nrm(ks[13], (nA, E, E), E)
    ssm_w_out = nrm(ks[14], (nA, E, D_MODEL), E)
    att_w_in = nrm(ks[15], (nB, D_MODEL, ATT_IN_COLS), D_MODEL)
    att_w_out = nrm(ks[16], (nB, N_HEADS * HEAD_DIM, D_MODEL), N_HEADS * HEAD_DIM)
    return {"x": x, "norm_g": norm_g, "mlp_w1": mlp_w1, "mlp_w2": mlp_w2,
            "ssm_w_in": ssm_w_in, "ssm_lam_re": ssm_lam_re, "ssm_lam_im": ssm_lam_im,
            "ssm_log_dt": ssm_log_dt, "ssm_b_re": ssm_b_re, "ssm_b_im": ssm_b_im,
            "ssm_c_re": ssm_c_re, "ssm_c_im": ssm_c_im, "ssm_d": ssm_d,
            "ssm_w_glu": ssm_w_glu, "ssm_w_out": ssm_w_out,
            "att_w_in": att_w_in, "att_w_out": att_w_out}

def first_block(x, norm_g, mlp_w1, mlp_w2, ssm_w_in, ssm_lam_re, ssm_lam_im, ssm_log_dt,
              ssm_b_re, ssm_b_im, ssm_c_re, ssm_c_im, ssm_d, ssm_w_glu, ssm_w_out,
              att_w_in, att_w_out):
    h = x
    for i in range(DEPTH):
        j = i // N_MIXERS
        pre = rms_norm(h, norm_g[i, 0])
        if i % N_MIXERS == 0:
            mix = s5_mixer(pre, ssm_w_in[j], ssm_lam_re[j], ssm_lam_im[j], ssm_log_dt[j],
                           ssm_b_re[j], ssm_b_im[j], ssm_c_re[j], ssm_c_im[j], ssm_d[j],
                           ssm_w_glu[j], ssm_w_out[j])
        else:
            mix = dsa_mixer(pre, att_w_in[j], att_w_out[j])
        h = h + rms_norm(mix, norm_g[i, 1])
        ff = sq_relu_mlp(rms_norm(h, norm_g[i, 2]), mlp_w1[i], mlp_w2[i])
        h = h + rms_norm(ff, norm_g[i, 3])
    return h


DEPTH_2 = 1

GRID_W = 64
CTX_LEN = 256
A_HEADS = 8
A_KV_HEADS = 2
A_GROUP = A_HEADS // A_KV_HEADS
A_WIDTH = A_HEADS * HEAD_DIM
B_HEADS = 4
B_V_DIM = 2 * HEAD_DIM
B_WIDTH = B_HEADS * B_V_DIM
N_BRANCH = 2
A_Q_COLS = A_HEADS * HEAD_DIM
A_KV_COLS = A_KV_HEADS * HEAD_DIM
B_QK_COLS = B_HEADS * 2 * HEAD_DIM
IN_SPLIT = [A_Q_COLS, A_KV_COLS, A_KV_COLS, B_QK_COLS, B_QK_COLS, B_WIDTH, D_MODEL, D_MODEL]
IN_COLS = sum(IN_SPLIT)
IN_OFFSETS = [int(v) for v in np.cumsum(IN_SPLIT)[:-1]]
AXIS_PAIRS = HEAD_DIM // 4
N_EXPERTS = 32
TOP_K = 4
D_EXPERT = D_MODEL
SWIGLU_LIMIT = 7.0
SWIGLU_ALPHA = 1.702
MOE_BLOCK = 128
N_MOD = 6
EPS = 1e-6
SUBLN_EPS = 1e-5


def _rmsnorm(x, gain, eps=EPS):
    xf = x.astype(jnp.float32)
    y = xf * lax.rsqrt(jnp.mean(xf * xf, axis=-1, keepdims=True) + eps)
    return (y * gain.astype(jnp.float32)).astype(x.dtype)

def _modulate(h, shift, scale):
    return h * (1 + scale) + shift

def _axial_rope(rows):
    row = jnp.repeat(jnp.arange(rows, dtype=jnp.float32), GRID_W)
    col = jnp.tile(jnp.arange(GRID_W, dtype=jnp.float32), rows)
    inv = 1.0 / (ROPE_THETA ** (jnp.arange(AXIS_PAIRS, dtype=jnp.float32) / AXIS_PAIRS))
    ang = jnp.concatenate([row[:, None] * inv, col[:, None] * inv], axis=-1)
    return jnp.cos(ang), jnp.sin(ang)

def _apply_rope(x, cos, sin):
    extra = x.ndim - 3
    cos = cos.reshape(cos.shape[0], *([1] * extra), cos.shape[1])
    sin = sin.reshape(sin.shape[0], *([1] * extra), sin.shape[1])
    xp = x.reshape(*x.shape[:-1], HEAD_DIM // 2, 2)
    x0, x1 = xp[..., 0], xp[..., 1]
    out = jnp.stack([x0 * cos - x1 * sin, x0 * sin + x1 * cos], axis=-1)
    return out.reshape(x.shape).astype(x.dtype)

def _project(h, w_in, q_norm_a, k_norm_a, q_norm_b, k_norm_b):
    b, n, _ = h.shape
    qa, ka, va, qb, kb, vb, ga, gb = jnp.split(h @ w_in, IN_OFFSETS, axis=-1)
    qa = _rmsnorm(qa.reshape(b, n, A_HEADS, HEAD_DIM), q_norm_a)
    ka = _rmsnorm(ka.reshape(b, n, A_KV_HEADS, HEAD_DIM), k_norm_a)
    va = va.reshape(b, n, A_KV_HEADS, HEAD_DIM)
    qb = _rmsnorm(qb.reshape(b, n, B_HEADS, 2, HEAD_DIM), q_norm_b)
    kb = _rmsnorm(kb.reshape(b, n, B_HEADS, 2, HEAD_DIM), k_norm_b)
    vb = vb.reshape(b, n, B_HEADS, B_V_DIM)
    return qa, ka, va, qb, kb, vb, ga, gb

def _gqa_attend(q, k, v):
    b, n = q.shape[:2]
    qg = q.reshape(b, n, A_KV_HEADS, A_GROUP, HEAD_DIM)
    s = jnp.einsum('bqhgd,bkhd->bhgqk', qg, k).astype(jnp.float32) * (HEAD_DIM ** -0.5)
    p = jax.nn.softmax(s, axis=-1).astype(v.dtype)
    o = jnp.einsum('bhgqk,bkhd->bqhgd', p, v)
    return o.reshape(b, n, A_WIDTH)

def _diff_attend(q, k, v, lam):
    s = jnp.einsum('bqhmd,bkhmd->bhmqk', q, k).astype(jnp.float32) * (HEAD_DIM ** -0.5)
    p = jax.nn.softmax(s, axis=-1)
    a = (p[:, :, 0] - lam * p[:, :, 1]).astype(v.dtype)
    return jnp.einsum('bhqk,bkhe->bqhe', a, v)

def _sweep_query_blocks(attend, q, k, v):
    b, s = q.shape[:2]
    nb = s // Q_BLOCK
    qb = jnp.moveaxis(q.reshape(b, nb, Q_BLOCK, *q.shape[2:]), 1, 0)
    o = lax.map(lambda qq: attend(qq, k, v), qb)
    o = jnp.moveaxis(o, 0, 1)
    return o.reshape(b, s, *o.shape[3:])

def _diff_out(o, subln, lam_init):
    o = _rmsnorm(o, subln, SUBLN_EPS) * (1.0 - lam_init)
    return o.reshape(o.shape[0], o.shape[1], B_WIDTH)

def _merge(ya, yb, ga, gb, w_oa, w_ob, w_out):
    merged = jax.nn.sigmoid(ga) * (ya @ w_oa) + jax.nn.sigmoid(gb) * (yb @ w_ob)
    return merged @ w_out

def _moe(h, router_w, router_b, w_gate, b_gate, w_up, b_up, w_down, b_down):
    t = h.shape[0]
    logits = (h @ router_w + router_b).astype(jnp.float32)
    top_logit, top_e = lax.top_k(logits, TOP_K)
    top_w = jax.nn.softmax(top_logit, axis=-1)
    n_assign = t * TOP_K
    flat_e = top_e.reshape(-1)
    order = jnp.argsort(flat_e)
    sorted_e = flat_e[order]
    sorted_tok = order // TOP_K
    sorted_w = top_w.reshape(-1)[order]
    counts = jnp.bincount(flat_e, length=N_EXPERTS)
    padded = (counts + MOE_BLOCK - 1) // MOE_BLOCK * MOE_BLOCK
    pad_end = jnp.cumsum(padded)
    pad_start = pad_end - padded
    start = jnp.cumsum(counts) - counts
    dest = pad_start[sorted_e] + jnp.arange(n_assign) - start[sorted_e]
    n_blocks = -(-n_assign // MOE_BLOCK) + N_EXPERTS
    buf_tok = jnp.zeros((n_blocks * MOE_BLOCK,), jnp.int32).at[dest].set(sorted_tok.astype(jnp.int32))
    block_e = jnp.minimum(jnp.searchsorted(pad_end, jnp.arange(n_blocks) * MOE_BLOCK, side='right'),
                          N_EXPERTS - 1)
    xb = h[buf_tok].reshape(n_blocks, MOE_BLOCK, h.shape[-1])

    def expert_block(args):
        xe, e = args
        gate = jnp.minimum(xe @ w_gate[e] + b_gate[e], SWIGLU_LIMIT)
        up = jnp.clip(xe @ w_up[e] + b_up[e], -SWIGLU_LIMIT, SWIGLU_LIMIT)
        act = (up + 1) * (gate * jax.nn.sigmoid(SWIGLU_ALPHA * gate))
        return act @ w_down[e] + b_down[e]

    yb = lax.map(expert_block, (xb, block_e)).reshape(-1, h.shape[-1])
    y = yb[dest] * sorted_w[:, None].astype(h.dtype)
    return jax.ops.segment_sum(y, sorted_tok, num_segments=t)

def second_inputs(seed: int = 0) -> dict:
    key = jax.random.key(seed)
    ks = jax.random.split(key, 32)
    f32 = jnp.float32
    L = DEPTH_2

    def nrm(k, shape, scale):
        return jax.random.normal(k, shape, f32) * scale

    def gain(k, shape):
        return 1.0 + 0.05 * jax.random.normal(k, shape, f32)

    return {
        "x": nrm(ks[0], (BATCH, SEQ, D_MODEL), 1.0),
        "c": nrm(ks[1], (BATCH, D_MODEL), 1.0),
        "ctx": nrm(ks[2], (BATCH, CTX_LEN, D_MODEL), 1.0),
        "c_ctx": nrm(ks[3], (D_MODEL,), 1.0),
        "w_ada": nrm(ks[4], (L, D_MODEL, N_MOD * D_MODEL), 0.5 * D_MODEL ** -0.5),
        "b_ada": nrm(ks[5], (L, N_MOD * D_MODEL), 0.02),
        "norm_attn": gain(ks[6], (L, D_MODEL)),
        "w_in": nrm(ks[7], (L, D_MODEL, IN_COLS), D_MODEL ** -0.5),
        "q_norm_a": gain(ks[8], (L, HEAD_DIM)),
        "k_norm_a": gain(ks[9], (L, HEAD_DIM)),
        "q_norm_b": gain(ks[10], (L, HEAD_DIM)),
        "k_norm_b": gain(ks[11], (L, HEAD_DIM)),
        "lambda_q1": nrm(ks[12], (L, HEAD_DIM), 0.1),
        "lambda_k1": nrm(ks[13], (L, HEAD_DIM), 0.1),
        "lambda_q2": nrm(ks[14], (L, HEAD_DIM), 0.1),
        "lambda_k2": nrm(ks[15], (L, HEAD_DIM), 0.1),
        "subln_b": gain(ks[16], (L, B_V_DIM)),
        "w_oa": nrm(ks[17], (L, A_WIDTH, D_MODEL), A_WIDTH ** -0.5),
        "w_ob": nrm(ks[18], (L, B_WIDTH, D_MODEL), B_WIDTH ** -0.5),
        "w_out": nrm(ks[19], (L, D_MODEL, D_MODEL), D_MODEL ** -0.5),
        "norm_mlp": gain(ks[20], (L, D_MODEL)),
        "router_w": nrm(ks[21], (L, D_MODEL, N_EXPERTS), D_MODEL ** -0.5),
        "router_b": nrm(ks[22], (L, N_EXPERTS), 0.01),
        "w_gate": nrm(ks[23], (L, N_EXPERTS, D_MODEL, D_EXPERT), D_MODEL ** -0.5),
        "b_gate": nrm(ks[24], (L, N_EXPERTS, D_EXPERT), 0.02),
        "w_up": nrm(ks[25], (L, N_EXPERTS, D_MODEL, D_EXPERT), D_MODEL ** -0.5),
        "b_up": nrm(ks[26], (L, N_EXPERTS, D_EXPERT), 0.02),
        "w_down": nrm(ks[27], (L, N_EXPERTS, D_EXPERT, D_MODEL), D_EXPERT ** -0.5),
        "b_down": nrm(ks[28], (L, N_EXPERTS, D_MODEL), 0.02),
    }

def second_block(x, c, ctx, c_ctx, w_ada, b_ada, norm_attn, w_in, q_norm_a, k_norm_a, q_norm_b,
              k_norm_b, lambda_q1, lambda_k1, lambda_q2, lambda_k2, subln_b, w_oa, w_ob, w_out,
              norm_mlp, router_w, router_b, w_gate, b_gate, w_up, b_up, w_down, b_down):
    b, s, d = x.shape
    rows = s // GRID_W
    cos, sin = _axial_rope(rows)
    cx = ctx
    for l in range(DEPTH_2):
        last = l == DEPTH_2 - 1
        lam_init = 0.8 - 0.6 * math.exp(-0.3 * l)
        lam = (jnp.exp(jnp.sum(lambda_q1[l].astype(jnp.float32) * lambda_k1[l].astype(jnp.float32)))
               - jnp.exp(jnp.sum(lambda_q2[l].astype(jnp.float32) * lambda_k2[l].astype(jnp.float32)))
               + lam_init)
        mod_x = (jax.nn.silu(c) @ w_ada[l] + b_ada[l])[:, None, :]
        mod_c = (jax.nn.silu(c_ctx) @ w_ada[l] + b_ada[l])[None, None, :]
        sh_a, sc_a, g_a, sh_m, sc_m, g_m = jnp.split(mod_x, N_MOD, axis=-1)
        csh_a, csc_a, cg_a, csh_m, csc_m, cg_m = jnp.split(mod_c, N_MOD, axis=-1)
        proj = functools.partial(_project, w_in=w_in[l], q_norm_a=q_norm_a[l], k_norm_a=k_norm_a[l],
                                 q_norm_b=q_norm_b[l], k_norm_b=k_norm_b[l])

        hx = _modulate(_rmsnorm(x, norm_attn[l]), sh_a, sc_a)
        hc = _modulate(_rmsnorm(cx, norm_attn[l]), csh_a, csc_a)
        qa, ka, va, qb, kb, vb, ga, gb = proj(hx)
        cqa, cka, cva, cqb, ckb, cvb, cga, cgb = proj(hc)
        qa, ka = _apply_rope(qa, cos, sin), _apply_rope(ka, cos, sin)
        qb, kb = _apply_rope(qb, cos, sin), _apply_rope(kb, cos, sin)
        ka_all = jnp.concatenate([ka, cka], axis=1)
        va_all = jnp.concatenate([va, cva], axis=1)
        kb_all = jnp.concatenate([kb, ckb], axis=1)
        vb_all = jnp.concatenate([vb, cvb], axis=1)
        ya = _sweep_query_blocks(_gqa_attend, qa, ka_all, va_all)
        yb = _sweep_query_blocks(lambda qq, kk, vv: _diff_attend(qq, kk, vv, lam), qb, kb_all, vb_all)
        yb = _diff_out(yb, subln_b[l], lam_init)
        x = x + g_a * _merge(ya, yb, ga, gb, w_oa[l], w_ob[l], w_out[l])
        if not last:
            cya = _gqa_attend(cqa, cka, cva)
            cyb = _diff_out(_diff_attend(cqb, ckb, cvb, lam), subln_b[l], lam_init)
            cx = cx + cg_a * _merge(cya, cyb, cga, cgb, w_oa[l], w_ob[l], w_out[l])

        moe = functools.partial(_moe, router_w=router_w[l], router_b=router_b[l], w_gate=w_gate[l],
                                b_gate=b_gate[l], w_up=w_up[l], b_up=b_up[l], w_down=w_down[l],
                                b_down=b_down[l])
        hx = _modulate(_rmsnorm(x, norm_mlp[l]), sh_m, sc_m)
        x = x + g_m * moe(hx.reshape(b * s, d)).reshape(b, s, d)
        if not last:
            hc = _modulate(_rmsnorm(cx, norm_mlp[l]), csh_m, csc_m)
            cx = cx + cg_m * moe(hc.reshape(-1, d)).reshape(cx.shape)
    return x


def setup_inputs(seed=0):
    out = dict(first_inputs(seed))
    for name, value in second_inputs(seed + 1).items():
        if name != "x":
            out[name + "_2"] = value
    return out


def reference(
    x, norm_g, mlp_w1, mlp_w2, ssm_w_in, ssm_lam_re, ssm_lam_im, ssm_log_dt, ssm_b_re, ssm_b_im,
    ssm_c_re, ssm_c_im, ssm_d, ssm_w_glu, ssm_w_out, att_w_in, att_w_out, c_2, ctx_2, c_ctx_2,
    w_ada_2, b_ada_2, norm_attn_2, w_in_2, q_norm_a_2, k_norm_a_2, q_norm_b_2, k_norm_b_2,
    lambda_q1_2, lambda_k1_2, lambda_q2_2, lambda_k2_2, subln_b_2, w_oa_2, w_ob_2, w_out_2,
    norm_mlp_2, router_w_2, router_b_2, w_gate_2, b_gate_2, w_up_2, b_up_2, w_down_2, b_down_2,
):
    x = first_block(
        x, norm_g, mlp_w1, mlp_w2, ssm_w_in, ssm_lam_re, ssm_lam_im, ssm_log_dt, ssm_b_re,
        ssm_b_im, ssm_c_re, ssm_c_im, ssm_d, ssm_w_glu, ssm_w_out, att_w_in, att_w_out,
    )
    return second_block(
        x, c_2, ctx_2, c_ctx_2, w_ada_2, b_ada_2, norm_attn_2, w_in_2, q_norm_a_2, k_norm_a_2,
        q_norm_b_2, k_norm_b_2, lambda_q1_2, lambda_k1_2, lambda_q2_2, lambda_k2_2, subln_b_2,
        w_oa_2, w_ob_2, w_out_2, norm_mlp_2, router_w_2, router_b_2, w_gate_2, b_gate_2, w_up_2,
        b_up_2, w_down_2, b_down_2,
    )


_drawn_inputs = setup_inputs


def setup_inputs(seed=0):
    import zlib

    import numpy as np

    out = dict(_drawn_inputs(seed))
    spreads = {}
    factors = {'ssm_lam_re': 8.0,
     'ctx_2': 5.786,
     'b_ada_2': 4.837,
     'norm_attn_2': 8.0,
     'q_norm_a_2': 8.0,
     'k_norm_a_2': 8.0,
     'q_norm_b_2': 8.0,
     'k_norm_b_2': 8.0,
     'lambda_q1_2': 8.0,
     'lambda_k1_2': 8.0,
     'lambda_q2_2': 8.0,
     'lambda_k2_2': 8.0,
     'subln_b_2': 8.0,
     'norm_mlp_2': 4.029,
     'router_b_2': 8.0,
     'b_gate_2': 8.0,
     'b_up_2': 8.0,
     'b_down_2': 46.318}
    for name, (base, spread) in spreads.items():
        noise = np.random.default_rng([zlib.crc32(name.encode()), seed]).standard_normal(out[name].shape)
        drawn = base * np.exp(spread * noise) if base else spread * noise
        out[name] = __import__('jax').numpy.asarray(drawn.astype(out[name].dtype))
    for name, factor in factors.items():
        out[name] = (out[name] * factor).astype(out[name].dtype)
    return out
```

```python
from contextlib import ExitStack

import numpy as np

import concourse.bass as bass
from concourse import mybir

F32 = mybir.dt.float32
F32R = mybir.dt.float32r
I32 = mybir.dt.int32
U32 = mybir.dt.uint32
ALU = mybir.AluOpType
ACT = mybir.ActivationFunctionType
AX = mybir.AxisListType

P = 128
D = 1024
DT = D // P
S = 512
ST = S // P
CTX = 256
CT = CTX // P
NB = 512
NSLOT = 3
CHUNK = 8 * NB
PIECE = CHUNK // 2

DFF = 4096
SSM_W = 512
WT = SSM_W // P
NJ = 16
HD = 64
NH = 16
NKV = 4
IH = 8
TOPK = 128
EPS = 1e-6

AH = 8
BH = 4
KEYS = S + CTX
KT2 = KEYS // P
SUBLN_EPS = 1e-5
LAM_INIT = 0.8 - 0.6
NE = 32
NK = 4
CAP = 128
NBLK = 48
N_MOD = 6
LIMIT = 7.0
ALPHA = 1.702

TWO_PI_HI, TWO_PI_MID = 6.28125, 0.0019350051879882812
TWO_PI_LO = float(2 * np.pi - 6.28125 - 0.0019350051879882812)
ROUND = 1.5 * 2.0 ** 23
PI_F = 3.1415925

COLS = {}
_n = 0
for _name, _width in (("gains", 8 * DT), ("ssm_d", WT), ("lam_re", NJ), ("lam_im", NJ), ("log_dt", NJ),
                      ("cond", 2 * DT), ("b_ada", N_MOD * DT), ("norm_attn", DT), ("norm_mlp", DT),
                      ("subln", 1), ("lambdas", 4)):
    COLS[_name] = (_n, _width)
    _n += _width
NCOLS = _n

CONST = {}
_n = 0
for _name, _width in (("ident", P), ("ones", P), ("before", P), ("rope1", 2 * ST * (HD // 2)),
                      ("rope2", 2 * ST * (HD // 2)), ("iota_e", NE), ("assign", ST * NK)):
    CONST[_name] = (_n, _width)
    _n += _width
NCONST = _n

DENSE = (("ssm_in", 1, CHUNK), ("ada", 12, CHUNK), ("ssm_glu", 1, WT * NB), ("ssm_out", 1, CHUNK),
         ("w1_0", 8, CHUNK), ("w2_0", 8, CHUNK),
         ("att_in", 4, CHUNK), ("att_idx", 1, DT * 72), ("att_out", 2, CHUNK),
         ("w1_1", 8, CHUNK), ("w2_1", 8, CHUNK),
         ("qa", 1, CHUNK), ("kva", 1, DT * 256), ("qb", 1, CHUNK), ("kb", 1, CHUNK), ("vb", 1, CHUNK),
         ("ga", 1, CHUNK), ("w_oa", 1, WT * NB), ("gb", 1, CHUNK), ("w_ob", 1, WT * NB),
         ("ga1", 1, CHUNK), ("w_oa1", 1, WT * NB), ("gb1", 1, CHUNK), ("w_ob1", 1, WT * NB),
         ("w_out", 2, CHUNK))
FIRST = {}
_n = 0
DENSE_USED = []
for _name, _many, _used in DENSE:
    FIRST[_name] = _n
    DENSE_USED += [_used] * _many
    _n += _many
NDENSE = _n


class Count:

    def __init__(self, sem):
        self.sem, self.n = sem, 0

    def by(self, instruction):
        instruction.then_inc(self.sem, 1)
        self.n += 1
        return self.n

    def then_wait(self, engine, instruction):
        engine.wait_ge(self.sem, self.by(instruction))


def stage(f):
    def run(k, *args):
        lasting, k.stage_sems = k.stage_sems, []
        result = f(k, *args)
        numbers = sorted(s.num for s in k.stage_sems)
        while numbers:
            run_of = 1
            while run_of < len(numbers) and numbers[run_of] == numbers[0] + run_of:
                run_of += 1
            k.nc.gpsimd.sem_clear(range(numbers[0], numbers[0] + run_of))
            numbers = numbers[run_of:]
        for s in k.cleared_sems:
            k.nc.release_semaphore(s)
        k.cleared_sems, k.stage_sems = k.stage_sems, lasting
        return result
    return run


class Kernel:

    def __init__(self, nc, ctx, io):
        self.nc, self.ctx, self.io = nc, ctx, io
        self.cleared_sems = []
        self.stage_sems = []

        def sb(name, width):
            return ctx.enter_context(nc.sbuf_tensor(name, [P, width], F32))

        def sb_both(name, width, parts=1):
            at = (nc.sbuf_base + 31) // 32 * 32
            plain = sb(name, width)
            assert nc.sbuf_base == at + 4 * width
            size = width // parts
            return plain, [nc.alloc_sbuf_tensor_at(f"{name}_rounded_{n}", [P, size], F32R, offset=at + 4 * size * n)
                           for n in range(parts)]

        self.resid = sb("resid", ST * D)[:, :].rearrange("p (t d) -> p t d", t=ST)
        operand, (self.operand_r,) = sb_both("operand", DT * KEYS + 2 * D)
        self.turned = operand[:, 0:DT * KEYS].rearrange("p (k s) -> p k s", k=DT)
        self.gate_rows = operand[:, DT * KEYS:]
        self.x_high, self.x_low = (self.operand_r[:, n * DT * S:(n + 1) * DT * S].rearrange("p (k s) -> p k s", k=DT) for n in range(2))
        self.left = self.operand_r[:, 0:4 * D].rearrange("p (b h k s) -> p b h k s", b=2, h=2, k=2)
        self.arena, self.arena_r = sb_both("arena", 9 * CHUNK, 9)
        self.ring = self.arena[:, 0:NSLOT * CHUNK].rearrange("p (n c) -> p n c", n=NSLOT)
        self.work = self.arena[:, (NSLOT + 1) * CHUNK:9 * CHUNK]
        self.small, (self.small_r,) = sb_both("small", 2304)
        self.cols = sb("cols", NCOLS)
        self.const = sb("const", NCONST)
        self.stat = sb("stat", 64)
        self.mod = sb("mod", 2 * N_MOD * DT)
        self.affine = sb("affine", 6 * DT)
        self.u = self.work[:, 16384:18432].rearrange("p (n s) -> p n s", n=WT)
        self.bt_mat = self.work[:, 18432:19456]
        self.c_mat = self.work[:, 19456:20480]
        self.turned_flat = self.turned.rearrange("p k s -> p (k s)")
        self.ssm_cols = sb("ssm_cols", 4 * NJ)
        self.decay, self.cos1, self.sin1, self.silu_c = (self.ssm_cols[:, NJ * i:NJ * (i + 1)] for i in range(4))
        self.head_gains = self.small[:, 2048:2304]
        self.neg_lam = self.stat[:, 63:64]
        self.psum = ctx.enter_context(nc.psum_tensor("banks", [P, 8, NB], F32))
        self.loaded = [self.sem(f"weights_in_slot{i}") for i in range(NSLOT)]

    def sem(self, name):
        self.stage_sems.append(self.nc.alloc_semaphore(name=name))
        return self.stage_sems[-1]

    def col(self, name, i=0, n=None):
        at, width = COLS[name]
        return self.cols[:, at + i:at + (i + n if n else width)]

    def cst(self, name):
        at, width = CONST[name]
        return self.const[:, at:at + width]

    def load_chunk(self, sp, n):
        if n < NDENSE:
            sp.dma_start(self.ring[:, n % NSLOT, 0:DENSE_USED[n]],
                         self.io["dense"][n, :, 0:DENSE_USED[n]]).then_inc(self.loaded[n % NSLOT], 16)

    def replace_chunks(self, sp, first, many, product, step):
        for c in range(many):
            sp.wait_ge(product, step * (c + 1))
            self.load_chunk(sp, first + c + NSLOT)

    def chunk(self, pe, n, width):
        pe.wait_ge(self.loaded[n % NSLOT], 16 * (n // NSLOT + 1))
        return self.ring[:, n % NSLOT, 0:DENSE_USED[n]].rearrange("p (k n) -> p k n", n=width)

    def piece(self, n, m):
        at = slice((m % 2) * PIECE, (m % 2 + 1) * PIECE)
        slot = (n + m // 2) % NSLOT
        return self.ring[:, slot, at], self.arena_r[slot][:, at], self.arena_r[NSLOT][:, at]

    def split_high(self, act, n, m, used, done):
        chunk = n + m // 2
        act.wait_ge(self.loaded[chunk % NSLOT], 16 * (chunk // NSLOT + 1))
        if m >= 2:
            act.wait_ge(used, m - 1)
        raw, low, high = self.piece(n, m)
        self.nc.scalar.activation(high, raw, ACT.Copy).then_inc(done, 1)

    def split_low(self, n, m, done):
        raw, low, high = self.piece(n, m)
        self.nc.vector.tensor_tensor(low, raw, high.bitcast(F32), ALU.subtract).then_inc(done, 1)

    def parts(self, n, m, tiles):
        raw, low, high = self.piece(n, m)
        return [x.rearrange("p (k n) -> p k n", k=tiles) for x in (high, low)]


def exact_product(nc, out, left, right, start, stop):
    nc.tensor.matmul(out, left[0], right[0], start=start, stop=False)
    nc.tensor.matmul(out, left[0], right[1], start=False, stop=False)
    return nc.tensor.matmul(out, left[1], right[0], start=False, stop=stop)


@stage
def load_inputs(k):
    nc, small_in = k.nc, k.sem("small_inputs_in")
    with nc.Block() as block:
        @block.sync
        def _(sp):
            sp.dma_start(k.resid, k.io["x"].rearrange("(t p) d -> p t d", p=P)).then_inc(small_in, 16)
            for n in range(NSLOT):
                k.load_chunk(sp, n)

        @block.scalar
        def _(act):
            act.dma_start(k.const[:, :], k.io["consts"]).then_inc(small_in, 16)
            act.dma_start(k.cols[:, :], k.io["cols"]).then_inc(small_in, 16)
            act.wait_ge(small_in, 48)


@stage
def norm_turned(k, tag, src, tiles, at, scale, shift=None, split=False):
    nc = k.nc
    rows = k.work[:, 16384:16384 + ST * D].rearrange("p (t d) -> p t d", t=ST)
    ssq, mean, root, rstd = (k.stat[:, 4 * i:4 * i + tiles] for i in range(4))
    squares, mean_ready, root_ready = k.sem(f"{tag}_squares"), k.sem(f"{tag}_mean"), k.sem(f"{tag}_root")
    rows_ready, transposed = k.sem(f"{tag}_rows"), k.sem(f"{tag}_transposed")
    placed_dve, placed_act, chain = k.sem(f"{tag}_placed_dve"), k.sem(f"{tag}_placed_act"), k.sem(f"{tag}_chain")
    n = tiles * P

    with nc.Block() as block:
        @block.scalar
        def _(act):
            for t in range(tiles):
                nc.scalar.activation(rows[:, t, :], src[:, t, :], ACT.Square, accum_out=ssq[:, t:t + 1]).then_inc(squares, 1)
            act.wait_ge(mean_ready, 1)
            nc.scalar.activation(root, mean, ACT.Sqrt).then_inc(root_ready, 1)
            for d in range(DT if split else 0):
                act.wait_ge(transposed, d + 1)
                nc.scalar.activation(k.x_high[:, d, :], k.psum[:, d, :], ACT.Identity,
                                     scale=scale[:, d:d + 1]).then_inc(placed_act, 1)
            for d in range(1, 1 if split else DT, 2):
                act.wait_ge(transposed, d + 1)
                nc.scalar.activation(k.turned[:, d, at:at + n], k.psum[:, d, 0:n], ACT.Identity,
                                     scale=scale[:, d:d + 1],
                                     bias=shift[:, d:d + 1] if shift is not None else 0.0).then_inc(placed_act, 1)

        @block.vector
        def _(dve):
            own = Count(chain)
            dve.wait_ge(squares, tiles)
            nc.vector.tensor_scalar(mean, ssq, 1.0 / D, EPS, ALU.mult, ALU.add).then_inc(mean_ready, 1)
            dve.wait_ge(root_ready, 1)
            own.then_wait(dve, nc.vector.reciprocal(rstd, root))
            for t in range(tiles):
                nc.vector.tensor_scalar(rows[:, t, :], src[:, t, :], rstd[:, t:t + 1], None,
                                        ALU.mult).then_inc(rows_ready, 1)
            for d in range(DT if split else 0):
                dve.wait_ge(placed_act, d + 1)
                nc.vector.scalar_tensor_tensor(out=k.x_low[:, d, :], in0=k.psum[:, d, :], scalar=scale[:, d:d + 1],
                                               in1=k.x_high[:, d, :].bitcast(F32), op0=ALU.mult, op1=ALU.subtract)
            for d in range(0, 0 if split else DT, 2):
                dve.wait_ge(transposed, d + 1)
                if shift is None:
                    i = nc.vector.tensor_scalar(k.turned[:, d, at:at + n], k.psum[:, d, 0:n],
                                                scale[:, d:d + 1], None, ALU.mult)
                else:
                    i = nc.vector.tensor_scalar(k.turned[:, d, at:at + n], k.psum[:, d, 0:n],
                                                scale[:, d:d + 1], shift[:, d:d + 1], ALU.mult, ALU.add)
                i.then_inc(placed_dve, 1)

        @block.tensor
        def _(pe):
            for d in range(DT):
                for t in range(tiles):
                    if d == 0:
                        pe.wait_ge(rows_ready, t + 1)
                    i = nc.tensor.transpose(k.psum[:, d, t * P:(t + 1) * P], rows[:, t, d * P:(d + 1) * P],
                                            k.cst("ident"))
                i.then_inc(transposed, 1)


@stage
def project_residual(k, tag, chunk0, chunks, lhs, row, normed):
    nc = k.nc
    row_tile = k.small[:, 0:D] if normed else row
    scaled_rows = k.work[:, 16384:16384 + 2 * D].rearrange("p (b d) -> p b d", b=2)
    junk = k.small[:, D:2 * D]
    ssq, mean, root, rstd = (k.stat[:, 4 * i:4 * i + 4] for i in range(4))
    names = ("row_in", "high", "low", "used", "product", "squares", "mean", "root", "rstd", "scaled", "added")
    row_in, high, low, used, product, squares, mean_ready, root_ready, rstd_ready, scaled, added = (k.sem(f"{tag}_{n}") for n in names)
    pieces = 2 * chunks
    banks = lambda t: k.psum[:, 2 * t:2 * t + 2, :].rearrange("p b s -> p (b s)")

    with nc.Block() as block:
        @block.sync
        def _(sp):
            if normed:
                sp.dma_start(row_tile, row.partition_broadcast(P)).then_inc(row_in, 16)
            for c in range(chunks):
                sp.wait_ge(used, 2 * (c + 1))
                k.load_chunk(sp, chunk0 + c + NSLOT)

        @block.tensor
        def _(pe):
            for m in range(pieces):
                w = k.parts(chunk0, m, 2)
                pe.wait_ge(low, 3 * (m + 1))
                for t in range(ST):
                    for j in range(2):
                        left = [k.left[:, m % 2, h, j, t * P:(t + 1) * P] for h in range(2)]
                        for c in range(2):
                            i = exact_product(nc, k.psum[:, 2 * t + c, :], left, [x[:, j, c * NB:(c + 1) * NB] for x in w],
                                              start=(m == 0 and j == 0), stop=(m == pieces - 1 and j == 1))
                    if m == pieces - 1:
                        i.then_inc(product, 1)
                if m < pieces - 1:
                    i.then_inc(used, 1)
                else:
                    pe.wait_ge(product, ST)
                    pe.sem_inc(used, 1)

        @block.scalar
        def _(act):
            for m in range(pieces):
                k.split_high(act, chunk0, m, used, high)
                for j in range(2):
                    nc.scalar.activation(k.left[:, m % 2, 0, j, :], lhs(2 * m + j), ACT.Copy).then_inc(high, 1)
            if normed:
                for t in range(ST):
                    act.wait_ge(product, t + 1)
                    if t:
                        act.wait_ge(squares, t)
                    nc.scalar.activation(junk, banks(t), ACT.Square, accum_out=ssq[:, t:t + 1]).then_inc(squares, 1)
                    act.wait_ge(mean_ready, t + 1)
                    nc.scalar.activation(root[:, t:t + 1], mean[:, t:t + 1], ACT.Sqrt).then_inc(root_ready, 1)

        @block.vector
        def _(dve):
            V = nc.vector
            for m in range(pieces):
                dve.wait_ge(high, 3 * m + 1)
                k.split_low(chunk0, m, low)
                for j in range(2):
                    dve.wait_ge(high, 3 * m + j + 2)
                    V.tensor_tensor(k.left[:, m % 2, 1, j, :], lhs(2 * m + j), k.left[:, m % 2, 0, j, :].bitcast(F32),
                                    ALU.subtract).then_inc(low, 1)
            if normed:
                dve.wait_ge(row_in, 16)
            for t in range(ST):
                one = lambda x: x[:, t:t + 1]
                if normed:
                    dve.wait_ge(squares, t + 1)
                    V.tensor_scalar(one(mean), one(ssq), 1.0 / D, EPS, ALU.mult, ALU.add).then_inc(mean_ready, 1)
                else:
                    dve.wait_ge(product, t + 1)
                if t >= 2:
                    dve.wait_ge(added, t - 1)
                V.tensor_tensor(scaled_rows[:, t % 2], banks(t), row_tile, ALU.mult).then_inc(scaled, 1)
                if normed:
                    dve.wait_ge(root_ready, t + 1)
                    V.reciprocal(one(rstd), one(root)).then_inc(rstd_ready, 1)
                    dve.wait_ge(rstd_ready, t + 1)
                dve.wait_ge(scaled, t + 1)
                if normed:
                    i = V.scalar_tensor_tensor(out=k.resid[:, t, :], in0=scaled_rows[:, t % 2], scalar=one(rstd),
                                               in1=k.resid[:, t, :], op0=ALU.mult, op1=ALU.add)
                else:
                    i = V.tensor_tensor(k.resid[:, t, :], scaled_rows[:, t % 2], k.resid[:, t, :], ALU.add)
                i.then_inc(added, 1)


@stage
def mlp_hidden(k, tag, chunk0):
    nc = k.nc
    hidden = k.work[:, 0:32 * NB].rearrange("p (f s) -> p f s", f=32)
    relu = k.small[:, 0:2 * NB].rearrange("p (b s) -> p b s", b=2)
    names = ("high", "low", "used", "product", "clipped", "squared")
    high, low, used, product, clipped, squared = (k.sem(f"{tag}_{n}") for n in names)
    PIECES_W1 = 16

    with nc.Block() as block:
        @block.sync
        def _(sp):
            for c in range(8):
                sp.wait_ge(product, 4 * (c + 1))
                k.load_chunk(sp, chunk0 + c + NSLOT)

        @block.tensor
        def _(pe):
            for m in range(PIECES_W1):
                c = m // 2
                w = k.parts(chunk0, m, 4)
                pe.wait_ge(low, m + 1)
                for f in range(4):
                    n = 4 * c + f
                    if m % 2 == 0 and n >= 8:
                        pe.wait_ge(clipped, n - 7)
                    for j in range(4):
                        d = 4 * (m % 2) + j
                        i = exact_product(nc, k.psum[:, n % 8, :], [x[:, j, f * P:(f + 1) * P] for x in w],
                                          (k.x_high[:, d, :], k.x_low[:, d, :]), start=(d == 0), stop=(d == DT - 1))
                    if m % 2:
                        i.then_inc(product, 1)
                if m % 2 == 0:
                    i.then_inc(used, 1)
                else:
                    pe.wait_ge(product, 4 * (c + 1))
                    pe.sem_inc(used, 1)

        @block.scalar
        def _(act):
            k.split_high(act, chunk0, 0, used, high)
            for m in range(PIECES_W1):
                if m + 1 < PIECES_W1:
                    k.split_high(act, chunk0, m + 1, used, high)
                if m % 2:
                    for n in range(2 * m - 2, 2 * m + 2):
                        act.wait_ge(product, n + 1)
                        if n >= 2:
                            act.wait_ge(squared, n - 1)
                        nc.scalar.activation(relu[:, n % 2, :], k.psum[:, n % 8, :], ACT.Relu).then_inc(clipped, 1)

        @block.vector
        def _(dve):
            for m in range(PIECES_W1):
                dve.wait_ge(high, m + 1)
                k.split_low(chunk0, m, low)

        @block.gpsimd
        def _(pool):
            for n in range(32):
                pool.wait_ge(clipped, n + 1)
                nc.gpsimd.tensor_tensor(hidden[:, n, :], relu[:, n % 2, :], relu[:, n % 2, :],
                                        ALU.mult).then_inc(squared, 1)
    return lambda ki: hidden[:, ki, :]


@stage
def ssm_parameters(k):
    nc = k.nc
    names = ("dt", "lr_dt", "angle", "turns", "whole", "rest", "sin_in", "cos_in", "re", "im", "re1", "a", "b", "den",
             "inv_den", "fr", "fi", "c")
    v = {n: k.work[:, NJ * i:NJ * (i + 1)] for i, n in enumerate(names)}
    raw = k.work[:, 1024:3072].rearrange("p (b j c) -> p b j c", b=4, j=NJ)
    prod = k.work[:, 3072:5120].rearrange("p (b j c) -> p b j c", b=4, j=NJ)
    bbar = k.work[:, 5120:6144].rearrange("p (b j c) -> p b j c", b=2, j=NJ)
    lr, li = k.col("lam_re"), k.col("lam_im")
    mag, cos, sin = k.decay, k.cos1, k.sin1
    raw_in, act_done, dve_done = k.sem("ssm_raw_in"), k.sem("ssm_par_act"), k.sem("ssm_par_dve")
    bbar_ready, bt_turned, silu_half = k.sem("ssm_bbar"), k.sem("ssm_bt_turned"), k.sem("silu_half")

    with nc.Block() as block:
        @block.sync
        def _(sp):
            sp.dma_start(raw, k.io["ssm_bc"].rearrange("p (b j c) -> p b j c", b=4, j=NJ)).then_inc(raw_in, 16)

        @block.scalar
        def _(act):
            nc.scalar.activation(v["dt"], k.col("log_dt"), ACT.Exp).then_inc(act_done, 1)
            act.wait_ge(dve_done, 1)
            nc.scalar.activation(mag, v["lr_dt"], ACT.Exp).then_inc(act_done, 1)
            act.wait_ge(dve_done, 17)
            nc.scalar.activation(sin, v["sin_in"], ACT.Sin).then_inc(act_done, 1)
            nc.scalar.activation(cos, v["cos_in"], ACT.Sin).then_inc(act_done, 1)
            nc.scalar.activation(k.silu_c, k.col("cond"), ACT.Sigmoid).then_inc(silu_half, 1)

        @block.vector
        def _(dve):
            own = Count(dve_done)
            V = nc.vector

            def step(i):
                own.then_wait(dve, i)

            dve.wait_ge(act_done, 1)
            step(V.tensor_tensor(v["lr_dt"], lr, v["dt"], ALU.mult))
            step(V.tensor_tensor(v["angle"], li, v["dt"], ALU.mult))
            for out, quarter in (("sin_in", 0.0), ("cos_in", 0.25)):
                step(V.tensor_scalar(v["turns"], v["angle"], 1.0 / (2 * np.pi), quarter, ALU.mult, ALU.add))
                step(V.tensor_scalar(v["whole"], v["turns"], ROUND, None, ALU.add))
                step(V.tensor_scalar(v["whole"], v["whole"], -ROUND, None, ALU.add))
                step(V.scalar_tensor_tensor(out=v["rest"], in0=v["whole"], scalar=-TWO_PI_HI, in1=v["angle"],
                                            op0=ALU.mult, op1=ALU.add))
                step(V.scalar_tensor_tensor(out=v["rest"], in0=v["whole"], scalar=-TWO_PI_MID, in1=v["rest"],
                                            op0=ALU.mult, op1=ALU.add))
                step(V.scalar_tensor_tensor(out=v[out], in0=v["whole"], scalar=-TWO_PI_LO, in1=v["rest"],
                                            op0=ALU.mult, op1=ALU.add))
                if quarter:
                    step(V.tensor_scalar(v[out], v[out], float(np.pi / 2), None, ALU.add))
                step(V.tensor_scalar(v[out], v[out], PI_F, -PI_F, ALU.min, ALU.max))
            assert own.n == 17
            step(V.tensor_tensor(v["a"], lr, lr, ALU.mult))
            step(V.tensor_tensor(v["b"], li, li, ALU.mult))
            step(V.tensor_tensor(v["den"], v["a"], v["b"], ALU.add))
            step(V.reciprocal(v["inv_den"], v["den"]))
            dve.wait_ge(act_done, 4)
            step(V.tensor_tensor(v["re"], mag, cos, ALU.mult))
            step(V.tensor_tensor(v["im"], mag, sin, ALU.mult))
            step(V.tensor_scalar(v["re1"], v["re"], -1.0, None, ALU.add))
            for out, x, y, op in (("fr", "re1", "im", ALU.add), ("fi", "im", "re1", ALU.subtract)):
                step(V.tensor_tensor(v["a"], v[x], lr, ALU.mult))
                step(V.tensor_tensor(v["b"], v[y], li, ALU.mult))
                step(V.tensor_tensor(v["c"], v["a"], v["b"], op))
                step(V.tensor_tensor(v[out], v["c"], v["inv_den"], ALU.mult))
            dve.wait_ge(raw_in, 16)
            fr = v["fr"].unsqueeze(2).broadcast_to([P, NJ, 32])
            fi = v["fi"].unsqueeze(2).broadcast_to([P, NJ, 32])
            V.tensor_tensor(prod[:, 0], raw[:, 0], fr, ALU.mult)
            V.tensor_tensor(prod[:, 1], raw[:, 1], fi, ALU.mult)
            V.tensor_tensor(prod[:, 2], raw[:, 1], fr, ALU.mult)
            step(V.tensor_tensor(prod[:, 3], raw[:, 0], fi, ALU.mult))
            V.tensor_tensor(bbar[:, 0], prod[:, 0], prod[:, 1], ALU.subtract).then_inc(bbar_ready, 1)
            V.tensor_tensor(bbar[:, 1], prod[:, 2], prod[:, 3], ALU.add).then_inc(bbar_ready, 1)
            V.tensor_copy(k.c_mat[:, 0:512], raw[:, 2].rearrange("p j c -> p (j c)"))
            V.tensor_scalar(k.c_mat[:, 512:1024], raw[:, 3].rearrange("p j c -> p (j c)"), -1.0, None, ALU.mult)
            dve.wait_ge(silu_half, 1)
            V.tensor_tensor(k.silu_c, k.silu_c, k.col("cond"), ALU.mult)
            for part in range(2):
                dve.wait_ge(bt_turned, part + 1)
                V.tensor_copy(k.bt_mat[:, part * 512:(part + 1) * 512], k.psum[:, part, :])

        @block.tensor
        def _(pe):
            for part in range(2):
                pe.wait_ge(bbar_ready, part + 1)
                flat = bbar[:, part].rearrange("p j c -> p (j c)")
                for i in range(WT):
                    t = nc.tensor.transpose(k.psum[:, part, i * P:(i + 1) * P], flat[:, i * P:(i + 1) * P], k.cst("ident"))
                t.then_inc(bt_turned, 1)


@stage
def ssm_input(k):
    nc = k.nc
    product, copied = k.sem("ssm_u_product"), k.sem("ssm_u_copied")
    with nc.Block() as block:
        @block.sync
        def _(sp):
            k.replace_chunks(sp, 0, 1, product, WT)

        @block.tensor
        def _(pe):
            w = k.chunk(pe, 0, NB)
            for n in range(WT):
                for d in range(DT):
                    i = nc.tensor.matmul(k.psum[:, n, :], w[:, d, n * P:(n + 1) * P], k.turned[:, d, 0:S],
                                         start=(d == 0), stop=(d == DT - 1))
                i.then_inc(product, 1)

        @block.scalar
        def _(act):
            for n in range(WT):
                act.wait_ge(product, n + 1)
                nc.scalar.activation(k.u[:, n, :], k.psum[:, n, :], ACT.Copy).then_inc(copied, 1)


@stage
def ssm_tables(k):
    nc = k.nc
    cos = k.work[:, 0:NJ * S].rearrange("p (j s) -> p j s", j=NJ)
    sin = k.work[:, NJ * S:2 * NJ * S].rearrange("p (j s) -> p j s", j=NJ)
    tmp = k.turned_flat
    step_c = [k.small[:, 32 * i:32 * i + NJ] for i in range(10)]
    step_s = [k.small[:, 32 * i + NJ:32 * i + 32] for i in range(10)]
    sq = [k.small[:, 320 + NJ * i:320 + NJ * (i + 1)] for i in range(3)]
    chain = k.sem("ssm_tables")
    with nc.Block() as block:
        @block.vector
        def _(dve):
            own = Count(chain)
            V = nc.vector
            V.memset(cos[:, :, 0:1], 1.0)
            V.memset(sin[:, :, 0:1], 0.0)
            V.tensor_copy(step_c[0], k.cos1)
            own.then_wait(dve, V.tensor_copy(step_s[0], k.sin1))
            s, level = 1, 0
            while s < S:
                c, d = step_c[level], step_s[level]
                wide = [P, NJ, s]
                cb, db = c.unsqueeze(2).broadcast_to(wide), d.unsqueeze(2).broadcast_to(wide)
                t0 = tmp[:, 0:NJ * s].rearrange("p (j s) -> p j s", j=NJ)
                V.tensor_tensor(cos[:, :, s:2 * s], cos[:, :, 0:s], cb, ALU.mult)
                V.tensor_tensor(sin[:, :, s:2 * s], sin[:, :, 0:s], cb, ALU.mult)
                own.then_wait(dve, V.tensor_tensor(t0, sin[:, :, 0:s], db, ALU.mult))
                own.then_wait(dve, V.tensor_tensor(cos[:, :, s:2 * s], cos[:, :, s:2 * s], t0, ALU.subtract))
                own.then_wait(dve, V.tensor_tensor(t0, cos[:, :, 0:s], db, ALU.mult))
                own.then_wait(dve, V.tensor_tensor(sin[:, :, s:2 * s], sin[:, :, s:2 * s], t0, ALU.add))
                V.tensor_tensor(sq[0], c, c, ALU.mult)
                V.tensor_tensor(sq[1], d, d, ALU.mult)
                own.then_wait(dve, V.tensor_tensor(sq[2], c, d, ALU.mult))
                V.tensor_tensor(step_c[level + 1], sq[0], sq[1], ALU.subtract)
                own.then_wait(dve, V.tensor_scalar(step_s[level + 1], sq[2], 2.0, None, ALU.mult))
                s, level = 2 * s, level + 1


@stage
def ssm_scan(k):
    nc = k.nc
    cos = k.work[:, 0:NJ * S].rearrange("p (j s) -> p j s", j=NJ)
    sin = k.work[:, NJ * S:2 * NJ * S].rearrange("p (j s) -> p j s", j=NJ)
    buf = k.turned_flat.rearrange("p (b s) -> p b s", s=S)
    back = k.small[:, 0:4 * S].rearrange("p (b s) -> p b s", s=S)
    bu, bu_copied = k.sem("ssm_bu"), k.sem("ssm_bu_copied")
    in_dve, in_pool = k.sem("ssm_in_dve"), k.sem("ssm_in_pool")
    zin_re, zin_im, z_done = k.sem("ssm_zin_re"), k.sem("ssm_zin_im"), k.sem("ssm_z_done")
    back_dve, back_pool, y_done = k.sem("ssm_back_dve"), k.sem("ssm_back_pool"), k.sem("ssm_y_done")
    ada_done = k.sem("ada_done")
    ada0 = FIRST["ada"]
    mod_psum = k.psum[:, 2, 0:2 * N_MOD * DT]

    def bufs(j):
        return [buf[:, 6 * (j % 2) + i, :] for i in range(6)]

    with nc.Block() as block:
        @block.sync
        def _(sp):
            k.replace_chunks(sp, ada0, 12, ada_done, 1)

        @block.tensor
        def _(pe):
            for j in range(NJ + 1):
                if j < NJ:
                    i, q = j // 4, 32 * (j % 4)
                    if j >= 1:
                        pe.wait_ge(bu_copied, 2 * j)
                    for part in range(2):
                        m = nc.tensor.matmul(k.psum[:, part, :], k.bt_mat[q:q + 32, part * 512 + i * P:part * 512 + (i + 1) * P],
                                             k.u[q:q + 32, i, :], start=True, stop=True)
                    m.then_inc(bu, 1)
                if j < 12:
                    w = k.chunk(pe, ada0 + j, NB)
                    for n in range(4):
                        col = 2 * (4 * j + n)
                        for d in range(DT):
                            m = nc.tensor.matmul(mod_psum[:, col:col + 2], w[:, d, n * P:(n + 1) * P],
                                                 k.silu_c[:, 2 * d:2 * d + 2], start=(d == 0), stop=(d == DT - 1))
                    m.then_inc(ada_done, 1)
                if j >= 1:
                    jj = j - 1
                    i, q = jj // 4, 32 * (jj % 4)
                    pe.wait_ge(back_dve, jj + 1)
                    pe.wait_ge(back_pool, jj + 1)
                    for n, part in enumerate((0, 0, 1, 1)):
                        m = nc.tensor.matmul(k.psum[q:q + 32, 4 + i, :], k.c_mat[:, part * 512 + 32 * jj:part * 512 + 32 * jj + 32],
                                             back[:, n, :], start=(n == 0), stop=(n == 3), tile_position=(0, q))
                    m.then_inc(y_done, 1)

        @block.scalar
        def _(act):
            for j in range(NJ):
                b = bufs(j)
                act.wait_ge(bu, j + 1)
                if j >= 2:
                    act.wait_ge(zin_im, j - 1)
                    act.wait_ge(zin_re, j - 1)
                nc.scalar.activation(b[0], k.psum[:, 0, :], ACT.Copy).then_inc(bu_copied, 1)
                nc.scalar.activation(b[1], k.psum[:, 1, :], ACT.Copy).then_inc(bu_copied, 1)

        @block.gpsimd
        def _(pool):
            for j in range(NJ):
                b = bufs(j)
                pool.wait_ge(bu_copied, 2 * j + 2)
                if j >= 2:
                    pool.wait_ge(back_dve, j - 1)
                    pool.wait_ge(back_pool, j - 1)
                nc.gpsimd.tensor_tensor(b[4], cos[:, j, :], b[1], ALU.mult).then_inc(in_pool, 1)
                nc.gpsimd.tensor_tensor(b[5], sin[:, j, :], b[0], ALU.mult).then_inc(in_pool, 1)
                pool.wait_ge(in_pool, 2 * j + 2)
                nc.gpsimd.tensor_tensor(b[4], b[4], b[5], ALU.subtract).then_inc(zin_im, 1)
                pool.wait_ge(z_done, 2 * j + 2)
                if j >= 1:
                    pool.wait_ge(y_done, j)
                nc.gpsimd.tensor_tensor(back[:, 3, :], cos[:, j, :], b[5], ALU.mult).then_inc(back_pool, 1)

        @block.vector
        def _(dve):
            V = nc.vector
            for j in range(NJ):
                b = bufs(j)
                a = k.decay[:, j:j + 1].broadcast_to([P, S])
                dve.wait_ge(bu_copied, 2 * j + 2)
                if j >= 2:
                    dve.wait_ge(back_dve, j - 1)
                V.tensor_tensor(b[2], cos[:, j, :], b[0], ALU.mult)
                V.tensor_tensor(b[3], sin[:, j, :], b[1], ALU.mult).then_inc(in_dve, 1)
                dve.wait_ge(in_dve, j + 1)
                V.tensor_tensor(b[2], b[2], b[3], ALU.add).then_inc(zin_re, 1)
                dve.wait_ge(zin_re, j + 1)
                V.tensor_tensor_scan(b[3], a, b[2], 0.0, ALU.mult, ALU.add).then_inc(z_done, 1)
                dve.wait_ge(zin_im, j + 1)
                V.tensor_tensor_scan(b[5], a, b[4], 0.0, ALU.mult, ALU.add).then_inc(z_done, 1)
                dve.wait_ge(z_done, 2 * j + 2)
                if j >= 1:
                    dve.wait_ge(y_done, j)
                V.tensor_tensor(back[:, 0, :], cos[:, j, :], b[3], ALU.mult)
                V.tensor_tensor(back[:, 2, :], sin[:, j, :], b[3], ALU.mult)
                V.scalar_tensor_tensor(out=back[:, 1, :], in0=b[5], scalar=-1.0, in1=sin[:, j, :],
                                       op0=ALU.mult, op1=ALU.mult).then_inc(back_dve, 1)
            dve.wait_ge(ada_done, 12)
            nc.vector.tensor_tensor(k.mod[:, :].rearrange("p (c w) -> p c w", w=2),
                                    mod_psum.rearrange("p (c w) -> p c w", w=2),
                                    k.col("b_ada").unsqueeze(2).broadcast_to([P, N_MOD * DT, 2]), ALU.add)


@stage
def ssm_gate(k):
    nc = k.nc
    y, z, gate, gated = (k.work[:, 2048 * i:2048 * (i + 1)].rearrange("p (n s) -> p n s", n=WT) for i in range(4))
    summed, gelu, product, opened = (k.sem(f"ssm_{n}") for n in ("summed", "gelu", "glu_product", "glu_opened"))
    g0 = FIRST["ssm_glu"]
    with nc.Block() as block:
        @block.vector
        def _(dve):
            for n in range(WT):
                nc.vector.scalar_tensor_tensor(out=y[:, n, :], in0=k.u[:, n, :], scalar=k.col("ssm_d", n, 1),
                                               in1=k.psum[:, 4 + n, :], op0=ALU.mult, op1=ALU.add).then_inc(summed, 1)
            for n in range(WT):
                dve.wait_ge(opened, n + 1)
                nc.vector.tensor_tensor(gated[:, n, :], z[:, n, :], gate[:, n, :], ALU.mult)

        @block.scalar
        def _(act):
            for n in range(WT):
                act.wait_ge(summed, n + 1)
                nc.scalar.activation(z[:, n, :], y[:, n, :], ACT.Gelu_apprx_tanh).then_inc(gelu, 1)
            for n in range(WT):
                act.wait_ge(product, n + 1)
                nc.scalar.activation(gate[:, n, :], k.psum[:, n, :], ACT.Sigmoid).then_inc(opened, 1)

        @block.tensor
        def _(pe):
            w = k.chunk(pe, g0, NB)
            pe.wait_ge(gelu, WT)
            for n in range(WT):
                for c in range(WT):
                    i = nc.tensor.matmul(k.psum[:, n, :], w[:, c, n * P:(n + 1) * P], z[:, c, :],
                                         start=(c == 0), stop=(c == WT - 1))
                i.then_inc(product, 1)

        @block.sync
        def _(sp):
            k.replace_chunks(sp, g0, 1, product, WT)
    return lambda ki: gated[:, ki, :]


NEG = -1e30
TAKEN = -3e38
HUGE = 3e38


def attention_layout(k):
    w = k.work
    a = {}
    a["q"] = w[:, 0:4096].rearrange("p (f s) -> p f s", f=8)
    a["k"] = w[:, 4096:6144].rearrange("p (f s) -> p f s", f=NKV)
    a["qi"] = w[:, 6144:8192].rearrange("p (f s) -> p f s", f=4)
    a["ki"] = w[:, 8192:8704].rearrange("p (f s) -> p f s", f=1)
    a["v"] = w[:, 8704:9728].rearrange("p (t c) -> p t c", t=ST)
    a["bias"] = w[:, 9728:11776].rearrange("p (t s) -> p t s", t=ST)
    a["out"] = w[:, 11776:15872].rearrange("p (f s) -> p f s", f=8)
    a["wi"] = w[:, 15872:15904].rearrange("p (t h) -> p t h", t=ST)
    a["staged"] = w[:, 16384:17408].rearrange("p (b c) -> p b c", b=2)
    a["m1"], a["m2"], a["kr"] = w[:, 17408:17920], w[:, 17920:18432], w[:, 18432:18688]
    return a


@stage
def attention_project(k, a):
    nc = k.nc
    first = FIRST["att_in"]
    rope = k.cst("rope1").rearrange("p (f t c) -> p f t c", f=2, t=ST)
    units = [(c, t) for c in range(5) for t in range(ST)]
    tiles = {0: 4, 1: 4, 2: NKV, 3: 4, 4: 1}
    place = {0: ("q", 0), 1: ("q", 4), 2: ("k", 0), 3: ("qi", 0), 4: ("ki", 0)}
    product, staged, turned, placed, chain = (k.sem(f"att_{n}") for n in ("product", "staged", "turned", "placed", "rope"))

    with nc.Block() as block:
        @block.sync
        def _(sp):
            k.replace_chunks(sp, first, 5, product, ST)

        @block.tensor
        def _(pe):
            for n in range(len(units) + 1):
                if n < len(units):
                    c, t = units[n]
                    width = NB if c < 4 else 72
                    w = k.chunk(pe, first + c, width)
                    if n >= 4:
                        pe.wait_ge(staged, n - 3)
                    for d in range(DT):
                        i = nc.tensor.matmul(k.psum[:, n % 4, 0:width], k.turned[:, d, t * P:(t + 1) * P], w[:, d, :],
                                             start=(d == 0), stop=(d == DT - 1))
                    i.then_inc(product, 1)
                if n >= 1:
                    c, t = units[n - 1]
                    pe.wait_ge(staged, n)
                    if n >= 3:
                        pe.wait_ge(placed, n - 2)
                    for f in range(tiles[c]):
                        i = nc.tensor.transpose(k.psum[:, 4 + (n - 1) % 2, f * P:(f + 1) * P],
                                                a["staged"][:, (n - 1) % 2, f * P:(f + 1) * P], k.cst("ident"))
                    i.then_inc(turned, 1)

        @block.scalar
        def _(act):
            for n, (c, t) in enumerate(units):
                name, f0 = place[c]
                act.wait_ge(turned, n + 1)
                m = tiles[c]
                nc.scalar.activation(a[name][:, f0:f0 + m, t * P:(t + 1) * P],
                                     k.psum[:, 4 + n % 2, 0:m * P].rearrange("p (f s) -> p f s", f=m), ACT.Copy,
                                     scale=HD ** -0.5 if name == "q" else 1.0).then_inc(placed, 1)

        @block.vector
        def _(dve):
            own, V = Count(chain), nc.vector

            def rotate(out, x, heads, t):
                half = HD // 2
                xs = x.rearrange("p (h c) -> p h c", c=HD)
                m1 = a["m1"][:, 0:heads * HD].rearrange("p (h c) -> p h c", c=HD)
                m2 = a["m2"][:, 0:heads * HD].rearrange("p (h c) -> p h c", c=HD)
                both = lambda f: rope[:, f, t, :].unsqueeze(1)
                wide = [P, 2 * heads, half]
                V.tensor_tensor(a["m1"][:, 0:heads * HD].rearrange("p (h c) -> p h c", c=half),
                                x.rearrange("p (h c) -> p h c", c=half), both(0).broadcast_to(wide), ALU.mult)
                sin = both(1).broadcast_to([P, heads, half])
                V.tensor_tensor(m2[:, :, 0:half], xs[:, :, half:HD], sin, ALU.mult)
                own.then_wait(dve, V.tensor_tensor(m2[:, :, half:HD], xs[:, :, 0:half], sin, ALU.mult))
                os = out.rearrange("p (h c) -> p h c", c=HD)
                V.tensor_tensor(os[:, :, 0:half], m1[:, :, 0:half], m2[:, :, 0:half], ALU.subtract)
                return V.tensor_tensor(os[:, :, half:HD], m1[:, :, half:HD], m2[:, :, half:HD], ALU.add)

            for n, (c, t) in enumerate(units):
                ps, out = k.psum[:, n % 4, :], a["staged"][:, n % 2, :]
                dve.wait_ge(product, n + 1)
                if n:
                    dve.wait_ge(staged, n)
                if n >= 2:
                    dve.wait_ge(turned, n - 1)
                if c in (0, 1, 3):
                    i = rotate(out, ps, NB // HD, t)
                else:
                    heads = NKV if c == 2 else 1
                    own.then_wait(dve, rotate(a["kr"][:, 0:heads * HD], ps[:, 0:heads * HD], heads, t))
                    if c == 2:
                        V.tensor_copy(a["v"][:, t, :], ps[:, 256:512])
                    else:
                        V.tensor_scalar(a["wi"][:, t, :], ps[:, HD:HD + IH], IH ** -0.5 * HD ** -0.5, None, ALU.mult)
                    i = V.tensor_copy(out[:, 0:heads * 2 * HD].rearrange("p (h b c) -> p h b c", b=2, c=HD),
                                      a["kr"][:, 0:heads * HD].rearrange("p (h c) -> p h c", c=HD).unsqueeze(2)
                                      .broadcast_to([P, heads, 2, HD]))
                i.then_inc(staged, 1)


@stage
def attention_select(k, a):
    nc = k.nc
    units = [(i, h) for i in range(1, ST) for h in range(IH)]
    relu = k.turned_flat[:, 0:2048].rearrange("p (b s) -> p b s", b=4)
    score = k.turned_flat[:, 2048:2048 + 3 * S].rearrange("p (t s) -> p t s", t=3)
    best = k.small[:, 0:24].rearrange("p (t c) -> p t c", t=3)
    product, clipped, summed, causal, chain = (k.sem(f"idx_{n}") for n in ("product", "clipped", "summed", "causal", "chain"))

    with nc.Block() as block:
        @block.tensor
        def _(pe):
            for n, (i, h) in enumerate(units):
                r, keys = HD * (h % 2), (i + 1) * P
                if n >= 4:
                    pe.wait_ge(clipped, n - 3)
                nc.tensor.matmul(k.psum[:, n % 4, 0:keys], a["qi"][r:r + HD, h // 2, i * P:(i + 1) * P],
                                 a["ki"][r:r + HD, 0, 0:keys], start=True, stop=True).then_inc(product, 1)

        @block.scalar
        def _(act):
            for n, (i, h) in enumerate(units):
                act.wait_ge(product, n + 1)
                if n >= 4:
                    act.wait_ge(summed, n - 3)
                nc.scalar.activation(relu[:, n % 4, 0:(i + 1) * P], k.psum[:, n % 4, 0:(i + 1) * P],
                                     ACT.Relu).then_inc(clipped, 1)

        @block.gpsimd
        def _(pool):
            nc.gpsimd.memset(a["bias"][:, 0, 0:P], 0.0).then_inc(causal, 1)
            pool.wait_ge(causal, 1)
            nc.gpsimd.affine_select(out=a["bias"][:, 0, 0:P], in_=a["bias"][:, 0, 0:P], pattern=[[-1, P]],
                                    compare_op=ALU.is_ge, fill=NEG, base=0, channel_multiplier=1).then_inc(causal, 1)
            for i in range(1, ST):
                pool.wait_ge(summed, IH * i)
                own = score[:, i - 1, i * P:(i + 1) * P]
                nc.gpsimd.affine_select(out=own, in_=own, pattern=[[-1, P]], compare_op=ALU.is_ge, fill=NEG,
                                        base=0, channel_multiplier=1).then_inc(causal, 1)

        @block.vector
        def _(dve):
            own, V = Count(chain), nc.vector
            for i in range(1, ST):
                keys = (i + 1) * P
                for h in range(IH):
                    n = (i - 1) * IH + h
                    s = score[:, i - 1, 0:keys]
                    dve.wait_ge(clipped, n + 1)
                    w = a["wi"][:, i, h:h + 1]
                    if h == 0:
                        j = V.tensor_scalar(s, relu[:, n % 4, 0:keys], w, None, ALU.mult)
                    else:
                        dve.wait_ge(summed, n)
                        j = V.scalar_tensor_tensor(out=s, in0=relu[:, n % 4, 0:keys], scalar=w, in1=s,
                                                   op0=ALU.mult, op1=ALU.add)
                    j.then_inc(summed, 1)
            for i in range(1, ST):
                s = score[:, i - 1, 0:(i + 1) * P]
                dve.wait_ge(causal, 2 + i)
                for r in range(TOPK // 8):
                    own.then_wait(dve, V.max(best[:, i - 1, :], s))
                    own.then_wait(dve, V.match_replace(s, best[:, i - 1, :], s, TAKEN))
                V.tensor_scalar(a["bias"][:, i, 0:(i + 1) * P], s, TAKEN, NEG, ALU.not_equal, ALU.mult)


@stage
def attention_heads(k, a):
    nc = k.nc
    units = [(i, h) for i in range(ST) for h in range(NH)]
    N = len(units)
    flat = k.turned_flat
    minus = flat[:, 0:1024].rearrange("p (b s) -> p b s", b=2)
    prob = flat[:, 1024:2560].rearrange("p (b s) -> p b s", b=3)
    prob_t = flat[:, 2560:3584].rearrange("p (b s) -> p b s", b=2)
    top, total, inv = (k.stat[:, 8 * j:8 * j + 8] for j in range(3))
    names = ("score", "masked", "exp", "inverse", "scaled", "turned", "placed", "product", "kept")
    score, masked, exped, inverse, scaled, turned, placed, product, kept = (k.sem(f"heads_{n}") for n in names)

    with nc.Block() as block:
        @block.tensor
        def _(pe):
            for n in range(N + 3):
                if n < N:
                    i, h = units[n]
                    r, keys = HD * (h % 2), (i + 1) * P
                    if n >= 2:
                        pe.wait_ge(masked, n - 1)
                    nc.tensor.matmul(k.psum[:, n % 2, 0:keys], a["q"][r:r + HD, h // 2, i * P:(i + 1) * P],
                                     a["k"][r:r + HD, h // 4, 0:keys], start=True, stop=True).then_inc(score, 1)
                m = n - 2
                if 0 <= m < N:
                    i, h = units[m]
                    pe.wait_ge(scaled, m + 1)
                    if m >= 2:
                        pe.wait_ge(placed, m - 1)
                    for b in range(i + 1):
                        j = nc.tensor.transpose(k.psum[:, 2 + m % 2, b * P:(b + 1) * P],
                                                prob[:, m % 3, b * P:(b + 1) * P], k.cst("ident"))
                    j.then_inc(turned, 1)
                m = n - 3
                if 0 <= m < N:
                    i, h = units[m]
                    r, pair = HD * (h % 2), m // 2
                    pe.wait_ge(placed, m + 1)
                    if h % 2 == 0 and pair >= 2:
                        pe.wait_ge(kept, pair - 1)
                    for b in range(i + 1):
                        j = nc.tensor.matmul(k.psum[r:r + HD, 4 + pair % 2, 0:P],
                                             a["v"][:, b, (h // 4) * HD:(h // 4 + 1) * HD],
                                             prob_t[:, m % 2, b * P:(b + 1) * P], start=(b == 0), stop=(b == i),
                                             tile_position=(0, r))
                    j.then_inc(product, 1)

        @block.vector
        def _(dve):
            V = nc.vector
            for n in range(N + 5):
                if n < N:
                    i, h = units[n]
                    keys = (i + 1) * P
                    dve.wait_ge(score, n + 1)
                    if n >= 2:
                        dve.wait_ge(exped, n - 1)
                    V.tensor_tensor_reduce(minus[:, n % 2, 0:keys], k.psum[:, n % 2, 0:keys], a["bias"][:, i, 0:keys],
                                           -1.0, HUGE, ALU.add, ALU.min, top[:, n % 8:n % 8 + 1]).then_inc(masked, 1)
                if 1 <= n <= N:
                    m = n - 1
                    dve.wait_ge(exped, m + 1)
                    V.reciprocal(inv[:, m % 8:m % 8 + 1], total[:, m % 8:m % 8 + 1]).then_inc(inverse, 1)
                m = n - 4
                if 0 <= m < N and m % 2 == 1:
                    i, h = units[m]
                    dve.wait_ge(product, m + 1)
                    V.tensor_copy(a["out"][:, h // 2, i * P:(i + 1) * P], k.psum[:, 4 + (m // 2) % 2, 0:P]).then_inc(kept, 1)

        @block.scalar
        def _(act):
            for n in range(N + 2):
                if n < N:
                    i, h = units[n]
                    keys = (i + 1) * P
                    act.wait_ge(masked, n + 1)
                    if n >= 3:
                        act.wait_ge(turned, n - 2)
                    nc.scalar.activation(prob[:, n % 3, 0:keys], minus[:, n % 2, 0:keys], ACT.Exp,
                                         bias=top[:, n % 8:n % 8 + 1], scale=-1.0,
                                         accum_out=total[:, n % 8:n % 8 + 1]).then_inc(exped, 1)
                m = n - 2
                if m >= 0:
                    i, h = units[m]
                    keys = (i + 1) * P
                    act.wait_ge(turned, m + 1)
                    if m >= 2:
                        act.wait_ge(product, m - 1)
                    nc.scalar.activation(prob_t[:, m % 2, 0:keys], k.psum[:, 2 + m % 2, 0:keys],
                                         ACT.Copy).then_inc(placed, 1)

        @block.gpsimd
        def _(pool):
            for n, (i, h) in enumerate(units):
                pool.wait_ge(inverse, n + 1)
                p = prob[:, n % 3, 0:(i + 1) * P]
                nc.gpsimd.tensor_scalar(p, p, inv[:, n % 8:n % 8 + 1], 1.0, ALU.mult, ALU.mult).then_inc(scaled, 1)
    return lambda ki: a["out"][:, ki, :]


def blend_layout(k):
    w = k.work
    b = {}

    def take(name, at, tiles, width):
        b[name] = w[:, at:at + tiles * width].rearrange("p (f s) -> p f s", f=tiles)
        return at + tiles * width

    at = take("qa", 0, 4, S)
    at = take("ka", at, 2, KEYS)
    at = take("qb", at, BH, S)
    at = take("kb", at, BH, KEYS)
    at = take("va", at, KT2, P)
    at = take("vb", at, KT2, BH * P)
    at = take("ya", at, 4, S)
    at = take("yb", at, BH, S)
    b["free"] = w[:, at:20480]
    return b


@stage
def modulation(k):
    nc = k.nc
    m = k.mod[:, :].rearrange("p (m d w) -> p m d w", m=N_MOD, w=2)
    scale = k.affine[:, :].rearrange("p (n d) -> p n d", n=6)
    diag = k.work[:, 0:2 * D].rearrange("p (g d) -> p g d", g=2)
    chain, prods, sums, exps, diags, rows = (k.sem(f"mod_{n}") for n in ("chain", "prods", "sums", "exps", "diags", "rows"))
    lam_prod, lam_exp = k.stat[:, 0:2], k.stat[:, 2:4]
    with nc.Block() as block:
        @block.vector
        def _(dve):
            own, V = Count(chain), nc.vector
            lam = k.col("lambdas")
            V.tensor_tensor(lam_prod[:, 0:1], lam[:, 0:1], lam[:, 1:2], ALU.mult)
            V.tensor_tensor(lam_prod[:, 1:2], lam[:, 2:3], lam[:, 3:4], ALU.mult).then_inc(prods, 1)
            for g, mod in enumerate((2, 5)):
                for d in range(DT):
                    V.tensor_scalar(diag[:, g, d * P:(d + 1) * P], k.cst("ident"), m[:, mod, d, 0:1], None,
                                    ALU.mult).then_inc(diags, 1)
            for n, (base, sh, sc, w) in enumerate((("norm_attn", 0, 1, 0), ("norm_attn", 0, 1, 1), ("norm_mlp", 3, 4, 0))):
                V.tensor_copy(scale[:, 2 * n + 1], m[:, sh, :, w])
                own.then_wait(dve, V.tensor_scalar(scale[:, 2 * n], m[:, sc, :, w], 1.0, None, ALU.add))
                own.then_wait(dve, V.tensor_tensor(scale[:, 2 * n], scale[:, 2 * n], k.col(base), ALU.mult))
            dve.wait_ge(exps, 1)
            own.then_wait(dve, V.tensor_tensor(k.neg_lam, lam_exp[:, 1:2], lam_exp[:, 0:1], ALU.subtract))
            V.tensor_scalar(k.neg_lam, k.neg_lam, -LAM_INIT, None, ALU.add)
            for n in range(4):
                dve.wait_ge(rows, n + 1)
                V.tensor_copy(k.gate_rows[:, n * NB:(n + 1) * NB], k.psum[:, n, :])

        @block.tensor
        def _(pe):
            pe.wait_ge(prods, 1)
            nc.tensor.matmul(k.psum[:, 4, 0:2], k.cst("ones"), lam_prod, start=True, stop=True).then_inc(sums, 1)
            for g in range(2):
                for half in range(2):
                    pe.wait_ge(diags, DT * g + 4 * half + 4)
                    nc.tensor.matmul(k.psum[:, 2 * g + half, :], k.cst("ones"), diag[:, g, half * NB:(half + 1) * NB],
                                     start=True, stop=True).then_inc(rows, 1)

        @block.scalar
        def _(act):
            act.wait_ge(sums, 1)
            nc.scalar.activation(lam_exp, k.psum[:, 4, 0:2], ACT.Exp).then_inc(exps, 1)


@stage
def load_context(k):
    nc, ctx_in = k.nc, k.sem("ctx_in")
    ctx = k.work[:, 0:CT * D].rearrange("p (t d) -> p t d", t=CT)
    with nc.Block() as block:
        @block.sync
        def _(sp):
            sp.dma_start(ctx, k.io["ctx"].rearrange("(t p) d -> p t d", p=P)).then_inc(ctx_in, 16)
            sp.dma_start(k.head_gains, k.io["rows"][8, 0:4 * HD].partition_broadcast(P)).then_inc(ctx_in, 16)
            sp.wait_ge(ctx_in, 32)
    return ctx


@stage
def blend_project(k, b):
    nc = k.nc
    first = FIRST["qa"]
    units = ([("qa", t) for t in range(ST)] + [("kva", t) for t in range(ST + CT)] + [("qb", t) for t in range(ST)]
             + [("kb", t) for t in range(ST + CT)] + [("vb", t) for t in range(ST + CT)])
    order = ("qa", "kva", "qb", "kb", "vb")
    width = {"kva": 256}
    gain_of = {"qa": 0, "kva": 1, "qb": 2, "kb": 3}
    rope = k.cst("rope2").rearrange("p (f t c) -> p f t c", f=2, t=ST)
    free = b["free"][:, 0:3584].rearrange("p (n c) -> p n c", n=7)
    late = b["ya"]
    raw = [free[:, 0], free[:, 1]]
    squares = [free[:, 2], free[:, 3]]
    staged = [free[:, 4], free[:, 5]]
    normal = free[:, 6]
    m1, m2 = late[:, 0], late[:, 1]
    small = late[:, 2, 0:96].rearrange("p (n c) -> p n c", c=8)
    ssq, mean, root, rstd = ([small[:, 2 * j], small[:, 2 * j + 1]] for j in range(4))
    normed = [n for n, (c, t) in enumerate(units) if c != "vb"]
    M = len(normed)
    names = ("product", "copied", "squared", "meaned", "rooted", "staged", "turned", "placed", "chain", "v_copied")
    product, copied, squared, meaned, rooted, staged_s, turned, placed, chain, v_copied = (k.sem(f"blend_{n}") for n in names)

    def token0(t):
        return t * P

    ends = {c: max(n for n, u in enumerate(units) if u[0] == c) + 1 for c in order}

    with nc.Block() as block:
        @block.sync
        def _(sp):
            for i, c in enumerate(order):
                sp.wait_ge(product, ends[c])
                k.load_chunk(sp, first + i + NSLOT)

        @block.tensor
        def _(pe):
            for n in range(len(units) + 2):
                if n < len(units):
                    c, t = units[n]
                    wd = width.get(c, NB)
                    w = k.chunk(pe, first + order.index(c), wd)
                    if n >= 4:
                        pe.wait_ge(copied, n - 3)
                    for d in range(DT):
                        i = nc.tensor.matmul(k.psum[:, n % 4, 0:wd], k.turned[:, d, t * P:(t + 1) * P], w[:, d, :],
                                             start=(d == 0), stop=(d == DT - 1))
                    i.then_inc(product, 1)
                m = n - 2
                if 0 <= m < M:
                    c, t = units[m]
                    pe.wait_ge(staged_s, m + 1)
                    if m >= 2:
                        pe.wait_ge(placed, m - 1)
                    for f in range(2 if c == "kva" else 4):
                        i = nc.tensor.transpose(k.psum[:, 4 + m % 2, f * P:(f + 1) * P],
                                                staged[m % 2][:, f * P:(f + 1) * P], k.cst("ident"))
                    i.then_inc(turned, 1)

        @block.scalar
        def _(act):
            for n in range(len(units) + 3):
                if n < len(units):
                    c, t = units[n]
                    act.wait_ge(product, n + 1)
                    ps = k.psum[:, n % 4, :]
                    if c == "vb":
                        nc.scalar.activation(b["vb"][:, t, :], ps, ACT.Copy).then_inc(copied, 1)
                    else:
                        wd = width.get(c, NB)
                        if n >= 2:
                            act.wait_ge(staged_s, n - 1)
                        nc.scalar.activation(raw[n % 2][:, 0:wd], ps[:, 0:wd], ACT.Copy).then_inc(copied, 1)
                        act.wait_ge(copied, n + 1)
                        wd = P if c == "kva" else NB
                        nc.scalar.activation(squares[n % 2][:, 0:wd], raw[n % 2][:, 0:wd], ACT.Square).then_inc(squared, 1)
                        act.wait_ge(meaned, n + 1)
                        nc.scalar.activation(root[n % 2][:, 0:wd // HD], mean[n % 2][:, 0:wd // HD], ACT.Sqrt).then_inc(rooted, 1)
                m = n - 3
                if 0 <= m < M:
                    c, t = units[m]
                    tiles = 2 if c == "kva" else 4
                    act.wait_ge(turned, m + 1)
                    dst = b["ka" if c == "kva" else c]
                    nc.scalar.activation(dst[:, :, token0(t):token0(t) + P],
                                         k.psum[:, 4 + m % 2, 0:tiles * P].rearrange("p (f s) -> p f s", f=tiles),
                                         ACT.Copy, scale=HD ** -0.5 if c[0] == "q" else 1.0).then_inc(placed, 1)

        @block.vector
        def _(dve):
            own, V = Count(chain), nc.vector

            def heads_of(x, heads):
                return x[:, 0:heads * HD].rearrange("p (h c) -> p h c", c=HD)

            for m in range(M + 1):
                if m < M:
                    c, t = units[m]
                    heads = 2 if c == "kva" else 8
                    dve.wait_ge(squared, m + 1)
                    own.then_wait(dve, V.tensor_reduce(ssq[m % 2][:, 0:heads], heads_of(squares[m % 2], heads), AX.X, ALU.add))
                    V.tensor_scalar(mean[m % 2][:, 0:heads], ssq[m % 2][:, 0:heads], 1.0 / HD, EPS, ALU.mult,
                                    ALU.add).then_inc(meaned, 1)
                n = m - 1
                if n < 0:
                    continue
                c, t = units[n]
                heads = 2 if c == "kva" else 8
                wide = [P, heads, HD]
                dve.wait_ge(rooted, n + 1)
                r, x, y = rstd[n % 2][:, 0:heads], heads_of(raw[n % 2], heads), heads_of(normal, heads)
                own.then_wait(dve, V.reciprocal(r, root[n % 2][:, 0:heads]))
                if n:
                    dve.wait_ge(staged_s, n)
                own.then_wait(dve, V.tensor_tensor(y, x, r.unsqueeze(2).broadcast_to(wide), ALU.mult))
                gain = k.head_gains[:, gain_of[c] * HD:(gain_of[c] + 1) * HD].unsqueeze(1).broadcast_to(wide)
                if c == "kva":
                    V.tensor_copy(b["va"][:, t, :], raw[n % 2][:, P:2 * P])
                if n >= 2:
                    dve.wait_ge(turned, n - 1)
                out = staged[n % 2]
                o = heads_of(out if c != "kva" else normal, heads)
                if t >= ST:
                    if c == "kva":
                        own.then_wait(dve, V.tensor_tensor(y, y, gain, ALU.mult))
                    else:
                        V.tensor_tensor(o, y, gain, ALU.mult).then_inc(staged_s, 1)
                else:
                    own.then_wait(dve, V.tensor_tensor(y, y, gain, ALU.mult))
                    yp = y.rearrange("p h (c two) -> p h c two", two=2)
                    a1 = heads_of(m1, heads).rearrange("p h (c two) -> p h c two", two=2)
                    a2 = heads_of(m2, heads).rearrange("p h (c two) -> p h c two", two=2)
                    op = o.rearrange("p h (c two) -> p h c two", two=2)
                    half = [P, heads, HD // 2]
                    cos = rope[:, 0, t, :].unsqueeze(1).broadcast_to(half)
                    sin = rope[:, 1, t, :].unsqueeze(1).broadcast_to(half)
                    V.tensor_tensor(a1[:, :, :, 0], yp[:, :, :, 0], cos, ALU.mult)
                    V.tensor_tensor(a1[:, :, :, 1], yp[:, :, :, 1], cos, ALU.mult)
                    V.tensor_tensor(a2[:, :, :, 0], yp[:, :, :, 1], sin, ALU.mult)
                    own.then_wait(dve, V.tensor_tensor(a2[:, :, :, 1], yp[:, :, :, 0], sin, ALU.mult))
                    V.tensor_tensor(op[:, :, :, 0], a1[:, :, :, 0], a2[:, :, :, 0], ALU.subtract)
                    j = V.tensor_tensor(op[:, :, :, 1], a1[:, :, :, 1], a2[:, :, :, 1], ALU.add)
                    if c == "kva":
                        own.then_wait(dve, j)
                    else:
                        j.then_inc(staged_s, 1)
                if c == "kva":
                    V.tensor_copy(out[:, 0:4 * HD].rearrange("p (h b c) -> p h b c", b=2, c=HD),
                                  y.unsqueeze(2).broadcast_to([P, 2, 2, HD])).then_inc(staged_s, 1)


@stage
def blend_heads_a(k, b):
    nc = k.nc
    units = [(i, h) for i in range(ST) for h in range(AH)]
    N = len(units)
    prob = b["free"][:, 0:3 * KEYS].rearrange("p (n s) -> p n s", n=3)
    prob_t = b["free"][:, 3 * KEYS:5 * KEYS].rearrange("p (n s) -> p n s", n=2)
    flat = k.psum.rearrange("p b s -> p (b s)")
    scores = lambda n: flat[:, 2 * NB * (n % 2):2 * NB * (n % 2) + KEYS]
    turned_bank = flat[:, 4 * NB:4 * NB + KEYS]
    top, total, inv = (k.stat[:, 8 * j:8 * j + 8] for j in range(3))
    names = ("score", "topped", "exp", "inverse", "scaled", "turned", "placed", "product", "kept")
    score, topped, exped, inverse, scaled, turned, placed, product, kept = (k.sem(f"branch_a_{n}") for n in names)

    with nc.Block() as block:
        @block.tensor
        def _(pe):
            for n in range(N + 3):
                if n < N:
                    i, h = units[n]
                    r = HD * (h % 2)
                    if n >= 2:
                        pe.wait_ge(exped, n - 1)
                    for lo, hi in ((0, S), (S, KEYS)):
                        j = nc.tensor.matmul(scores(n)[:, lo:hi], b["qa"][r:r + HD, h // 2, i * P:(i + 1) * P],
                                             b["ka"][r:r + HD, h // 4, lo:hi], start=True, stop=True)
                    j.then_inc(score, 1)
                m = n - 2
                if 0 <= m < N:
                    pe.wait_ge(scaled, m + 1)
                    if m >= 1:
                        pe.wait_ge(placed, m)
                    for t in range(KT2):
                        j = nc.tensor.transpose(turned_bank[:, t * P:(t + 1) * P], prob[:, m % 3, t * P:(t + 1) * P],
                                                k.cst("ident"))
                    j.then_inc(turned, 1)
                m = n - 3
                if 0 <= m < N:
                    i, h = units[m]
                    r, pair = HD * (h % 2), m // 2
                    pe.wait_ge(placed, m + 1)
                    if h % 2 == 0 and pair >= 2:
                        pe.wait_ge(kept, pair - 1)
                    for t in range(KT2):
                        j = nc.tensor.matmul(k.psum[r:r + HD, 6 + pair % 2, 0:P], b["va"][:, t, (h // 4) * HD:(h // 4 + 1) * HD],
                                             prob_t[:, m % 2, t * P:(t + 1) * P], start=(t == 0), stop=(t == KT2 - 1),
                                             tile_position=(0, r))
                    j.then_inc(product, 1)

        @block.vector
        def _(dve):
            V = nc.vector
            for n in range(N + 4):
                if n < N:
                    dve.wait_ge(score, n + 1)
                    V.tensor_reduce(top[:, n % 8:n % 8 + 1], scores(n), AX.X, ALU.max, negate=True).then_inc(topped, 1)
                if 1 <= n <= N:
                    m = n - 1
                    dve.wait_ge(exped, m + 1)
                    V.reciprocal(inv[:, m % 8:m % 8 + 1], total[:, m % 8:m % 8 + 1]).then_inc(inverse, 1)
                m = n - 4
                if 0 <= m < N and m % 2 == 1:
                    i, h = units[m]
                    dve.wait_ge(product, m + 1)
                    V.tensor_copy(b["ya"][:, h // 2, i * P:(i + 1) * P], k.psum[:, 6 + (m // 2) % 2, 0:P]).then_inc(kept, 1)

        @block.scalar
        def _(act):
            for n in range(N + 2):
                if n < N:
                    act.wait_ge(topped, n + 1)
                    if n >= 3:
                        act.wait_ge(turned, n - 2)
                    nc.scalar.activation(prob[:, n % 3, :], scores(n), ACT.Exp, bias=top[:, n % 8:n % 8 + 1],
                                         accum_out=total[:, n % 8:n % 8 + 1]).then_inc(exped, 1)
                m = n - 2
                if m >= 0:
                    act.wait_ge(turned, m + 1)
                    if m >= 2:
                        act.wait_ge(product, m - 1)
                    nc.scalar.activation(prob_t[:, m % 2, :], turned_bank, ACT.Copy).then_inc(placed, 1)

        @block.gpsimd
        def _(pool):
            for n in range(N):
                pool.wait_ge(inverse, n + 1)
                nc.gpsimd.tensor_scalar(prob[:, n % 3, :], prob[:, n % 3, :], inv[:, n % 8:n % 8 + 1], 1.0,
                                        ALU.mult, ALU.mult).then_inc(scaled, 1)


@stage
def blend_heads_b(k, b):
    nc = k.nc
    units = [(i, h) for i in range(ST) for h in range(BH)]
    N = len(units)
    prob = b["free"][:, 0:4 * KEYS].rearrange("p (n m s) -> p n m s", n=2, m=2)
    prob_t = b["free"][:, 4 * KEYS:5 * KEYS]
    flat = k.psum.rearrange("p b s -> p (b s)")
    scores = lambda m: flat[:, 2 * NB * m:2 * NB * m + KEYS]
    turned_bank = flat[:, 4 * NB:4 * NB + KEYS]
    top, total, inv = (k.stat[:, 8 * j:8 * j + 8] for j in range(3))
    names = ("score", "topped", "exp", "inverse", "weight", "scaled", "mixed", "turned", "placed", "product", "kept")
    (score, topped, exped, inverse, weight, scaled, mixed, turned, placed, product,
     kept) = (k.sem(f"branch_b_{n}") for n in names)

    def at(x, n, m):
        j = (2 * n + m) % 8
        return x[:, j:j + 1]

    with nc.Block() as block:
        @block.tensor
        def _(pe):
            for n in range(N + 2):
                if n < N:
                    i, h = units[n]
                    for m in range(2):
                        if n >= 1:
                            pe.wait_ge(exped, 2 * n - 1 + m)
                        for lo, hi in ((0, S), (S, KEYS)):
                            j = nc.tensor.matmul(scores(m)[:, lo:hi], b["qb"][HD * m:HD * (m + 1), h, i * P:(i + 1) * P],
                                                 b["kb"][HD * m:HD * (m + 1), h, lo:hi], start=True, stop=True)
                        j.then_inc(score, 1)
                m = n - 1
                if 0 <= m < N:
                    i, h = units[m]
                    pe.wait_ge(mixed, m + 1)
                    if m >= 1:
                        pe.wait_ge(placed, m)
                    for t in range(KT2):
                        j = nc.tensor.transpose(turned_bank[:, t * P:(t + 1) * P], prob[:, m % 2, 0, t * P:(t + 1) * P],
                                                k.cst("ident"))
                    j.then_inc(turned, 1)
                    pe.wait_ge(placed, m + 1)
                    if m >= 2:
                        pe.wait_ge(kept, m - 1)
                    for t in range(KT2):
                        j = nc.tensor.matmul(k.psum[:, 6 + m % 2, 0:P], b["vb"][:, t, h * P:(h + 1) * P],
                                             prob_t[:, t * P:(t + 1) * P], start=(t == 0), stop=(t == KT2 - 1))
                    j.then_inc(product, 1)

        @block.vector
        def _(dve):
            V = nc.vector
            for n in range(N + 1):
                if n < N:
                    for m in range(2):
                        dve.wait_ge(score, 2 * n + m + 1)
                        V.tensor_reduce(at(top, n, m), scores(m), AX.X, ALU.max, negate=True).then_inc(topped, 1)
                    for m in range(2):
                        dve.wait_ge(exped, 2 * n + m + 1)
                        V.reciprocal(at(inv, n, m), at(total, n, m)).then_inc(inverse, 1)
                    dve.wait_ge(inverse, 2 * n + 2)
                    V.tensor_tensor(at(inv, n, 1), at(inv, n, 1), k.neg_lam, ALU.mult).then_inc(weight, 1)
                    dve.wait_ge(weight, n + 1)
                    dve.wait_ge(scaled, n + 1)
                    V.scalar_tensor_tensor(out=prob[:, n % 2, 0, :], in0=prob[:, n % 2, 1, :], scalar=at(inv, n, 1),
                                           in1=prob[:, n % 2, 0, :], op0=ALU.mult, op1=ALU.add).then_inc(mixed, 1)
                m = n - 1
                if m >= 0:
                    i, h = units[m]
                    dve.wait_ge(product, m + 1)
                    V.tensor_copy(b["yb"][:, h, i * P:(i + 1) * P], k.psum[:, 6 + m % 2, 0:P]).then_inc(kept, 1)

        @block.scalar
        def _(act):
            for n in range(N + 1):
                if n < N:
                    for m in range(2):
                        act.wait_ge(topped, 2 * n + m + 1)
                        if n >= 2:
                            act.wait_ge(turned, n - 1)
                        nc.scalar.activation(prob[:, n % 2, m, :], scores(m), ACT.Exp, bias=at(top, n, m),
                                             accum_out=at(total, n, m)).then_inc(exped, 1)
                m = n - 1
                if m >= 0:
                    act.wait_ge(turned, m + 1)
                    if m >= 1:
                        act.wait_ge(product, m)
                    nc.scalar.activation(prob_t, turned_bank, ACT.Copy).then_inc(placed, 1)

        @block.gpsimd
        def _(pool):
            for n in range(N):
                pool.wait_ge(inverse, 2 * n + 1)
                nc.gpsimd.tensor_scalar(prob[:, n % 2, 0, :], prob[:, n % 2, 0, :], at(inv, n, 0), 1.0,
                                        ALU.mult, ALU.mult).then_inc(scaled, 1)


@stage
def blend_subnorm(k, b):
    nc = k.nc
    sq = b["free"][:, 0:2048].rearrange("p (h s) -> p h s", h=BH)
    sub = k.stat[:, 0:1]
    squared, summed, meaned, rooted, chain = (k.sem(f"subln_{n}") for n in ("squared", "summed", "meaned", "rooted", "chain"))
    with nc.Block() as block:
        @block.scalar
        def _(act):
            for h in range(BH):
                nc.scalar.activation(sq[:, h], b["yb"][:, h, :], ACT.Square).then_inc(squared, 1)
            for h in range(BH):
                act.wait_ge(meaned, h + 1)
                nc.scalar.activation(sq[:, h], sq[:, h], ACT.Sqrt).then_inc(rooted, 1)

        @block.tensor
        def _(pe):
            for h in range(BH):
                pe.wait_ge(squared, h + 1)
                nc.tensor.matmul(k.psum[:, h, :], k.cst("ones"), sq[:, h], start=True, stop=True).then_inc(summed, 1)

        @block.vector
        def _(dve):
            own, V = Count(chain), nc.vector
            own.then_wait(dve, V.tensor_scalar(sub, k.col("subln"), 1.0 - LAM_INIT, None, ALU.mult))
            for h in range(BH):
                dve.wait_ge(summed, h + 1)
                V.tensor_scalar(sq[:, h], k.psum[:, h, :], 1.0 / P, SUBLN_EPS, ALU.mult, ALU.add).then_inc(meaned, 1)
            for h in range(BH):
                dve.wait_ge(rooted, h + 1)
                own.then_wait(dve, V.reciprocal(sq[:, h], sq[:, h]))
                V.scalar_tensor_tensor(out=b["yb"][:, h, :], in0=b["yb"][:, h, :], scalar=sub, in1=sq[:, h],
                                       op0=ALU.mult, op1=ALU.mult)


@stage
def blend_merge(k, b):
    nc = k.nc
    first = FIRST["ga"]
    merged = k.work[:, 0:4096].rearrange("p (f s) -> p f s", f=8)
    gate = k.work[:, 4096:6144].rearrange("p (n s) -> p n s", n=4)
    part = k.work[:, 6144:10240].rearrange("p (n s) -> p n s", n=8)
    product, opened, gated, added = (k.sem(f"merge_{n}") for n in ("product", "opened", "gated", "added"))
    units = [(half, br, f) for half in range(2) for br in range(2) for f in range(4)]
    with nc.Block() as block:
        @block.sync
        def _(sp):
            for c in range(4):
                sp.wait_ge(product, 8 * (c + 1))
                k.load_chunk(sp, first + 2 * c + NSLOT)
                k.load_chunk(sp, first + 2 * c + 1 + NSLOT)

        @block.tensor
        def _(pe):
            for n, (half, br, ff) in enumerate(units):
                wg = k.chunk(pe, first + 4 * half + 2 * br, NB)
                wo = k.chunk(pe, first + 4 * half + 2 * br + 1, NB)
                if n >= 4:
                    pe.wait_ge(gated, n - 3)
                for d in range(DT):
                    i = nc.tensor.matmul(k.psum[:, 2 * (n % 4), :], wg[:, d, ff * P:(ff + 1) * P], k.turned[:, d, 0:S],
                                         start=(d == 0), stop=(d == DT - 1))
                i.then_inc(product, 1)
                y = b["ya" if br == 0 else "yb"]
                for c in range(4):
                    i = nc.tensor.matmul(k.psum[:, 2 * (n % 4) + 1, :], wo[:, c, ff * P:(ff + 1) * P], y[:, c, :],
                                         start=(c == 0), stop=(c == 3))
                i.then_inc(product, 1)

        @block.scalar
        def _(act):
            for n in range(len(units)):
                act.wait_ge(product, 2 * n + 1)
                if n >= 4:
                    act.wait_ge(gated, n - 3)
                nc.scalar.activation(gate[:, n % 4], k.psum[:, 2 * (n % 4), :], ACT.Sigmoid).then_inc(opened, 1)

        @block.vector
        def _(dve):
            for n in range(len(units)):
                dve.wait_ge(product, 2 * n + 2)
                dve.wait_ge(opened, n + 1)
                if n >= 8:
                    dve.wait_ge(added, n % 4 + 1)
                nc.vector.tensor_tensor(part[:, n % 8], gate[:, n % 4], k.psum[:, 2 * (n % 4) + 1, :],
                                        ALU.mult).then_inc(gated, 1)

        @block.gpsimd
        def _(pool):
            for f in range(DT):
                half, ff = f // 4, f % 4
                pool.wait_ge(gated, 8 * half + ff + 5)
                nc.gpsimd.tensor_tensor(merged[:, f, :], part[:, ff], part[:, 4 + ff], ALU.add).then_inc(added, 1)
    return lambda ki: merged[:, ki, :]


EXTRA = NBLK - NE + 2
ROLES = ("gate", "up", "gate", "up", "down", "down")
PAD_ROWS = S * NK
SLOTS_E = S // CAP


PIECES = 12
NHI = 3
BY_POOL = (5, 10)


def expert_layout(k):
    e, w = {}, k.work
    piece_at = lambda n: k.arena_r[n // 2][:, n % 2 * PIECE:(n % 2 + 1) * PIECE]
    e["raw"] = k.arena[:, 0:PIECES * PIECE].rearrange("p (n c) -> p n c", n=PIECES)
    e["low"] = [piece_at(n) for n in range(PIECES)]
    at = 2 * CHUNK

    def take(name, width, dt=F32):
        nonlocal at
        e[name] = w[:, at:at + width] if dt == F32 else w[:, at:at + width].bitcast(dt)
        at += width

    e["high"] = [piece_at(PIECES + n) for n in range(NHI)]
    at += NHI * PIECE
    e["bias_high"], e["bias_low"] = (piece_at(PIECES + NHI + n)[0:NE, :] for n in range(2))
    e["bias"] = w[0:NE, at + 2 * D:at + 4 * D]
    at += 4 * D
    take("token", NE * SLOTS_E, I32)
    take("home", NE * SLOTS_E, I32)
    take("plan", 2 * (NE + EXTRA) + 2, I32)
    take("token_col", 2, I32)
    take("home_col", 2, I32)
    e["choice"] = k.arena_r[8][0:NE, at - 4 * CHUNK:at - 4 * CHUNK + CAP]
    at += CAP
    take("open", D)
    assert at <= 20480
    e["x_rows"], _, _, e["y"], e["gate"], e["up"] = (k.turned_flat[:, n * D:(n + 1) * D] for n in range(6))
    e["x_high"], e["x_low"] = (k.operand_r[:, n * D:(n + 1) * D] for n in (1, 2))
    e["hidden_high"], e["hidden_low"] = k.operand_r[:, 6 * D:7 * D], k.small_r[:, D:2 * D]
    e["weight"] = k.small[:, 0:ST * NK]
    e["spread"] = k.small[:, 64:64 + ST * NE].rearrange("p (t e) -> p t e", t=ST)
    e["spread_t"] = k.small[0:NE, 192:192 + S]
    for name, rows in (("tokens_dram", S), ("routed", PAD_ROWS + P)):
        e[name] = k.nc.dram_tensor(name, (rows, D), F32, kind="Internal").ap()
    e["list"] = k.nc.dram_tensor("assignments", (NE * S, 1), F32, kind="Internal").ap()
    e["in"] = [k.nc.alloc_semaphore(name=f"expert_weights_in_{n}") for n in range(PIECES)]
    return e


def load_expert_piece(k, e, sp, q, expert):
    role, part = q // 2, q % 2
    half = (0, 0, 1, 1, 0, 1)[role]
    src = k.io[ROLES[role]].rearrange("(e h) p (s c) -> e h s p c", h=2, s=2)
    sp.dma_start(e["raw"][:, q, :], src[expert, half, part]).then_inc(e["in"][q], 16)


@stage
def route(k, e):
    nc = k.nc
    rows = [k.work[:, 11264 + D * t:11264 + D * (t + 1)] for t in range(3)] + [k.gate_rows[:, 0:D]]
    free = k.work[:, 8192:11264]
    NA = ST * NK
    used = 0

    def take(width, **shape):
        nonlocal used
        used += width
        assert used <= free.shape[1]
        return free[:, used - width:used]

    router = take(DT * NE).rearrange("p (d e) -> p d e", d=DT)
    router_b = take(NE)
    logits = take(ST * NE).rearrange("p (t e) -> p t e", t=ST)
    best = take(ST * 8).rearrange("p (t n) -> p t n", t=ST)
    index = take(ST * 8).rearrange("p (t n) -> p t n", t=ST).bitcast(U32)
    index_f = take(NA)
    chosen = take(NA * NE).rearrange("p (a e) -> p a e", a=NA)
    spare = take(NA * NE).rearrange("p (a e) -> p a e", a=NA)
    member = take(ST * NE).rearrange("p (t e) -> p t e", t=ST)
    rank = take(ST * NE).rearrange("p (t e) -> p t e", t=ST)
    place, place_f = take(NA).bitcast(I32), take(NA)
    total, top = take(ST), take(ST)
    count, extra, end = take(NE), take(NE), take(NE)
    part = take(3 * NE).rearrange("p (n e) -> p n e", n=3)
    plan_f = take(2 * (NE + EXTRA) + 2)
    listed, value = take(P), take(P)
    weight = e["weight"].rearrange("p (t n) -> p t n", t=ST)
    NP = NE + EXTRA
    index_3d = lambda a: a.rearrange("p (t n) -> p t n", t=ST)
    names = ("inputs", "list_ready", "logits", "chain", "exp", "member", "ranked", "counted", "placed", "scattered",
             "list_in", "list_turned", "spread", "spread_turned", "rows_out", "turned_back", "copied", "bias_in", "bias_split")
    (inputs, list_ready, logits_s, chain, exped, member_s, ranked, counted, placed_s, scattered, list_in, list_turned,
     spread_s, spread_turned, rows_out, turned_back, copied, bias_in, bias_split) = (k.sem(f"route_{n}") for n in names)

    with nc.Block() as block:
        @block.sync
        def _(sp):
            sp.dma_start(e["list"].rearrange("(a b) c -> a (b c)", a=P), k.io["pad_list"].rearrange("(a b) c -> a (b c)", a=P)).then_inc(list_ready, 16)
            for q in range(PIECES):
                load_expert_piece(k, e, sp, q, 0)
            for t in range(ST):
                sp.wait_ge(copied, 2 * t + 2)
                sp.dma_start(e["tokens_dram"][t * P:(t + 1) * P, :], rows[t]).then_inc(rows_out, 16)
            sp.wait_ge(rows_out, 16 * ST)

        @block.scalar
        def _(act):
            act.dma_start(router, k.io["router"].rearrange("p (d e) -> p d e", d=DT)).then_inc(inputs, 16)
            act.dma_start(router_b, k.io["rows"][9, 0:NE].partition_broadcast(P)).then_inc(inputs, 16)
            act.dma_start(e["bias"], k.io["moe_bias"]).then_inc(bias_in, 16)
            for n in range(2 * ST):
                act.wait_ge(turned_back, n + 1)
                nc.scalar.activation(rows[n // 2][:, (n % 2) * NB:(n % 2 + 1) * NB], k.psum[:, 4 + n % 4, :],
                                     ACT.Copy).then_inc(copied, 1)
            act.wait_ge(exped, 1)
            nc.scalar.activation(weight, weight, ACT.Exp).then_inc(exped, 1)
            act.wait_ge(bias_in, 16)
            nc.scalar.activation(e["bias_high"], e["bias"], ACT.Copy).then_inc(bias_split, 1)
            act.wait_ge(scattered, 16 * NA)
            act.dma_start(listed, e["list"].rearrange("(b s) c -> b (s c)", s=CAP)).then_inc(list_in, 16)

        @block.tensor
        def _(pe):
            pe.wait_ge(inputs, 32)
            for t in range(ST):
                for d in range(DT):
                    i = nc.tensor.matmul(k.psum[:, 0, t * NE:(t + 1) * NE], k.turned[:, d, t * P:(t + 1) * P], router[:, d, :],
                                         start=(d == 0), stop=(d == DT - 1))
            i.then_inc(logits_s, 1)
            for n in range(2 * ST):
                if n >= 4:
                    pe.wait_ge(copied, n - 3)
                for d in range(4):
                    i = nc.tensor.transpose(k.psum[:, 4 + n % 4, d * P:(d + 1) * P],
                                            k.turned[:, 4 * (n % 2) + d, (n // 2) * P:(n // 2 + 1) * P], k.cst("ident"))
                i.then_inc(turned_back, 1)
            pe.wait_ge(member_s, 1)
            for t in range(ST):
                i = nc.tensor.matmul(k.psum[:, 2, 0:NE], k.cst("ones"), member[:, t, :], start=(t == 0), stop=(t == ST - 1))
            i.then_inc(counted, 1)
            for t in range(ST):
                for before in range(t + 1):
                    i = nc.tensor.matmul(k.psum[:, 1, t * NE:(t + 1) * NE], k.cst("ones" if before < t else "before"),
                                         member[:, before, :], start=(before == 0), stop=(before == t))
            i.then_inc(ranked, 1)
            pe.wait_ge(spread_s, 1)
            for t in range(ST):
                i = nc.tensor.transpose(k.psum[0:NE, 3, t * P:(t + 1) * P], e["spread"][:, t, :], k.cst("ident"))
            i.then_inc(spread_turned, 1)
            pe.wait_ge(list_in, 16)
            nc.tensor.transpose(k.psum[:, 4, 0:P], listed, k.cst("ident")).then_inc(list_turned, 1)

        @block.vector
        def _(dve):
            own, V = Count(chain), nc.vector
            then = lambda i: own.then_wait(dve, i)
            iota = k.cst("iota_e")
            dve.wait_ge(logits_s, 1)
            then(V.tensor_tensor(logits, k.psum[:, 0, 0:ST * NE].rearrange("p (t e) -> p t e", t=ST),
                                 router_b.unsqueeze(1).broadcast_to([P, ST, NE]), ALU.add))
            for t in range(ST):
                i = V.max(best[:, t, :], logits[:, t, :])
            then(i)
            for t in range(ST):
                i = V.max_index(index[:, t, :], best[:, t, :], logits[:, t, :])
            then(i)
            V.tensor_tensor(weight, best[:, :, 0:NK], best[:, :, 0:1].broadcast_to([P, ST, NK]), ALU.subtract).then_inc(exped, 1)
            then(V.tensor_copy(index_3d(index_f), index[:, :, 0:NK]))
            then(V.tensor_tensor(chosen, iota.unsqueeze(1).broadcast_to([P, NA, NE]),
                                 index_f.unsqueeze(2).broadcast_to([P, NA, NE]), ALU.is_equal))
            by_k = chosen.rearrange("p (t n) e -> p t e n", t=ST)
            V.tensor_reduce(member, by_k, AX.X, ALU.add).then_inc(member_s, 1)
            dve.wait_ge(counted, 1)
            then(V.tensor_copy(count, k.psum[:, 2, 0:NE]))
            for n in range(3):
                i = V.tensor_scalar(part[:, n, :], count, float(CAP * (n + 1)), None, ALU.is_gt)
            then(i)
            then(V.tensor_reduce(extra, part.rearrange("p n e -> p e n"), AX.X, ALU.add))
            then(V.tensor_tensor_scan(end, k.cst("ones")[:, 0:NE], extra, 0.0, ALU.mult, ALU.add))
            dve.wait_ge(ranked, 1)
            passed = spare[:, 0:NA, :]
            ordinal = iota[:, 0:EXTRA]
            expert_f, col_f = plan_f[:, 0:NP], plan_f[:, NP:2 * NP]
            V.tensor_scalar(plan_f[:, 2 * NP:2 * NP + 2], end[:, NE - 1:NE].broadcast_to([P, 2]), float(NE), None, ALU.add)
            V.tensor_copy(expert_f[:, 0:NE], iota)
            V.tensor_scalar(col_f[:, 0:NE], iota, float(SLOTS_E), None, ALU.mult)
            for lo in range(0, EXTRA, NA):
                n = min(NA, EXTRA - lo)
                then(V.tensor_tensor(passed[:, 0:n, :], ordinal[:, lo:lo + n].unsqueeze(2).broadcast_to([P, n, NE]),
                                     end.unsqueeze(1).broadcast_to([P, n, NE]), ALU.is_ge))
                then(V.tensor_reduce(expert_f[:, NE + lo:NE + lo + n], passed[:, 0:n, :], AX.X, ALU.add))
                then(V.tensor_tensor(passed[:, 0:n, :], passed[:, 0:n, :], extra.unsqueeze(1).broadcast_to([P, n, NE]), ALU.mult))
                then(V.tensor_reduce(col_f[:, NE + lo:NE + lo + n], passed[:, 0:n, :], AX.X, ALU.add))
            more_e, more_c = expert_f[:, NE:NP], col_f[:, NE:NP]
            then(V.tensor_scalar(more_e, more_e, float(NE - 1), None, ALU.min))
            then(V.tensor_tensor(more_c, ordinal, more_c, ALU.subtract))
            then(V.tensor_scalar(more_c, more_c, 1.0, float(SLOTS_E - 1), ALU.add, ALU.min))
            then(V.scalar_tensor_tensor(out=more_c, in0=more_e, scalar=float(SLOTS_E), in1=more_c, op0=ALU.mult, op1=ALU.add))
            V.tensor_copy(e["plan"], plan_f)
            then(V.tensor_copy(rank, k.psum[:, 1, 0:ST * NE].rearrange("p (t e) -> p t e", t=ST)))
            then(V.tensor_tensor(spare.rearrange("p (t n) e -> p t n e", t=ST), chosen.rearrange("p (t n) e -> p t n e", t=ST),
                                 rank.unsqueeze(2).broadcast_to([P, ST, NK, NE]), ALU.mult))
            then(V.tensor_reduce(place_f, spare, AX.X, ALU.add))
            then(V.scalar_tensor_tensor(out=place_f, in0=index_f, scalar=float(S), in1=place_f, op0=ALU.mult, op1=ALU.add))
            V.tensor_copy(place, place_f).then_inc(placed_s, 1)
            dve.wait_ge(exped, 2)
            then(V.tensor_reduce(total, weight, AX.X, ALU.add))
            then(V.reciprocal(total, total))
            then(V.tensor_tensor(weight, weight, total.unsqueeze(2).broadcast_to([P, ST, NK]), ALU.mult))
            then(V.tensor_tensor(spare, chosen, e["weight"].unsqueeze(2).broadcast_to([P, NA, NE]), ALU.mult))
            V.tensor_reduce(e["spread"], spare.rearrange("p (t n) e -> p t e n", t=ST), AX.X, ALU.add).then_inc(spread_s, 1)
            dve.wait_ge(bias_split, 1)
            V.tensor_tensor(e["bias_low"], e["bias"], e["bias_high"].bitcast(F32), ALU.subtract)
            dve.wait_ge(spread_turned, 1)
            V.tensor_copy(e["spread_t"], k.psum[0:NE, 3, :])
            dve.wait_ge(list_turned, 1)
            then(V.tensor_copy(value, k.psum[:, 4, 0:P]))
            V.tensor_copy(e["home"], value)
            then(V.tensor_scalar(value, value, 1.0 / NK, -0.375, ALU.mult, ALU.add))
            then(V.tensor_scalar(value, value, float(S - 1), ROUND, ALU.min, ALU.add))
            then(V.tensor_scalar(value, value, ROUND, None, ALU.subtract))
            V.tensor_copy(e["token"], value)

        @block.gpsimd
        def _(pool):
            pool.wait_ge(list_ready, 16)
            pool.wait_ge(placed_s, 1)
            for a in range(NA):
                pool.indirect_dma_start(e["list"], bass.IndirectOffsetOnAxis(ap=place[:, a:a + 1], axis=0),
                                        k.cst("assign")[:, a:a + 1], None).then_inc(scattered, 16)


@stage
def experts(k, e):
    nc = k.nc
    NP = NE + EXTRA
    plan, raw, low, high = e["plan"], e["raw"], e["low"], e["high"]
    half = lambda x, h: x[:, h * NB:(h + 1) * NB]
    names = ("x_in", "x_turned", "x_high_ready", "x_ready", "staged", "chosen", "used", "high_ready", "low_dve", "low_pool",
             "gate_ready", "up_ready", "opened", "gated", "hidden_ready", "hidden_turned", "hidden_high_ready", "hidden_split",
             "y_act", "y_dve", "y_out", "passed")
    (x_in, x_turned, x_high_ready, x_ready, staged, chosen, used, high_ready, low_dve, low_pool, gate_ready, up_ready,
     opened, gated, hidden_ready, hidden_turned, hidden_high_ready, hidden_split, y_act, y_dve, y_out,
     passed) = (k.sem(f"experts_{n}") for n in names)
    during = lambda b, q: PIECES * b + (q + 1)
    pool_before = lambda q: sum(p < q for p in BY_POOL)
    N_POOL = len(BY_POOL)

    def number_of_blocks(engine):
        return engine.value_load(plan[0:1, 2 * NP:2 * NP + 1], min_val=NE, max_val=NBLK)

    def gather_rows(pool):
        pool.indirect_dma_start(e["x_rows"], None, e["tokens_dram"],
                                bass.IndirectOffsetOnAxis(ap=e["token_col"][:, 0:1], axis=0)).then_inc(x_in, 16)

    def turn_rows():
        for d in range(DT):
            i = nc.tensor.transpose(k.psum[:, 4 + d // 4, (d % 4) * P:(d % 4 + 1) * P], e["x_rows"][:, d * P:(d + 1) * P],
                                    k.cst("ident"))
        i.then_inc(x_turned, 1)

    x_banks = k.psum[:, 4:6, :].rearrange("p b s -> p (b s)")

    def take_x_high():
        nc.scalar.activation(e["x_high"], x_banks, ACT.Copy).then_inc(x_high_ready, 1)

    def take_x_low():
        nc.vector.tensor_tensor(e["x_low"], x_banks, e["x_high"].bitcast(F32), ALU.subtract).then_inc(x_ready, 1)

    def take_high(act, b, q):
        act.wait_ge(e["in"][q], 16 * b + 16)
        nc.scalar.activation(high[q % NHI], raw[:, q, :], ACT.Copy).then_inc(high_ready, 1)

    def take_low(engine, compute, b, q, done):
        engine.wait_ge(high_ready, PIECES * b + (q + 1))
        compute.tensor_tensor(low[q], raw[:, q, :], high[q % NHI].bitcast(F32), ALU.subtract).then_inc(done, 1)

    with nc.Block() as block:
        @block.sync
        def _(sp):
            n = number_of_blocks(sp)
            with sp.Fori(1, NBLK) as b:
                with sp.If(b < n):
                    expert = sp.value_load(plan[0:1, bass.ds(b, 1)], min_val=0, max_val=NE - 1)
                    for q in range(PIECES):
                        sp.wait_ge(used, PIECES * b + (q + 2 - PIECES))
                        load_expert_piece(k, e, sp, q, expert)

        @block.gpsimd
        def _(pool):
            n = number_of_blocks(pool)
            column = pool.value_load(plan[0:1, NP:NP + 1], min_val=0, max_val=P - 1)
            nc.gpsimd.tensor_copy(e["token_col"][:, 0:1], e["token"][:, bass.ds(column, 1)]).then_inc(staged, 1)
            nc.gpsimd.tensor_copy(e["choice"], k.cst("ident")[0:NE, 0:1].broadcast_to([NE, CAP])).then_inc(chosen, 1)
            pool.wait_ge(staged, 1)
            gather_rows(pool)
            with pool.Fori(0, NBLK) as b:
                with pool.If(b < n):
                    column = pool.value_load(plan[0:1, bass.ds(b + NP, 1)], min_val=0, max_val=P - 1)
                    next_column = pool.value_load(plan[0:1, bass.ds(b + NP + 1, 1)], min_val=0, max_val=P - 1)
                    next_expert = pool.value_load(plan[0:1, bass.ds(b + 1, 1)], min_val=0, max_val=NE - 1)
                    pool.wait_ge(x_turned, b + 1)
                    nc.gpsimd.tensor_copy(e["token_col"][:, 0:1], e["token"][:, bass.ds(next_column, 1)]).then_inc(staged, 1)
                    pool.wait_ge(staged, 2 * b + 2)
                    pool.sem_inc(passed, 1)
                    gather_rows(pool)
                    for h in range(2):
                        if h == 1:
                            with pool.If(b > 0):
                                pool.wait_ge(y_out, 16 * b)
                            nc.gpsimd.tensor_copy(e["home_col"][:, 0:1], e["home"][:, bass.ds(column, 1)]).then_inc(staged, 1)
                        pool.wait_ge(opened, 2 * b + h + 1)
                        nc.gpsimd.tensor_tensor(half(e["open"], h), half(e["gate"], h), half(e["open"], h), ALU.mult).then_inc(gated, 1)
                        take_low(pool, nc.gpsimd, b, BY_POOL[h], low_pool)
                    pool.wait_ge(y_act, b + 1)
                    pool.wait_ge(y_dve, b + 1)
                    nc.gpsimd.tensor_copy(e["choice"], k.cst("ident")[0:NE, bass.ds(next_expert, 1)].broadcast_to([NE, CAP])).then_inc(chosen, 1)
                    pool.wait_ge(staged, 2 * b + 3)
                    pool.sem_inc(passed, 1)
                    pool.indirect_dma_start(e["routed"], bass.IndirectOffsetOnAxis(ap=e["home_col"][:, 0:1], axis=0),
                                            e["y"], None).then_inc(y_out, 16)
            pool.wait_ge(y_out, 16 * n)
            pool.wait_ge(x_in, 16 * n + 16)

        @block.tensor
        def _(pe):
            n = number_of_blocks(pe)
            pe.wait_ge(x_in, 16)
            nc.tensor.transpose(k.psum[:, 0, 0:P], k.cst("ident"), k.cst("ident")).then_inc(used, 1)
            turn_rows()

            def turn_hidden(b, h):
                pe.wait_ge(hidden_ready, 2 * b + h + 1)
                for f in range(4):
                    i = nc.tensor.transpose(k.psum[:, 2 * h, f * P:(f + 1) * P], e["gate"][:, (4 * h + f) * P:(4 * h + f + 1) * P],
                                            k.cst("ident"))
                i.then_inc(hidden_turned, 1)

            with pe.Fori(0, NBLK) as b:
                with pe.If(b < n):
                    pe.wait_ge(x_ready, b + 1)
                    for q in range(PIECES):
                        if q in BY_POOL:
                            pe.wait_ge(low_pool, N_POOL * b + (pool_before(q) + 1))
                        else:
                            pe.wait_ge(low_dve, (PIECES - N_POOL) * b + (q + 1 - pool_before(q)))
                        if q < 8:
                            r = q // 2
                            w = [x.rearrange("p (d f) -> p d f", d=4) for x in (high[q % NHI], low[q])]
                            for j in range(4):
                                d = 4 * (q % 2) + j
                                x = [t[:, d * P:(d + 1) * P] for t in (e["x_high"], e["x_low"])]
                                i = exact_product(nc, k.psum[:, r, :], x, (w[0][:, j, :], w[1][:, j, :]), start=(d == 0), stop=False)
                            if q % 2 == 1:
                                if q == 1:
                                    pe.wait_ge(chosen, b + 1)
                                at = (r % 2) * D + (r // 2) * NB
                                for bias in (e["bias_high"], e["bias_low"]):
                                    i = nc.tensor.matmul(k.psum[:, r, :], e["choice"], bias[:, at:at + NB],
                                                         start=False, stop=(bias is e["bias_low"]))
                        else:
                            w = [x.rearrange("p (f c) -> p f c", f=2) for x in (high[q % NHI], low[q])]
                            if q % 2 == 0:
                                pe.wait_ge(hidden_split, 2 * b + ((q - 8) // 2 + 1))
                            for j in range(2):
                                f = 2 * (q - 8) + j
                                x = [t[:, f * P:(f + 1) * P] for t in (e["hidden_high"], e["hidden_low"])]
                                for c in range(2):
                                    i = exact_product(nc, k.psum[:, 6 + c, :], x, [t[:, j, c * NB:(c + 1) * NB] for t in w],
                                                      start=(f == 0), stop=(f == DT - 1))
                        i.then_inc(used, 1)
                        if q == 5:
                            turn_hidden(b, 0)
                        if q == 7:
                            pe.wait_ge(x_in, 16 * b + 32)
                            turn_rows()
                        if q == 8:
                            turn_hidden(b, 1)

        @block.scalar
        def _(act):
            n = number_of_blocks(act)
            for q in range(2):
                take_high(act, 0, q)
            act.wait_ge(x_turned, 1)
            take_x_high()

            def open_gate(b, h):
                act.wait_ge(gate_ready, 2 * b + h + 1)
                nc.scalar.activation(half(e["open"], h), half(e["gate"], h), ACT.Sigmoid, scale=ALPHA).then_inc(opened, 1)

            def take_hidden_high(b, h):
                act.wait_ge(hidden_turned, 2 * b + h + 1)
                nc.scalar.activation(half(e["hidden_high"], h), k.psum[:, 2 * h, :], ACT.Copy).then_inc(hidden_high_ready, 1)

            with act.Fori(0, NBLK) as b:
                with act.If(b < n):
                    for q in range(PIECES):
                        if q == 9:
                            take_hidden_high(b, 1)
                        if q + 2 < PIECES:
                            act.wait_ge(used, during(b, q))
                            take_high(act, b, q + 2)
                        else:
                            with act.If(b + 1 < n):
                                act.wait_ge(used, during(b, q))
                                take_high(act, b + 1, q + 2 - PIECES)
                        if q == 2:
                            open_gate(b, 0)
                        if q == 6:
                            take_hidden_high(b, 0)
                            open_gate(b, 1)
                        if q == 8:
                            act.wait_ge(x_turned, b + 2)
                            take_x_high()
                    act.wait_ge(used, during(b, PIECES))
                    nc.scalar.activation(half(e["y"], 0), k.psum[:, 6, :], ACT.Copy).then_inc(y_act, 1)

        @block.vector
        def _(dve):
            V = nc.vector
            n = number_of_blocks(dve)
            for q in range(2):
                take_low(dve, V, 0, q, low_dve)
            dve.wait_ge(x_high_ready, 1)
            take_x_low()

            def clip_gate(b, h):
                dve.wait_ge(used, during(b, 4 * h + 2))
                V.tensor_scalar(half(e["gate"], h), k.psum[:, 2 * h, :], LIMIT, None, ALU.min).then_inc(gate_ready, 1)

            def hide(b, h):
                dve.wait_ge(used, during(b, 4 * h + 4))
                V.tensor_scalar(half(e["up"], h), k.psum[:, 2 * h + 1, :], LIMIT, -LIMIT, ALU.min, ALU.max).then_inc(up_ready, 1)
                dve.wait_ge(up_ready, 2 * b + h + 1)
                dve.wait_ge(gated, 2 * b + h + 1)
                V.scalar_tensor_tensor(out=half(e["gate"], h), in0=half(e["up"], h), scalar=1.0, in1=half(e["open"], h),
                                       op0=ALU.add, op1=ALU.mult).then_inc(hidden_ready, 1)

            def take_hidden_low(b, h):
                dve.wait_ge(hidden_high_ready, 2 * b + h + 1)
                V.tensor_tensor(half(e["hidden_low"], h), k.psum[:, 2 * h, :], half(e["hidden_high"], h).bitcast(F32), ALU.subtract).then_inc(hidden_split, 1)

            with dve.Fori(0, NBLK) as b:
                with dve.If(b < n):
                    for q in range(PIECES):
                        if q == 2:
                            clip_gate(b, 0)
                        if q == 4:
                            hide(b, 0)
                        if q == 6:
                            clip_gate(b, 1)
                        if q == 8:
                            hide(b, 1)
                        if q == 9:
                            take_hidden_low(b, 1)
                        if (q + 2) % PIECES not in BY_POOL:
                            if q + 2 < PIECES:
                                take_low(dve, V, b, q + 2, low_dve)
                            else:
                                with dve.If(b + 1 < n):
                                    take_low(dve, V, b + 1, q + 2 - PIECES, low_dve)
                        if q == 6:
                            take_hidden_low(b, 0)
                        if q == 8:
                            dve.wait_ge(x_high_ready, b + 2)
                            take_x_low()
                    dve.wait_ge(used, during(b, PIECES))
                    V.tensor_copy(half(e["y"], 1), k.psum[:, 7, :]).then_inc(y_dve, 1)


@stage
def combine(k, e, stored):
    nc = k.nc
    rows = k.arena[:, 0:ST * NK * D].rearrange("p (t n d) -> p t n d", t=ST, n=NK)
    diag = k.turned_flat[:, 0:2 * ST * P].rearrange("p (n s) -> p n s", n=2 * ST)
    acc = k.turned_flat[:, 2 * D:4 * D].rearrange("p (n d) -> p n d", n=2)
    b_down = k.turned_flat[0:NE, 4 * D:5 * D]
    g_m = k.gate_rows[:, D:2 * D]
    names = ("diagonals", "product", "partial", "summed", "gated", "added")
    diagonals, product, partial, summed, gated, added = (k.sem(f"combine_{n}") for n in names)
    biases_in = k.sem("combine_biases_in")
    rows_in = [k.sem(f"combine_rows_in_{t}") for t in range(ST)]

    def add_tile(V, dve, t):
        dve.wait_ge(gated, t + 1)
        V.tensor_tensor(k.resid[:, t, :], rows[:, t, 0, :], k.resid[:, t, :], ALU.add).then_inc(added, 1)

    with nc.Block() as block:
        @block.sync
        def _(sp):
            src = e["routed"][0:S * NK].rearrange("(t p n) d -> t p n d", t=ST, p=P)
            sp.dma_start(b_down, k.io["b_down"]).then_inc(biases_in, 16)
            for t in range(ST):
                sp.dma_start(rows[:, t], src[t]).then_inc(rows_in[t], 16)
            for t in range(ST):
                sp.wait_ge(added, t + 1)
                sp.dma_start(k.io["out"][t * P:(t + 1) * P, :], k.resid[:, t, :]).then_inc(stored, 16)
            sp.wait_ge(stored, 16 * ST)

        @block.tensor
        def _(pe):
            for t in range(ST):
                pe.wait_ge(rows_in[t], 16)
                pe.wait_ge(biases_in, 16)
                pe.wait_ge(diagonals, 2 * t + 2)
                for c in range(2):
                    for n in range(2):
                        nc.tensor.matmul(k.psum[:, 2 * t + c, :], diag[:, 2 * t + n, :], rows[:, t, n, c * NB:(c + 1) * NB],
                                         start=(n == 0), stop=False)
                    i = nc.tensor.matmul(k.psum[:, 2 * t + c, :], e["spread_t"][:, t * P:(t + 1) * P],
                                         b_down[:, c * NB:(c + 1) * NB], start=False, stop=True)
                i.then_inc(product, 1)

        @block.vector
        def _(dve):
            V = nc.vector
            w = lambda t, n: e["weight"][:, NK * t + n:NK * t + n + 1]
            for t in range(ST):
                for n in range(2):
                    V.tensor_scalar(diag[:, 2 * t + n, :], k.cst("ident"), w(t, n), None, ALU.mult).then_inc(diagonals, 1)
            for t in range(ST):
                dve.wait_ge(product, t + 1)
                if t >= 2:
                    dve.wait_ge(gated, t - 1)
                V.scalar_tensor_tensor(out=acc[:, t % 2], in0=rows[:, t, 2, :], scalar=w(t, 2),
                                       in1=k.psum[:, 2 * t:2 * t + 2, :].rearrange("p b s -> p (b s)"),
                                       op0=ALU.mult, op1=ALU.add).then_inc(partial, 1)
                dve.wait_ge(partial, t + 1)
                V.scalar_tensor_tensor(out=acc[:, t % 2], in0=rows[:, t, 3, :], scalar=w(t, 3), in1=acc[:, t % 2],
                                       op0=ALU.mult, op1=ALU.add).then_inc(summed, 1)
                if t >= 1:
                    add_tile(V, dve, t - 1)
            add_tile(V, dve, ST - 1)

        @block.gpsimd
        def _(pool):
            for t in range(ST):
                pool.wait_ge(summed, t + 1)
                nc.gpsimd.tensor_tensor(rows[:, t, 0, :], acc[:, t % 2], g_m, ALU.mult).then_inc(gated, 1)


def shape_constants():
    out = np.zeros((P, NCONST), np.float32)

    def put(name, a):
        at, width = CONST[name]
        out[:, at:at + width] = np.asarray(a, np.float32).reshape(P, width)

    i = np.arange(P)
    put("ident", np.eye(P))
    put("ones", np.ones((P, P)))
    put("before", i[:, None] < i[None, :])
    pos = np.arange(S, dtype=np.float32)
    half = HD // 2
    inv = np.power(np.float32(10000.0), -np.arange(half, dtype=np.float32) * np.float32(2.0) / np.float32(HD)).astype(np.float32)
    ang = (pos[:, None] * inv[None, :]).astype(np.float32)
    tiles = lambda a: a.reshape(ST, P, -1).transpose(1, 0, 2)
    put("rope1", np.stack([tiles(np.cos(ang.astype(np.float64))), tiles(np.sin(ang.astype(np.float64)))], 1))
    pairs, grid_w = HD // 4, 64
    row, col = np.repeat(np.arange(S // grid_w), grid_w), np.tile(np.arange(grid_w), S // grid_w)
    inv = (np.float32(1.0) / np.power(np.float32(10000.0), np.arange(pairs, dtype=np.float32) / np.float32(pairs))).astype(np.float32)
    ang = np.concatenate([row.astype(np.float32)[:, None] * inv, col.astype(np.float32)[:, None] * inv], -1).astype(np.float32)
    put("rope2", np.stack([tiles(np.cos(ang.astype(np.float64))), tiles(np.sin(ang.astype(np.float64)))], 1))
    put("iota_e", np.tile(np.arange(NE), (P, 1)))
    tok = np.arange(ST)[None, :, None] * P + i[:, None, None]
    put("assign", tok * NK + np.arange(NK))
    return out


def columns(a):
    return np.ascontiguousarray(np.asarray(a).reshape(-1, P).T)


def chunks_by_columns(w, width=NB):
    kk, n = w.shape
    return w.reshape(kk // P, P, n // width, width).transpose(2, 1, 0, 3).reshape(n // width, P, -1)


def lay_out(inp):
    g = {n: np.asarray(a) for n, a in inp.items()}
    cols = np.zeros((P, NCOLS), np.float32)

    def put(name, a):
        at, width = COLS[name]
        cols[:, at:at + width] = a.reshape(P, width)

    put("gains", columns(g["norm_g"].reshape(-1)))
    put("ssm_d", columns(g["ssm_d"].reshape(-1)))
    states = lambda a: a.reshape(NJ, P).T
    put("lam_re", states(g["ssm_lam_re"][0]))
    put("lam_im", states(g["ssm_lam_im"][0]))
    put("log_dt", states(np.repeat(g["ssm_log_dt"][0][:, None], 64, 1)))
    put("cond", np.stack([columns(g["c_2"].reshape(-1)), columns(g["c_ctx_2"])], 2))
    put("b_ada", columns(g["b_ada_2"][0]))
    put("norm_attn", columns(g["norm_attn_2"][0]))
    put("norm_mlp", columns(g["norm_mlp_2"][0]))
    put("subln", columns(g["subln_b_2"][0]))
    lam = np.zeros((P, 4), np.float32)
    for i, n in enumerate(("lambda_q1_2", "lambda_k1_2", "lambda_q2_2", "lambda_k2_2")):
        lam[:HD, i] = g[n][0]
    put("lambdas", lam)

    bc = np.zeros((P, 4, NJ, 32), np.float32)
    for i, n in enumerate(("ssm_b_re", "ssm_b_im")):
        b = g[n][0].reshape(NJ, 2, 64, 16)
        for gg in range(2):
            bc[64 * gg:64 * gg + 64, i, :, 16 * gg:16 * gg + 16] = b[:, gg].transpose(1, 0, 2)
    for i, n in enumerate(("ssm_c_re", "ssm_c_im")):
        c = g[n][0].reshape(NJ, 2, 16, 64)
        for gg in range(2):
            bc[64 * gg:64 * gg + 64, 2 + i, :, 16 * gg:16 * gg + 16] = c[:, gg].transpose(2, 0, 1)

    dense = np.zeros((NDENSE, P, CHUNK), np.float32)

    def fill(name, a):
        at = FIRST[name]
        dense[at:at + len(a), :, :a.shape[2]] = a

    def by_rows(w):
        return w.reshape(-1, 4, P, D).transpose(0, 2, 1, 3).reshape(-1, P, CHUNK)

    fill("ssm_in", chunks_by_columns(g["ssm_w_in"][0]))
    fill("ssm_glu", chunks_by_columns(g["ssm_w_glu"][0]))
    fill("ssm_out", by_rows(g["ssm_w_out"][0]))
    fill("ada", chunks_by_columns(g["w_ada_2"][0]))
    for i in range(2):
        fill(f"w1_{i}", chunks_by_columns(g["mlp_w1"][i]))
        fill(f"w2_{i}", by_rows(g["mlp_w2"][i]))
    fill("att_in", chunks_by_columns(g["att_w_in"][0][:, :2048]))
    fill("att_idx", chunks_by_columns(g["att_w_in"][0][:, 2048:], 72))
    fill("att_out", by_rows(g["att_w_out"][0]))
    w = g["w_in_2"][0]
    fill("qa", chunks_by_columns(w[:, 0:512]))
    fill("kva", chunks_by_columns(w[:, 512:768], 256))
    fill("qb", chunks_by_columns(w[:, 768:1280]))
    fill("kb", chunks_by_columns(w[:, 1280:1792]))
    fill("vb", chunks_by_columns(w[:, 1792:2304]))
    for h, end in enumerate(("", "1")):
        half = slice(h * NB, (h + 1) * NB)
        fill("ga" + end, chunks_by_columns(w[:, 2304:3328][:, half]))
        fill("gb" + end, chunks_by_columns(w[:, 3328:4352][:, half]))
        fill("w_oa" + end, chunks_by_columns(g["w_oa_2"][0][:, half]))
        fill("w_ob" + end, chunks_by_columns(g["w_ob_2"][0][:, half]))
    fill("w_out", by_rows(g["w_out_2"][0]))
    rows = np.zeros((12, D), np.float32)
    rows[0:8] = g["norm_g"].reshape(8, D)
    rows[8, 0:4 * HD] = np.concatenate([g[n][0] for n in ("q_norm_a_2", "k_norm_a_2", "q_norm_b_2", "k_norm_b_2")])
    rows[9, 0:NE] = g["router_b_2"][0]
    gate = g["w_gate_2"][0].reshape(NE, DT, P, 2, NB).transpose(0, 3, 2, 1, 4).reshape(NE * 2, P, CHUNK)
    up = g["w_up_2"][0].reshape(NE, DT, P, 2, NB).transpose(0, 3, 2, 1, 4).reshape(NE * 2, P, CHUNK)
    down = g["w_down_2"][0].reshape(NE, 2, 4, P, D).transpose(0, 1, 3, 2, 4).reshape(NE * 2, P, CHUNK)
    pad = np.tile(S * NK + np.arange(P, dtype=np.float32), (4 * NE, 1))
    return {
        "x": g["x"].reshape(S, D), "ctx": g["ctx_2"].reshape(CTX, D), "cols": cols, "consts": shape_constants(),
        "ssm_bc": bc.reshape(P, -1), "dense": dense, "rows": rows, "moe_bias": np.concatenate([g["b_gate_2"][0], g["b_up_2"][0]], 1),
        "router": chunks_by_columns(g["router_w_2"][0], NE)[0], "b_down": g["b_down_2"][0],
        "gate": np.ascontiguousarray(gate), "up": np.ascontiguousarray(up), "down": np.ascontiguousarray(down),
        "pad_list": pad.reshape(4 * NE * P, 1),
    }


_SHAPES = {
    "x": (S, D), "ctx": (CTX, D), "cols": (P, NCOLS), "consts": (P, NCONST), "ssm_bc": (P, 4 * NJ * 32),
    "dense": (NDENSE, P, CHUNK), "rows": (12, D), "moe_bias": (NE, 2 * D), "router": (P, DT * NE),
    "b_down": (NE, D), "gate": (2 * NE, P, CHUNK), "up": (2 * NE, P, CHUNK), "down": (2 * NE, P, CHUNK),
    "pad_list": (4 * NE * P, 1),
}


def program(nc, io):
    with ExitStack() as ctx:
        k = Kernel(nc, ctx, io)
        k.stored = nc.alloc_semaphore(name="output_stored")
        gains, row = k.col("gains"), k.io["rows"]
        gain = lambda n: gains[:, n * DT:(n + 1) * DT]
        stages(k, gain, row)


def stages(k, gain, row):
    load_inputs(k)
    norm_turned(k, "ssm_norm", k.resid, ST, 0, gain(0))
    ssm_parameters(k)
    ssm_input(k)
    ssm_tables(k)
    ssm_scan(k)
    lhs = ssm_gate(k)
    project_residual(k, "ssm_out", FIRST["ssm_out"], 1, lhs, row[1], True)
    norm_turned(k, "mlp0_norm", k.resid, ST, 0, gain(2), None, True)
    lhs = mlp_hidden(k, "mlp0_hidden", FIRST["w1_0"])
    project_residual(k, "mlp0_out", FIRST["w2_0"], 8, lhs, row[3], True)
    norm_turned(k, "att_norm", k.resid, ST, 0, gain(4))
    a = attention_layout(k)
    attention_project(k, a)
    attention_select(k, a)
    lhs = attention_heads(k, a)
    project_residual(k, "att_out", FIRST["att_out"], 2, lhs, row[5], True)
    norm_turned(k, "mlp1_norm", k.resid, ST, 0, gain(6), None, True)
    lhs = mlp_hidden(k, "mlp1_hidden", FIRST["w1_1"])
    project_residual(k, "mlp1_out", FIRST["w2_1"], 8, lhs, row[7], True)
    modulation(k)
    affine = k.affine[:, :].rearrange("p (n d) -> p n d", n=6)
    ctx_rows = load_context(k)
    norm_turned(k, "ctx_norm", ctx_rows, CT, S, affine[:, 2], affine[:, 3])
    norm_turned(k, "blend_norm", k.resid, ST, 0, affine[:, 0], affine[:, 1])
    b = blend_layout(k)
    blend_project(k, b)
    blend_heads_a(k, b)
    blend_heads_b(k, b)
    blend_subnorm(k, b)
    lhs = blend_merge(k, b)
    project_residual(k, "blend_out", FIRST["w_out"], 2, lhs, k.gate_rows[:, 0:D], False)
    norm_turned(k, "moe_norm", k.resid, ST, 0, affine[:, 4], affine[:, 5])
    e = expert_layout(k)
    route(k, e)
    experts(k, e)
    combine(k, e, k.stored)


def kernel(**inputs):
    import concourse.bacc as bacc
    from concourse.bass_utils import run_bass_kernel_spmd

    nc = bacc.Bacc("TRN2", target_bir_lowering=False, num_devices=1)
    io = {n: nc.dram_tensor(f"in_{n}", s, F32, kind="ExternalInput").ap() for n, s in _SHAPES.items()}
    io["out"] = nc.dram_tensor("out_0", (S, D), F32, kind="ExternalOutput").ap()
    program(nc, io)
    arrays = {f"in_{n}": np.ascontiguousarray(a) for n, a in lay_out(inputs).items()}
    r = run_bass_kernel_spmd(nc, [arrays], core_ids=[0])
    return r.results[0]["out_0"].reshape(1, S, D)
```

```python
from contextlib import ExitStack

import numpy as np

import concourse.bass as bass
from concourse import mybir

F32 = mybir.dt.float32
F32R = mybir.dt.float32r
I32 = mybir.dt.int32
U32 = mybir.dt.uint32
ALU = mybir.AluOpType
ACT = mybir.ActivationFunctionType
AX = mybir.AxisListType

P = 128
D = 1024
DT = D // P
S = 512
ST = S // P
CTX = 256
CT = CTX // P
NB = 512
NSLOT = 3
CHUNK = 8 * NB
PIECE = CHUNK // 2

DFF = 4096
SSM_W = 512
WT = SSM_W // P
NJ = 16
HD = 64
NH = 16
NKV = 4
IH = 8
TOPK = 128
EPS = 1e-6

AH = 8
BH = 4
KEYS = S + CTX
KT2 = KEYS // P
SUBLN_EPS = 1e-5
LAM_INIT = 0.8 - 0.6
NE = 32
NK = 4
CAP = 128
NBLK = 48
N_MOD = 6
LIMIT = 7.0
ALPHA = 1.702

TWO_PI_HI, TWO_PI_MID = 6.28125, 0.0019350051879882812
TWO_PI_LO = float(2 * np.pi - 6.28125 - 0.0019350051879882812)
ROUND = 1.5 * 2.0 ** 23
PI_F = 3.1415925

COLS = {}
_n = 0
for _name, _width in (("gains", 8 * DT), ("ssm_d", WT), ("lam_re", NJ), ("lam_im", NJ), ("log_dt", NJ),
                      ("cond", 2 * DT), ("b_ada", N_MOD * DT), ("norm_attn", DT), ("norm_mlp", DT),
                      ("subln", 1), ("lambdas", 4)):
    COLS[_name] = (_n, _width)
    _n += _width
NCOLS = _n

CONST = {}
_n = 0
for _name, _width in (("ident", P), ("ones", P), ("before", P), ("rope1", 2 * ST * (HD // 2)),
                      ("rope2", 2 * ST * (HD // 2)), ("iota_e", NE), ("assign", ST * NK)):
    CONST[_name] = (_n, _width)
    _n += _width
NCONST = _n

DENSE = (("ssm_in", 1, CHUNK), ("ada", 12, CHUNK), ("ssm_glu", 1, WT * NB), ("ssm_out", 1, CHUNK),
         ("w1_0", 8, CHUNK), ("w2_0", 8, CHUNK),
         ("att_in", 4, CHUNK), ("att_idx", 1, DT * 72), ("att_out", 2, CHUNK),
         ("w1_1", 8, CHUNK), ("w2_1", 8, CHUNK),
         ("qa", 1, CHUNK), ("kva", 1, DT * 256), ("qb", 1, CHUNK), ("kb", 1, CHUNK), ("vb", 1, CHUNK),
         ("ga", 1, CHUNK), ("w_oa", 1, WT * NB), ("gb", 1, CHUNK), ("w_ob", 1, WT * NB),
         ("ga1", 1, CHUNK), ("w_oa1", 1, WT * NB), ("gb1", 1, CHUNK), ("w_ob1", 1, WT * NB),
         ("w_out", 2, CHUNK))
FIRST = {}
_n = 0
DENSE_USED = []
for _name, _many, _used in DENSE:
    FIRST[_name] = _n
    DENSE_USED += [_used] * _many
    _n += _many
NDENSE = _n


class Count:

    def __init__(self, sem):
        self.sem, self.n = sem, 0

    def by(self, instruction):
        instruction.then_inc(self.sem, 1)
        self.n += 1
        return self.n

    def then_wait(self, engine, instruction):
        engine.wait_ge(self.sem, self.by(instruction))


def stage(f):
    def run(k, *args):
        lasting, k.stage_sems = k.stage_sems, []
        result = f(k, *args)
        numbers = sorted(s.num for s in k.stage_sems)
        while numbers:
            run_of = 1
            while run_of < len(numbers) and numbers[run_of] == numbers[0] + run_of:
                run_of += 1
            k.nc.gpsimd.sem_clear(range(numbers[0], numbers[0] + run_of))
            numbers = numbers[run_of:]
        for s in k.cleared_sems:
            k.nc.release_semaphore(s)
        k.cleared_sems, k.stage_sems = k.stage_sems, lasting
        return result
    return run


class Kernel:

    def __init__(self, nc, ctx, io):
        self.nc, self.ctx, self.io = nc, ctx, io
        self.cleared_sems = []
        self.stage_sems = []

        def sb(name, width):
            return ctx.enter_context(nc.sbuf_tensor(name, [P, width], F32))

        def sb_both(name, width, parts=1):
            at = (nc.sbuf_base + 31) // 32 * 32
            plain = sb(name, width)
            assert nc.sbuf_base == at + 4 * width
            size = width // parts
            return plain, [nc.alloc_sbuf_tensor_at(f"{name}_rounded_{n}", [P, size], F32R, offset=at + 4 * size * n)
                           for n in range(parts)]

        self.resid = sb("resid", ST * D)[:, :].rearrange("p (t d) -> p t d", t=ST)
        operand, (self.operand_r,) = sb_both("operand", DT * KEYS + 2 * D)
        self.operand = operand[:, :]
        self.turned = operand[:, 0:DT * KEYS].rearrange("p (k s) -> p k s", k=DT)
        self.gate_rows = operand[:, DT * KEYS:]
        self.x_high, self.x_low = (self.operand_r[:, n * DT * S:(n + 1) * DT * S].rearrange("p (k s) -> p k s", k=DT) for n in range(2))
        self.left = self.operand_r[:, 0:4 * D].rearrange("p (b h k s) -> p b h k s", b=2, h=2, k=2)
        self.arena, self.arena_r = sb_both("arena", 9 * CHUNK, 9)
        self.ring = self.arena[:, 0:NSLOT * CHUNK].rearrange("p (n c) -> p n c", n=NSLOT)
        self.work = self.arena[:, (NSLOT + 1) * CHUNK:9 * CHUNK]
        self.small, (self.small_r,) = sb_both("small", 2304)
        self.cols = sb("cols", NCOLS)
        self.const = sb("const", NCONST)
        self.stat = sb("stat", 64)
        self.mod = sb("mod", 2 * N_MOD * DT)
        self.affine = sb("affine", 6 * DT)
        self.u = self.work[:, 16384:18432].rearrange("p (n s) -> p n s", n=WT)
        self.bt_mat = self.work[:, 18432:19456]
        self.c_mat = self.work[:, 19456:20480]
        self.turned_flat = self.turned.rearrange("p k s -> p (k s)")
        self.ssm_cols = sb("ssm_cols", 4 * NJ)
        self.decay, self.cos1, self.sin1, self.silu_c = (self.ssm_cols[:, NJ * i:NJ * (i + 1)] for i in range(4))
        self.head_gains = self.small[:, 2048:2304]
        self.neg_lam = self.stat[:, 63:64]
        self.psum = ctx.enter_context(nc.psum_tensor("banks", [P, 8, NB], F32))
        self.loaded = [self.sem(f"weights_in_slot{i}") for i in range(NSLOT)]

    def sem(self, name):
        self.stage_sems.append(self.nc.alloc_semaphore(name=name))
        return self.stage_sems[-1]

    def col(self, name, i=0, n=None):
        at, width = COLS[name]
        return self.cols[:, at + i:at + (i + n if n else width)]

    def cst(self, name):
        at, width = CONST[name]
        return self.const[:, at:at + width]

    def load_chunk(self, sp, n):
        if n < NDENSE:
            sp.dma_start(self.ring[:, n % NSLOT, 0:DENSE_USED[n]],
                         self.io["dense"][n, :, 0:DENSE_USED[n]]).then_inc(self.loaded[n % NSLOT], 16)

    def replace_chunks(self, sp, first, many, product, step):
        for c in range(many):
            sp.wait_ge(product, step * (c + 1))
            self.load_chunk(sp, first + c + NSLOT)

    def chunk(self, pe, n, width):
        pe.wait_ge(self.loaded[n % NSLOT], 16 * (n // NSLOT + 1))
        return self.ring[:, n % NSLOT, 0:DENSE_USED[n]].rearrange("p (k n) -> p k n", n=width)

    def piece(self, n, m):
        at = slice((m % 2) * PIECE, (m % 2 + 1) * PIECE)
        slot = (n + m // 2) % NSLOT
        return self.ring[:, slot, at], self.arena_r[slot][:, at], self.arena_r[NSLOT][:, at]

    def split_high(self, act, n, m, used, done):
        chunk = n + m // 2
        act.wait_ge(self.loaded[chunk % NSLOT], 16 * (chunk // NSLOT + 1))
        if m >= 2:
            act.wait_ge(used, m - 1)
        raw, low, high = self.piece(n, m)
        self.nc.scalar.activation(high, raw, ACT.Copy).then_inc(done, 1)

    def split_low(self, n, m, done):
        raw, low, high = self.piece(n, m)
        self.nc.vector.tensor_tensor(low, raw, high.bitcast(F32), ALU.subtract).then_inc(done, 1)

    def parts(self, n, m, tiles):
        raw, low, high = self.piece(n, m)
        return [x.rearrange("p (k n) -> p k n", k=tiles) for x in (high, low)]


def exact_product(nc, out, left, right, start, stop):
    nc.tensor.matmul(out, left[0], right[0], start=start, stop=False)
    nc.tensor.matmul(out, left[0], right[1], start=False, stop=False)
    return nc.tensor.matmul(out, left[1], right[0], start=False, stop=stop)


@stage
def load_inputs(k):
    nc, small_in = k.nc, k.sem("small_inputs_in")
    with nc.Block() as block:
        @block.sync
        def _(sp):
            sp.dma_start(k.resid, k.io["x"].rearrange("(t p) d -> p t d", p=P)).then_inc(small_in, 16)
            sp.wait_ge(small_in, 48)
            for n in range(NSLOT):
                k.load_chunk(sp, n)

        @block.scalar
        def _(act):
            act.dma_start(k.const[:, :], k.io["consts"]).then_inc(small_in, 16)
            act.dma_start(k.cols[:, :], k.io["cols"]).then_inc(small_in, 16)
            act.wait_ge(small_in, 48)


@stage
def norm_turned(k, tag, src, tiles, at, scale, shift=None, split=False, ahead=None):
    nc = k.nc
    rows = k.work[:, 16384:16384 + ST * D].rearrange("p (t d) -> p t d", t=ST)
    ssq, mean, root, rstd = (k.stat[:, 4 * i:4 * i + tiles] for i in range(4))
    names = ("squares", "mean", "root", "rstd", "rows", "transposed", "placed_act", "high", "low")
    squares, mean_ready, root_ready, rstd_ready, rows_ready, transposed, placed_act, high, low = (k.sem(f"{tag}_{n}") for n in names)
    n = tiles * P

    with nc.Block() as block:
        @block.scalar
        def _(act):
            for t in range(tiles):
                nc.scalar.activation(rows[:, t, :], src[:, t, :], ACT.Square, accum_out=ssq[:, t:t + 1]).then_inc(squares, 1)
                act.wait_ge(mean_ready, t + 1)
                nc.scalar.activation(root[:, t:t + 1], mean[:, t:t + 1], ACT.Sqrt).then_inc(root_ready, 1)
            if ahead is not None:
                k.split_high(act, ahead, 0, None, high)
            for d in range(DT if split else 0):
                act.wait_ge(transposed, d + 1)
                nc.scalar.activation(k.x_high[:, d, :], k.psum[:, d, :], ACT.Identity,
                                     scale=scale[:, d:d + 1]).then_inc(placed_act, 1)
            for d in range(1, 1 if split else DT, 2):
                act.wait_ge(transposed, d + 1)
                nc.scalar.activation(k.turned[:, d, at:at + n], k.psum[:, d, 0:n], ACT.Identity,
                                     scale=scale[:, d:d + 1],
                                     bias=shift[:, d:d + 1] if shift is not None else 0.0)

        @block.vector
        def _(dve):
            V = nc.vector
            for t in range(tiles):
                one = slice(t, t + 1)
                dve.wait_ge(squares, t + 1)
                V.tensor_scalar(mean[:, one], ssq[:, one], 1.0 / D, EPS, ALU.mult, ALU.add).then_inc(mean_ready, 1)
                dve.wait_ge(root_ready, t + 1)
                V.reciprocal(rstd[:, one], root[:, one]).then_inc(rstd_ready, 1)
                dve.wait_ge(rstd_ready, t + 1)
                V.tensor_scalar(rows[:, t, :], src[:, t, :], rstd[:, one], None, ALU.mult).then_inc(rows_ready, 1)
            if ahead is not None:
                dve.wait_ge(high, 1)
                k.split_low(ahead, 0, low)
            for d in range(DT if split else 0):
                dve.wait_ge(placed_act, d + 1)
                V.scalar_tensor_tensor(out=k.x_low[:, d, :], in0=k.psum[:, d, :], scalar=scale[:, d:d + 1],
                                       in1=k.x_high[:, d, :].bitcast(F32), op0=ALU.mult, op1=ALU.subtract)
            for d in range(0, 0 if split else DT, 2):
                dve.wait_ge(transposed, d + 1)
                if shift is None:
                    V.tensor_scalar(k.turned[:, d, at:at + n], k.psum[:, d, 0:n], scale[:, d:d + 1], None, ALU.mult)
                else:
                    V.tensor_scalar(k.turned[:, d, at:at + n], k.psum[:, d, 0:n],
                                    scale[:, d:d + 1], shift[:, d:d + 1], ALU.mult, ALU.add)

        @block.tensor
        def _(pe):
            for t in range(tiles):
                pe.wait_ge(rows_ready, t + 1)
                for d in range(DT):
                    i = nc.tensor.transpose(k.psum[:, d, t * P:(t + 1) * P], rows[:, t, d * P:(d + 1) * P], k.cst("ident"))
                    if t == tiles - 1:
                        i.then_inc(transposed, 1)


@stage
def project_residual(k, tag, chunk0, chunks, lhs, row, normed):
    nc = k.nc
    row_tile = k.small[:, 0:D] if normed else row
    scaled_rows = k.work[:, 16384:16384 + 2 * D].rearrange("p (b d) -> p b d", b=2)
    junk = k.small[:, D:2 * D]
    ssq, mean, root, rstd = (k.stat[:, 4 * i:4 * i + 4] for i in range(4))
    names = ("row_in", "high", "low", "used", "product", "squares", "mean", "root", "rstd", "scaled", "added")
    row_in, high, low, used, product, squares, mean_ready, root_ready, rstd_ready, scaled, added = (k.sem(f"{tag}_{n}") for n in names)
    pieces = 2 * chunks
    banks = lambda t: k.psum[:, 2 * t:2 * t + 2, :].rearrange("p b s -> p (b s)")

    with nc.Block() as block:
        @block.sync
        def _(sp):
            if normed:
                sp.dma_start(row_tile, row.partition_broadcast(P)).then_inc(row_in, 16)
            for c in range(chunks):
                sp.wait_ge(used, 2 * (c + 1))
                k.load_chunk(sp, chunk0 + c + NSLOT)

        @block.tensor
        def _(pe):
            for m in range(pieces):
                w = k.parts(chunk0, m, 2)
                pe.wait_ge(low, 3 * (m + 1))
                for t in range(ST):
                    for j in range(2):
                        left = [k.left[:, m % 2, h, j, t * P:(t + 1) * P] for h in range(2)]
                        for c in range(2):
                            i = exact_product(nc, k.psum[:, 2 * t + c, :], left, [x[:, j, c * NB:(c + 1) * NB] for x in w],
                                              start=(m == 0 and j == 0), stop=(m == pieces - 1 and j == 1))
                    if m == pieces - 1:
                        i.then_inc(product, 1)
                if m < pieces - 1:
                    i.then_inc(used, 1)
                else:
                    pe.wait_ge(product, ST)
                    pe.sem_inc(used, 1)

        @block.scalar
        def _(act):
            for m in range(pieces):
                k.split_high(act, chunk0, m, used, high)
                for j in range(2):
                    nc.scalar.activation(k.left[:, m % 2, 0, j, :], lhs(2 * m + j), ACT.Copy).then_inc(high, 1)
            if normed:
                for t in range(ST):
                    act.wait_ge(product, t + 1)
                    if t:
                        act.wait_ge(squares, t)
                    nc.scalar.activation(junk, banks(t), ACT.Square, accum_out=ssq[:, t:t + 1]).then_inc(squares, 1)
                    act.wait_ge(mean_ready, t + 1)
                    nc.scalar.activation(root[:, t:t + 1], mean[:, t:t + 1], ACT.Sqrt).then_inc(root_ready, 1)

        @block.vector
        def _(dve):
            V = nc.vector
            for m in range(pieces):
                dve.wait_ge(high, 3 * m + 1)
                k.split_low(chunk0, m, low)
                for j in range(2):
                    dve.wait_ge(high, 3 * m + j + 2)
                    V.tensor_tensor(k.left[:, m % 2, 1, j, :], lhs(2 * m + j), k.left[:, m % 2, 0, j, :].bitcast(F32),
                                    ALU.subtract).then_inc(low, 1)
            if normed:
                dve.wait_ge(row_in, 16)
            for t in range(ST):
                one = lambda x: x[:, t:t + 1]
                if normed:
                    dve.wait_ge(squares, t + 1)
                    V.tensor_scalar(one(mean), one(ssq), 1.0 / D, EPS, ALU.mult, ALU.add).then_inc(mean_ready, 1)
                else:
                    dve.wait_ge(product, t + 1)
                if t >= 2:
                    dve.wait_ge(added, t - 1)
                V.tensor_tensor(scaled_rows[:, t % 2], banks(t), row_tile, ALU.mult).then_inc(scaled, 1)
                if normed:
                    dve.wait_ge(root_ready, t + 1)
                    V.reciprocal(one(rstd), one(root)).then_inc(rstd_ready, 1)
                    dve.wait_ge(rstd_ready, t + 1)
                dve.wait_ge(scaled, t + 1)
                if normed:
                    i = V.scalar_tensor_tensor(out=k.resid[:, t, :], in0=scaled_rows[:, t % 2], scalar=one(rstd),
                                               in1=k.resid[:, t, :], op0=ALU.mult, op1=ALU.add)
                else:
                    i = V.tensor_tensor(k.resid[:, t, :], scaled_rows[:, t % 2], k.resid[:, t, :], ALU.add)
                i.then_inc(added, 1)


@stage
def mlp_hidden(k, tag, chunk0):
    nc = k.nc
    hidden = k.work[:, 0:32 * NB].rearrange("p (f s) -> p f s", f=32)
    relu = k.small[:, 0:2 * NB].rearrange("p (b s) -> p b s", b=2)
    names = ("high", "low", "used", "product", "clipped", "squared")
    high, low, used, product, clipped, squared = (k.sem(f"{tag}_{n}") for n in names)
    PIECES_W1 = 16

    with nc.Block() as block:
        @block.sync
        def _(sp):
            for c in range(8):
                sp.wait_ge(product, 4 * (c + 1))
                k.load_chunk(sp, chunk0 + c + NSLOT)

        @block.tensor
        def _(pe):
            for m in range(PIECES_W1):
                c = m // 2
                w = k.parts(chunk0, m, 4)
                if m:
                    pe.wait_ge(low, m)
                for f in range(4):
                    n = 4 * c + f
                    if m % 2 == 0 and n >= 8:
                        pe.wait_ge(clipped, n - 7)
                    for j in range(4):
                        d = 4 * (m % 2) + j
                        i = exact_product(nc, k.psum[:, n % 8, :], [x[:, j, f * P:(f + 1) * P] for x in w],
                                          (k.x_high[:, d, :], k.x_low[:, d, :]), start=(d == 0), stop=(d == DT - 1))
                    if m % 2:
                        i.then_inc(product, 1)
                if m % 2 == 0:
                    i.then_inc(used, 1)
                else:
                    pe.wait_ge(product, 4 * (c + 1))
                    pe.sem_inc(used, 1)

        @block.scalar
        def _(act):
            for m in range(PIECES_W1):
                if m + 1 < PIECES_W1:
                    k.split_high(act, chunk0, m + 1, used, high)
                if m % 2:
                    for n in range(2 * m - 2, 2 * m + 2):
                        act.wait_ge(product, n + 1)
                        if n >= 2:
                            act.wait_ge(squared, n - 1)
                        nc.scalar.activation(relu[:, n % 2, :], k.psum[:, n % 8, :], ACT.Relu).then_inc(clipped, 1)

        @block.vector
        def _(dve):
            for m in range(1, PIECES_W1):
                dve.wait_ge(high, m)
                k.split_low(chunk0, m, low)

        @block.gpsimd
        def _(pool):
            for n in range(32):
                pool.wait_ge(clipped, n + 1)
                nc.gpsimd.tensor_tensor(hidden[:, n, :], relu[:, n % 2, :], relu[:, n % 2, :],
                                        ALU.mult).then_inc(squared, 1)
    return lambda ki: hidden[:, ki, :]


@stage
def ssm_parameters(k):
    nc = k.nc
    names = ("dt", "lr_dt", "angle", "turns", "whole", "rest", "sin_in", "cos_in", "re", "im", "re1", "a", "b", "den",
             "inv_den", "fr", "fi", "c")
    v = {n: k.work[:, NJ * i:NJ * (i + 1)] for i, n in enumerate(names)}
    raw = k.work[:, 1024:3072].rearrange("p (b j c) -> p b j c", b=4, j=NJ)
    prod = k.work[:, 3072:5120].rearrange("p (b j c) -> p b j c", b=4, j=NJ)
    bbar = k.work[:, 5120:6144].rearrange("p (b j c) -> p b j c", b=2, j=NJ)
    lr, li = k.col("lam_re"), k.col("lam_im")
    mag, cos, sin = k.decay, k.cos1, k.sin1
    raw_in, act_done, dve_done = k.sem("ssm_raw_in"), k.sem("ssm_par_act"), k.sem("ssm_par_dve")
    bbar_ready, bt_turned, silu_half = k.sem("ssm_bbar"), k.sem("ssm_bt_turned"), k.sem("silu_half")

    u_product, u_copied = k.sem("ssm_u_product"), k.sem("ssm_u_copied")

    with nc.Block() as block:
        @block.sync
        def _(sp):
            sp.dma_start(raw, k.io["ssm_bc"].rearrange("p (b j c) -> p b j c", b=4, j=NJ)).then_inc(raw_in, 16)
            k.replace_chunks(sp, FIRST["ssm_in"], 1, u_product, WT)

        @block.scalar
        def _(act):
            nc.scalar.activation(v["dt"], k.col("log_dt"), ACT.Exp).then_inc(act_done, 1)
            act.wait_ge(dve_done, 1)
            nc.scalar.activation(mag, v["lr_dt"], ACT.Exp).then_inc(act_done, 1)
            act.wait_ge(dve_done, 17)
            nc.scalar.activation(sin, v["sin_in"], ACT.Sin).then_inc(act_done, 1)
            nc.scalar.activation(cos, v["cos_in"], ACT.Sin).then_inc(act_done, 1)
            nc.scalar.activation(k.silu_c, k.col("cond"), ACT.Sigmoid).then_inc(silu_half, 1)
            for n in range(WT):
                act.wait_ge(u_product, n + 1)
                nc.scalar.activation(k.u[:, n, :], k.psum[:, n, :], ACT.Copy).then_inc(u_copied, 1)

        @block.vector
        def _(dve):
            own = Count(dve_done)
            V = nc.vector

            def step(i):
                own.then_wait(dve, i)

            dve.wait_ge(act_done, 1)
            step(V.tensor_tensor(v["lr_dt"], lr, v["dt"], ALU.mult))
            step(V.tensor_tensor(v["angle"], li, v["dt"], ALU.mult))
            for out, quarter in (("sin_in", 0.0), ("cos_in", 0.25)):
                step(V.tensor_scalar(v["turns"], v["angle"], 1.0 / (2 * np.pi), quarter, ALU.mult, ALU.add))
                step(V.tensor_scalar(v["whole"], v["turns"], ROUND, None, ALU.add))
                step(V.tensor_scalar(v["whole"], v["whole"], -ROUND, None, ALU.add))
                step(V.scalar_tensor_tensor(out=v["rest"], in0=v["whole"], scalar=-TWO_PI_HI, in1=v["angle"],
                                            op0=ALU.mult, op1=ALU.add))
                step(V.scalar_tensor_tensor(out=v["rest"], in0=v["whole"], scalar=-TWO_PI_MID, in1=v["rest"],
                                            op0=ALU.mult, op1=ALU.add))
                step(V.scalar_tensor_tensor(out=v[out], in0=v["whole"], scalar=-TWO_PI_LO, in1=v["rest"],
                                            op0=ALU.mult, op1=ALU.add))
                if quarter:
                    step(V.tensor_scalar(v[out], v[out], float(np.pi / 2), None, ALU.add))
                step(V.tensor_scalar(v[out], v[out], PI_F, -PI_F, ALU.min, ALU.max))
            assert own.n == 17
            step(V.tensor_tensor(v["a"], lr, lr, ALU.mult))
            step(V.tensor_tensor(v["b"], li, li, ALU.mult))
            step(V.tensor_tensor(v["den"], v["a"], v["b"], ALU.add))
            step(V.reciprocal(v["inv_den"], v["den"]))
            dve.wait_ge(act_done, 4)
            step(V.tensor_tensor(v["re"], mag, cos, ALU.mult))
            step(V.tensor_tensor(v["im"], mag, sin, ALU.mult))
            step(V.tensor_scalar(v["re1"], v["re"], -1.0, None, ALU.add))
            for out, x, y, op in (("fr", "re1", "im", ALU.add), ("fi", "im", "re1", ALU.subtract)):
                step(V.tensor_tensor(v["a"], v[x], lr, ALU.mult))
                step(V.tensor_tensor(v["b"], v[y], li, ALU.mult))
                step(V.tensor_tensor(v["c"], v["a"], v["b"], op))
                step(V.tensor_tensor(v[out], v["c"], v["inv_den"], ALU.mult))
            dve.wait_ge(raw_in, 16)
            fr = v["fr"].unsqueeze(2).broadcast_to([P, NJ, 32])
            fi = v["fi"].unsqueeze(2).broadcast_to([P, NJ, 32])
            V.tensor_tensor(prod[:, 0], raw[:, 0], fr, ALU.mult)
            V.tensor_tensor(prod[:, 1], raw[:, 1], fi, ALU.mult)
            V.tensor_tensor(prod[:, 2], raw[:, 1], fr, ALU.mult)
            step(V.tensor_tensor(prod[:, 3], raw[:, 0], fi, ALU.mult))
            V.tensor_tensor(bbar[:, 0], prod[:, 0], prod[:, 1], ALU.subtract).then_inc(bbar_ready, 1)
            V.tensor_tensor(bbar[:, 1], prod[:, 2], prod[:, 3], ALU.add).then_inc(bbar_ready, 1)
            V.tensor_copy(k.c_mat[:, 0:512], raw[:, 2].rearrange("p j c -> p (j c)"))
            V.tensor_scalar(k.c_mat[:, 512:1024], raw[:, 3].rearrange("p j c -> p (j c)"), -1.0, None, ALU.mult)
            dve.wait_ge(silu_half, 1)
            V.tensor_tensor(k.silu_c, k.silu_c, k.col("cond"), ALU.mult)
            for part in range(2):
                dve.wait_ge(bt_turned, part + 1)
                V.tensor_copy(k.bt_mat[:, part * 512:(part + 1) * 512], k.psum[:, 4 + part, :])

        @block.tensor
        def _(pe):
            w = k.chunk(pe, FIRST["ssm_in"], NB)
            for n in range(WT):
                for d in range(DT):
                    i = nc.tensor.matmul(k.psum[:, n, :], w[:, d, n * P:(n + 1) * P], k.turned[:, d, 0:S],
                                         start=(d == 0), stop=(d == DT - 1))
                i.then_inc(u_product, 1)
            for part in range(2):
                pe.wait_ge(bbar_ready, part + 1)
                flat = bbar[:, part].rearrange("p j c -> p (j c)")
                for i in range(WT):
                    t = nc.tensor.transpose(k.psum[:, 4 + part, i * P:(i + 1) * P], flat[:, i * P:(i + 1) * P], k.cst("ident"))
                t.then_inc(bt_turned, 1)


@stage
def ssm_tables(k):
    nc = k.nc
    cos = k.work[:, 0:NJ * S].rearrange("p (j s) -> p j s", j=NJ)
    sin = k.work[:, NJ * S:2 * NJ * S].rearrange("p (j s) -> p j s", j=NJ)
    tmp = k.turned_flat
    step_c = [k.small[:, 32 * i:32 * i + NJ] for i in range(10)]
    step_s = [k.small[:, 32 * i + NJ:32 * i + 32] for i in range(10)]
    sq = [k.small[:, 320 + NJ * i:320 + NJ * (i + 1)] for i in range(3)]
    chain, ada_done, ada_copied, ada_turned = (k.sem(n) for n in ("ssm_tables", "ada_done", "ada_copied", "ada_turned"))
    mod_rows = k.small[0:2, D:2 * D].rearrange("p (b s) -> p b s", b=2)
    ada0 = FIRST["ada"]
    mod_psum = k.psum[:, 2, 0:2 * N_MOD * DT]
    with nc.Block() as block:
        @block.sync
        def _(sp):
            k.replace_chunks(sp, ada0, 12, ada_done, 1)

        @block.tensor
        def _(pe):
            for j in range(13):
                if j < 12:
                    w = k.chunk(pe, ada0 + j, NB)
                    if j >= 2:
                        pe.wait_ge(ada_copied, j - 1)
                    for d in range(DT):
                        m = nc.tensor.matmul(k.psum[0:2, j % 2, :], k.silu_c[:, 2 * d:2 * d + 2], w[:, d, :],
                                             start=(d == 0), stop=(d == DT - 1))
                    m.then_inc(ada_done, 1)
                if j >= 1:
                    pe.wait_ge(ada_copied, j)
                    for n in range(4):
                        col = 2 * (4 * (j - 1) + n)
                        m = nc.tensor.transpose(mod_psum[:, col:col + 2], mod_rows[:, (j - 1) % 2, n * P:(n + 1) * P],
                                                k.cst("ident")[0:2, 0:2])
                    m.then_inc(ada_turned, 1)

        @block.scalar
        def _(act):
            for j in range(12):
                act.wait_ge(ada_done, j + 1)
                if j >= 2:
                    act.wait_ge(ada_turned, j - 1)
                nc.scalar.activation(mod_rows[:, j % 2, :], k.psum[0:2, j % 2, :], ACT.Copy).then_inc(ada_copied, 1)

        @block.vector
        def _(dve):
            own = Count(chain)
            V = nc.vector
            V.memset(cos[:, :, 0:1], 1.0)
            V.memset(sin[:, :, 0:1], 0.0)
            V.tensor_copy(step_c[0], k.cos1)
            own.then_wait(dve, V.tensor_copy(step_s[0], k.sin1))
            s, level = 1, 0
            while s < S:
                c, d = step_c[level], step_s[level]
                wide = [P, NJ, s]
                cb, db = c.unsqueeze(2).broadcast_to(wide), d.unsqueeze(2).broadcast_to(wide)
                t0 = tmp[:, 0:NJ * s].rearrange("p (j s) -> p j s", j=NJ)
                V.tensor_tensor(cos[:, :, s:2 * s], cos[:, :, 0:s], cb, ALU.mult)
                V.tensor_tensor(sin[:, :, s:2 * s], sin[:, :, 0:s], cb, ALU.mult)
                own.then_wait(dve, V.tensor_tensor(t0, sin[:, :, 0:s], db, ALU.mult))
                own.then_wait(dve, V.tensor_tensor(cos[:, :, s:2 * s], cos[:, :, s:2 * s], t0, ALU.subtract))
                own.then_wait(dve, V.tensor_tensor(t0, cos[:, :, 0:s], db, ALU.mult))
                own.then_wait(dve, V.tensor_tensor(sin[:, :, s:2 * s], sin[:, :, s:2 * s], t0, ALU.add))
                V.tensor_tensor(sq[0], c, c, ALU.mult)
                V.tensor_tensor(sq[1], d, d, ALU.mult)
                own.then_wait(dve, V.tensor_tensor(sq[2], c, d, ALU.mult))
                V.tensor_tensor(step_c[level + 1], sq[0], sq[1], ALU.subtract)
                own.then_wait(dve, V.tensor_scalar(step_s[level + 1], sq[2], 2.0, None, ALU.mult))
                s, level = 2 * s, level + 1
            dve.wait_ge(ada_turned, 12)
            nc.vector.tensor_tensor(k.mod[:, :].rearrange("p (c w) -> p c w", w=2),
                                    mod_psum.rearrange("p (c w) -> p c w", w=2),
                                    k.col("b_ada").unsqueeze(2).broadcast_to([P, N_MOD * DT, 2]), ALU.add)


@stage
def ssm_scan(k):
    nc = k.nc
    cos = k.work[:, 0:NJ * S].rearrange("p (j s) -> p j s", j=NJ)
    sin = k.work[:, NJ * S:2 * NJ * S].rearrange("p (j s) -> p j s", j=NJ)
    buf = k.operand.rearrange("p (b s) -> p b s", s=S)
    back = k.small[:, 0:4 * S].rearrange("p (b s) -> p b s", s=S)
    bu, bu_copied = k.sem("ssm_bu"), k.sem("ssm_bu_copied")
    in_dve, in_pool = k.sem("ssm_in_dve"), k.sem("ssm_in_pool")
    zin_re, zin_im, z_done = k.sem("ssm_zin_re"), k.sem("ssm_zin_im"), k.sem("ssm_z_done")
    back_dve, back_pool, y_done = k.sem("ssm_back_dve"), k.sem("ssm_back_pool"), k.sem("ssm_y_done")

    def input_bufs(j):
        return buf[:, 2 * (j % 2), :], buf[:, 2 * (j % 2) + 1, :]

    def bufs(j):
        return [buf[:, 4 + 4 * (j % 3) + i, :] for i in range(4)]

    with nc.Block() as block:
        @block.tensor
        def _(pe):
            for s in range(NJ + 3):
                if s < NJ:
                    i, q = s // 4, 32 * (s % 4)
                    if s >= 2:
                        pe.wait_ge(bu_copied, 2 * (s - 1))
                    for part in range(2):
                        m = nc.tensor.matmul(k.psum[:, 2 * (s % 2) + part, :],
                                             k.bt_mat[q:q + 32, part * 512 + i * P:part * 512 + (i + 1) * P],
                                             k.u[q:q + 32, i, :], start=True, stop=True)
                    m.then_inc(bu, 1)
                j = s - 3
                if j >= 0:
                    i, q = j // 4, 32 * (j % 4)
                    pe.wait_ge(back_dve, j + 1)
                    pe.wait_ge(back_pool, j + 1)
                    for n, part in enumerate((0, 0, 1, 1)):
                        m = nc.tensor.matmul(k.psum[q:q + 32, 4 + i, :], k.c_mat[:, part * 512 + 32 * j:part * 512 + 32 * j + 32],
                                             back[:, n, :], start=(n == 0), stop=(n == 3), tile_position=(0, q))
                    m.then_inc(y_done, 1)

        @block.scalar
        def _(act):
            for j in range(NJ):
                act.wait_ge(bu, j + 1)
                if j >= 2:
                    act.wait_ge(in_dve, j - 1)
                    act.wait_ge(in_pool, 2 * (j - 1))
                for part, b in enumerate(input_bufs(j)):
                    nc.scalar.activation(b, k.psum[:, 2 * (j % 2) + part, :], ACT.Copy).then_inc(bu_copied, 1)

        @block.gpsimd
        def _(pool):
            for s in range(NJ + 2):
                if s < NJ:
                    re, im = input_bufs(s)
                    _, _, z_in, spare = bufs(s)
                    pool.wait_ge(bu_copied, 2 * s + 2)
                    if s >= 3:
                        pool.wait_ge(back_dve, s - 2)
                        pool.wait_ge(back_pool, s - 2)
                    nc.gpsimd.tensor_tensor(z_in, cos[:, s, :], im, ALU.mult).then_inc(in_pool, 1)
                    nc.gpsimd.tensor_tensor(spare, sin[:, s, :], re, ALU.mult).then_inc(in_pool, 1)
                    pool.wait_ge(in_pool, 2 * s + 2)
                    nc.gpsimd.tensor_tensor(z_in, z_in, spare, ALU.subtract).then_inc(zin_im, 1)
                j = s - 2
                if j >= 0:
                    pool.wait_ge(z_done, 2 * j + 2)
                    if j >= 1:
                        pool.wait_ge(y_done, j)
                    nc.gpsimd.tensor_tensor(back[:, 3, :], cos[:, j, :], bufs(j)[3], ALU.mult).then_inc(back_pool, 1)

        @block.vector
        def _(dve):
            V = nc.vector
            for s in range(NJ + 2):
                if s < NJ:
                    re, im = input_bufs(s)
                    z_in, spare, _, _ = bufs(s)
                    dve.wait_ge(bu_copied, 2 * s + 2)
                    if s >= 3:
                        dve.wait_ge(back_dve, s - 2)
                    V.tensor_tensor(z_in, cos[:, s, :], re, ALU.mult)
                    V.tensor_tensor(spare, sin[:, s, :], im, ALU.mult).then_inc(in_dve, 1)
                    dve.wait_ge(in_dve, s + 1)
                    V.tensor_tensor(z_in, z_in, spare, ALU.add).then_inc(zin_re, 1)
                j = s - 1
                if 0 <= j < NJ:
                    a = k.decay[:, j:j + 1].broadcast_to([P, S])
                    re_in, re_out, im_in, im_out = bufs(j)
                    dve.wait_ge(zin_re, j + 1)
                    V.tensor_tensor_scan(re_out, a, re_in, 0.0, ALU.mult, ALU.add).then_inc(z_done, 1)
                    dve.wait_ge(zin_im, j + 1)
                    V.tensor_tensor_scan(im_out, a, im_in, 0.0, ALU.mult, ALU.add).then_inc(z_done, 1)
                j = s - 2
                if j >= 0:
                    _, re_out, _, im_out = bufs(j)
                    dve.wait_ge(z_done, 2 * j + 2)
                    if j >= 1:
                        dve.wait_ge(y_done, j)
                    V.tensor_tensor(back[:, 0, :], cos[:, j, :], re_out, ALU.mult)
                    V.tensor_tensor(back[:, 2, :], sin[:, j, :], re_out, ALU.mult)
                    V.scalar_tensor_tensor(out=back[:, 1, :], in0=im_out, scalar=-1.0, in1=sin[:, j, :],
                                           op0=ALU.mult, op1=ALU.mult).then_inc(back_dve, 1)


@stage
def ssm_gate(k):
    nc = k.nc
    y, z, gate, gated = (k.work[:, 2048 * i:2048 * (i + 1)].rearrange("p (n s) -> p n s", n=WT) for i in range(4))
    summed, gelu, product, opened = (k.sem(f"ssm_{n}") for n in ("summed", "gelu", "glu_product", "glu_opened"))
    g0 = FIRST["ssm_glu"]
    with nc.Block() as block:
        @block.vector
        def _(dve):
            for n in range(WT):
                nc.vector.scalar_tensor_tensor(out=y[:, n, :], in0=k.u[:, n, :], scalar=k.col("ssm_d", n, 1),
                                               in1=k.psum[:, 4 + n, :], op0=ALU.mult, op1=ALU.add).then_inc(summed, 1)
            for n in range(WT):
                dve.wait_ge(opened, n + 1)
                nc.vector.tensor_tensor(gated[:, n, :], z[:, n, :], gate[:, n, :], ALU.mult)

        @block.scalar
        def _(act):
            for n in range(WT):
                act.wait_ge(summed, n + 1)
                nc.scalar.activation(z[:, n, :], y[:, n, :], ACT.Gelu_apprx_tanh).then_inc(gelu, 1)
            for n in range(WT):
                act.wait_ge(product, n + 1)
                nc.scalar.activation(gate[:, n, :], k.psum[:, n, :], ACT.Sigmoid).then_inc(opened, 1)

        @block.tensor
        def _(pe):
            w = k.chunk(pe, g0, NB)
            pe.wait_ge(gelu, WT)
            for n in range(WT):
                for c in range(WT):
                    i = nc.tensor.matmul(k.psum[:, n, :], w[:, c, n * P:(n + 1) * P], z[:, c, :],
                                         start=(c == 0), stop=(c == WT - 1))
                i.then_inc(product, 1)

        @block.sync
        def _(sp):
            k.replace_chunks(sp, g0, 1, product, WT)
    return lambda ki: gated[:, ki, :]


NEG = -1e30
TAKEN = -3e38
HUGE = 3e38


def attention_layout(k):
    w = k.work
    a = {}
    a["q"] = w[:, 0:4096].rearrange("p (f s) -> p f s", f=8)
    a["k"] = w[:, 4096:6144].rearrange("p (f s) -> p f s", f=NKV)
    a["qi"] = w[:, 6144:8192].rearrange("p (f s) -> p f s", f=4)
    a["ki"] = w[:, 8192:8704].rearrange("p (f s) -> p f s", f=1)
    a["v"] = w[:, 8704:9728].rearrange("p (t c) -> p t c", t=ST)
    a["bias"] = w[:, 9728:11776].rearrange("p (t s) -> p t s", t=ST)
    a["out"] = w[:, 11776:15872].rearrange("p (f s) -> p f s", f=8)
    a["wi"] = w[:, 15872:15904].rearrange("p (t h) -> p t h", t=ST)
    a["staged"] = w[:, 16384:17408].rearrange("p (b c) -> p b c", b=2)
    a["m1"], a["m2"], a["kr"] = w[:, 17408:17920], w[:, 17920:18432], w[:, 18432:18688]
    return a


@stage
def attention_project(k, a):
    nc = k.nc
    first = FIRST["att_in"]
    rope = k.cst("rope1").rearrange("p (f t c) -> p f t c", f=2, t=ST)
    units = [(c, t) for c in range(5) for t in range(ST)]
    tiles = {0: 4, 1: 4, 2: NKV, 3: 4, 4: 1}
    place = {0: ("q", 0), 1: ("q", 4), 2: ("k", 0), 3: ("qi", 0), 4: ("ki", 0)}
    names = ("high", "low", "used", "product", "staged", "turned", "placed", "rope")
    high, low, used, product, staged, turned, placed, chain = (k.sem(f"att_{n}") for n in names)
    M = 9
    width = lambda m: NB if m < 8 else 72

    def piece(m):
        slot, at = (first + m // 2) % NSLOT, slice((m % 2) * PIECE, (m % 2 + 1) * PIECE) if m < 8 else slice(0, DT * 72)
        return k.ring[:, slot, at], k.arena_r[slot][:, at], k.arena_r[NSLOT][:, (m % 2) * PIECE:(m % 2) * PIECE + at.stop - at.start]

    with nc.Block() as block:
        @block.sync
        def _(sp):
            for c in range(5):
                sp.wait_ge(used, min(2 * (c + 1), M))
                k.load_chunk(sp, first + c + NSLOT)

        @block.tensor
        def _(pe):
            def turn(n):
                c, t = units[n]
                pe.wait_ge(staged, n + 1)
                if n >= 2:
                    pe.wait_ge(placed, n - 1)
                for f in range(tiles[c]):
                    i = nc.tensor.transpose(k.psum[:, 4 + n % 2, f * P:(f + 1) * P],
                                            a["staged"][:, n % 2, f * P:(f + 1) * P], k.cst("ident"))
                i.then_inc(turned, 1)

            steps = [(m, t) for m in range(M) for t in range(ST)]
            ready = {}
            for g, (m, t) in enumerate(steps):
                n = ST * (m // 2) + t
                depth = 4 if m < 8 else DT
                w = [x.rearrange("p (k n) -> p k n", n=width(m)) for x in piece(m)[:0:-1]]
                if t == 0 and m:
                    pe.wait_ge(low, m)
                if m % 2 == 0 and n >= 4:
                    pe.wait_ge(staged, n - 3)
                whole = m % 2 == 1 or m == 8
                for j in range(depth):
                    d = 4 * (m % 2) + j
                    left = [x[:, d, t * P:(t + 1) * P] for x in (k.x_high, k.x_low)]
                    i = exact_product(nc, k.psum[:, t, 0:width(m)], left, [x[:, j, :] for x in w],
                                      start=(d == 0), stop=(d == DT - 1))
                if whole:
                    i.then_inc(product, 1)
                    ready[g + 3] = n
                if t == ST - 1:
                    if whole:
                        pe.wait_ge(product, n + 1)
                        pe.sem_inc(used, 1)
                    else:
                        i.then_inc(used, 1)
                if g in ready:
                    turn(ready.pop(g))
            for g in sorted(ready):
                turn(ready[g])

        @block.scalar
        def _(act):
            def split_high(m):
                chunk = first + m // 2
                act.wait_ge(k.loaded[chunk % NSLOT], 16 * (chunk // NSLOT + 1))
                if m >= 2:
                    act.wait_ge(used, m - 1)
                raw, _, w_high = piece(m)
                nc.scalar.activation(w_high, raw, ACT.Copy).then_inc(high, 1)

            split_high(1)
            for n, (c, t) in enumerate(units):
                m = 2 * c + 2 + t
                if t < 2 and m < M:
                    split_high(m)
                name, f0 = place[c]
                act.wait_ge(turned, n + 1)
                m = tiles[c]
                nc.scalar.activation(a[name][:, f0:f0 + m, t * P:(t + 1) * P],
                                     k.psum[:, 4 + n % 2, 0:m * P].rearrange("p (f s) -> p f s", f=m), ACT.Copy,
                                     scale=HD ** -0.5 if name == "q" else 1.0).then_inc(placed, 1)

        @block.vector
        def _(dve):
            own, V = Count(chain), nc.vector

            def rotate(out, x, heads, t):
                half = HD // 2
                xs = x.rearrange("p (h c) -> p h c", c=HD)
                m1 = a["m1"][:, 0:heads * HD].rearrange("p (h c) -> p h c", c=HD)
                m2 = a["m2"][:, 0:heads * HD].rearrange("p (h c) -> p h c", c=HD)
                both = lambda f: rope[:, f, t, :].unsqueeze(1)
                wide = [P, 2 * heads, half]
                V.tensor_tensor(a["m1"][:, 0:heads * HD].rearrange("p (h c) -> p h c", c=half),
                                x.rearrange("p (h c) -> p h c", c=half), both(0).broadcast_to(wide), ALU.mult)
                sin = both(1).broadcast_to([P, heads, half])
                V.tensor_tensor(m2[:, :, 0:half], xs[:, :, half:HD], sin, ALU.mult)
                own.then_wait(dve, V.tensor_tensor(m2[:, :, half:HD], xs[:, :, 0:half], sin, ALU.mult))
                os = out.rearrange("p (h c) -> p h c", c=HD)
                V.tensor_tensor(os[:, :, 0:half], m1[:, :, 0:half], m2[:, :, 0:half], ALU.subtract)
                return V.tensor_tensor(os[:, :, half:HD], m1[:, :, half:HD], m2[:, :, half:HD], ALU.add)

            def split_low(m):
                raw, w_low, w_high = piece(m)
                dve.wait_ge(high, m)
                V.tensor_tensor(w_low, raw, w_high.bitcast(F32), ALU.subtract).then_inc(low, 1)

            split_low(1)
            for n, (c, t) in enumerate(units):
                if t == 0 and 2 * c + 2 < M:
                    split_low(2 * c + 2)
                ps, out = k.psum[:, n % 4, :], a["staged"][:, n % 2, :]
                dve.wait_ge(product, n + 1)
                if n:
                    dve.wait_ge(staged, n)
                if n >= 2:
                    dve.wait_ge(turned, n - 1)
                if c in (0, 1, 3):
                    i = rotate(out, ps, NB // HD, t)
                else:
                    heads = NKV if c == 2 else 1
                    own.then_wait(dve, rotate(a["kr"][:, 0:heads * HD], ps[:, 0:heads * HD], heads, t))
                    if c == 2:
                        V.tensor_copy(a["v"][:, t, :], ps[:, 256:512])
                    else:
                        V.tensor_scalar(a["wi"][:, t, :], ps[:, HD:HD + IH], IH ** -0.5 * HD ** -0.5, None, ALU.mult)
                    i = V.tensor_copy(out[:, 0:heads * 2 * HD].rearrange("p (h b c) -> p h b c", b=2, c=HD),
                                      a["kr"][:, 0:heads * HD].rearrange("p (h c) -> p h c", c=HD).unsqueeze(2)
                                      .broadcast_to([P, heads, 2, HD]))
                i.then_inc(staged, 1)
                if t == ST - 1 and 2 * c + 3 < M:
                    split_low(2 * c + 3)


@stage
def attention_select(k, a):
    nc = k.nc
    units = [(i, h) for i in range(1, ST) for h in range(IH)]
    relu = k.turned_flat[:, 0:2048].rearrange("p (b s) -> p b s", b=4)
    score = k.turned_flat[:, 2048:2048 + 3 * S].rearrange("p (t s) -> p t s", t=3)
    best = k.small[:, 0:24].rearrange("p (t c) -> p t c", t=3)
    product, clipped, summed, causal, chain = (k.sem(f"idx_{n}") for n in ("product", "clipped", "summed", "causal", "chain"))

    with nc.Block() as block:
        @block.tensor
        def _(pe):
            for n, (i, h) in enumerate(units):
                r, keys = HD * (h % 2), (i + 1) * P
                if n >= 4:
                    pe.wait_ge(clipped, n - 3)
                nc.tensor.matmul(k.psum[:, n % 4, 0:keys], a["qi"][r:r + HD, h // 2, i * P:(i + 1) * P],
                                 a["ki"][r:r + HD, 0, 0:keys], start=True, stop=True).then_inc(product, 1)

        @block.scalar
        def _(act):
            for n, (i, h) in enumerate(units):
                act.wait_ge(product, n + 1)
                if n >= 4:
                    act.wait_ge(summed, n - 3)
                nc.scalar.activation(relu[:, n % 4, 0:(i + 1) * P], k.psum[:, n % 4, 0:(i + 1) * P],
                                     ACT.Relu).then_inc(clipped, 1)

        @block.gpsimd
        def _(pool):
            nc.gpsimd.memset(a["bias"][:, 0, 0:P], 0.0).then_inc(causal, 1)
            pool.wait_ge(causal, 1)
            nc.gpsimd.affine_select(out=a["bias"][:, 0, 0:P], in_=a["bias"][:, 0, 0:P], pattern=[[-1, P]],
                                    compare_op=ALU.is_ge, fill=NEG, base=0, channel_multiplier=1).then_inc(causal, 1)
            for i in range(1, ST):
                pool.wait_ge(summed, IH * i)
                own = score[:, i - 1, i * P:(i + 1) * P]
                nc.gpsimd.affine_select(out=own, in_=own, pattern=[[-1, P]], compare_op=ALU.is_ge, fill=NEG,
                                        base=0, channel_multiplier=1).then_inc(causal, 1)

        @block.vector
        def _(dve):
            own, V = Count(chain), nc.vector
            for i in range(1, ST):
                keys = (i + 1) * P
                for h in range(IH):
                    n = (i - 1) * IH + h
                    s = score[:, i - 1, 0:keys]
                    dve.wait_ge(clipped, n + 1)
                    w = a["wi"][:, i, h:h + 1]
                    if h == 0:
                        j = V.tensor_scalar(s, relu[:, n % 4, 0:keys], w, None, ALU.mult)
                    else:
                        dve.wait_ge(summed, n)
                        j = V.scalar_tensor_tensor(out=s, in0=relu[:, n % 4, 0:keys], scalar=w, in1=s,
                                                   op0=ALU.mult, op1=ALU.add)
                    j.then_inc(summed, 1)
            dve.wait_ge(causal, 1 + ST)
            later = range(1, ST)
            s = {i: score[:, i - 1, 0:(i + 1) * P] for i in later}
            found, taken = {}, {}
            for r in range(TOPK // 8):
                for i in later:
                    if r:
                        dve.wait_ge(own.sem, taken[i])
                    found[i] = own.by(V.max(best[:, i - 1, :], s[i]))
                for i in later:
                    dve.wait_ge(own.sem, found[i])
                    taken[i] = own.by(V.match_replace(s[i], best[:, i - 1, :], s[i], TAKEN))
            for i in later:
                dve.wait_ge(own.sem, taken[i])
                V.tensor_scalar(a["bias"][:, i, 0:(i + 1) * P], s[i], TAKEN, NEG, ALU.not_equal, ALU.mult)


@stage
def attention_heads(k, a):
    nc = k.nc
    units = [(i, h) for i in range(ST) for h in range(NH)]
    N = len(units)
    flat = k.turned_flat
    minus = flat[:, 0:1024].rearrange("p (b s) -> p b s", b=2)
    prob = flat[:, 1024:2560].rearrange("p (b s) -> p b s", b=3)
    prob_t = flat[:, 2560:3584].rearrange("p (b s) -> p b s", b=2)
    top, total, inv = (k.stat[:, 8 * j:8 * j + 8] for j in range(3))
    names = ("score", "masked", "exp", "inverse", "scaled", "turned", "placed", "product", "kept")
    score, masked, exped, inverse, scaled, turned, placed, product, kept = (k.sem(f"heads_{n}") for n in names)

    with nc.Block() as block:
        @block.tensor
        def _(pe):
            for n in range(N + 3):
                if n < N:
                    i, h = units[n]
                    r, keys = HD * (h % 2), (i + 1) * P
                    if n >= 2:
                        pe.wait_ge(masked, n - 1)
                    nc.tensor.matmul(k.psum[:, n % 2, 0:keys], a["q"][r:r + HD, h // 2, i * P:(i + 1) * P],
                                     a["k"][r:r + HD, h // 4, 0:keys], start=True, stop=True).then_inc(score, 1)
                m = n - 2
                if 0 <= m < N:
                    i, h = units[m]
                    pe.wait_ge(scaled, m + 1)
                    if m >= 2:
                        pe.wait_ge(placed, m - 1)
                    for b in range(i + 1):
                        j = nc.tensor.transpose(k.psum[:, 2 + m % 2, b * P:(b + 1) * P],
                                                prob[:, m % 3, b * P:(b + 1) * P], k.cst("ident"))
                    j.then_inc(turned, 1)
                m = n - 3
                if 0 <= m < N:
                    i, h = units[m]
                    r, pair = HD * (h % 2), m // 2
                    pe.wait_ge(placed, m + 1)
                    if h % 2 == 0 and pair >= 2:
                        pe.wait_ge(kept, pair - 1)
                    for b in range(i + 1):
                        j = nc.tensor.matmul(k.psum[r:r + HD, 4 + pair % 2, 0:P],
                                             a["v"][:, b, (h // 4) * HD:(h // 4 + 1) * HD],
                                             prob_t[:, m % 2, b * P:(b + 1) * P], start=(b == 0), stop=(b == i),
                                             tile_position=(0, r))
                    j.then_inc(product, 1)

        @block.vector
        def _(dve):
            V = nc.vector
            for n in range(N + 5):
                if n < N:
                    i, h = units[n]
                    keys = (i + 1) * P
                    dve.wait_ge(score, n + 1)
                    if n >= 2:
                        dve.wait_ge(exped, n - 1)
                    V.tensor_tensor_reduce(minus[:, n % 2, 0:keys], k.psum[:, n % 2, 0:keys], a["bias"][:, i, 0:keys],
                                           -1.0, HUGE, ALU.add, ALU.min, top[:, n % 8:n % 8 + 1]).then_inc(masked, 1)
                if 1 <= n <= N:
                    m = n - 1
                    dve.wait_ge(exped, m + 1)
                    V.reciprocal(inv[:, m % 8:m % 8 + 1], total[:, m % 8:m % 8 + 1]).then_inc(inverse, 1)
                m = n - 4
                if 0 <= m < N and m % 2 == 1:
                    i, h = units[m]
                    dve.wait_ge(product, m + 1)
                    V.tensor_copy(a["out"][:, h // 2, i * P:(i + 1) * P], k.psum[:, 4 + (m // 2) % 2, 0:P]).then_inc(kept, 1)

        @block.scalar
        def _(act):
            for n in range(N + 2):
                if n < N:
                    i, h = units[n]
                    keys = (i + 1) * P
                    act.wait_ge(masked, n + 1)
                    if n >= 3:
                        act.wait_ge(turned, n - 2)
                    nc.scalar.activation(prob[:, n % 3, 0:keys], minus[:, n % 2, 0:keys], ACT.Exp,
                                         bias=top[:, n % 8:n % 8 + 1], scale=-1.0,
                                         accum_out=total[:, n % 8:n % 8 + 1]).then_inc(exped, 1)
                m = n - 2
                if m >= 0:
                    i, h = units[m]
                    keys = (i + 1) * P
                    act.wait_ge(turned, m + 1)
                    if m >= 2:
                        act.wait_ge(product, m - 1)
                    nc.scalar.activation(prob_t[:, m % 2, 0:keys], k.psum[:, 2 + m % 2, 0:keys],
                                         ACT.Copy).then_inc(placed, 1)

        @block.gpsimd
        def _(pool):
            for n, (i, h) in enumerate(units):
                pool.wait_ge(inverse, n + 1)
                p = prob[:, n % 3, 0:(i + 1) * P]
                nc.gpsimd.tensor_scalar(p, p, inv[:, n % 8:n % 8 + 1], 1.0, ALU.mult, ALU.mult).then_inc(scaled, 1)
    return lambda ki: a["out"][:, ki, :]


def blend_layout(k):
    w = k.work
    b = {}

    def take(name, at, tiles, width):
        b[name] = w[:, at:at + tiles * width].rearrange("p (f s) -> p f s", f=tiles)
        return at + tiles * width

    at = take("qa", 0, 4, S)
    at = take("ka", at, 2, KEYS)
    at = take("qb", at, BH, S)
    at = take("kb", at, BH, KEYS)
    at = take("va", at, KT2, P)
    at = take("vb", at, KT2, BH * P)
    b["free"] = w[:, at:16384]
    at = take("ya", 16384, 4, S)
    at = take("yb", at, BH, S)
    return b


@stage
def modulation(k):
    nc = k.nc
    m = k.mod[:, :].rearrange("p (m d w) -> p m d w", m=N_MOD, w=2)
    scale = k.affine[:, :].rearrange("p (n d) -> p n d", n=6)
    diag = k.work[:, 0:2 * D].rearrange("p (g d) -> p g d", g=2)
    chain, prods, sums, exps, diags, rows = (k.sem(f"mod_{n}") for n in ("chain", "prods", "sums", "exps", "diags", "rows"))
    lam_prod, lam_exp = k.stat[:, 0:2], k.stat[:, 2:4]
    context = k.work[:, 2 * D:2 * D + CT * D].rearrange("p (t d) -> p t d", t=CT)
    context_in = k.sem("context_in")
    with nc.Block() as block:
        @block.sync
        def _(sp):
            sp.dma_start(context, k.io["ctx"].rearrange("(t p) d -> p t d", p=P)).then_inc(context_in, 16)
            sp.dma_start(k.head_gains, k.io["rows"][8, 0:4 * HD].partition_broadcast(P)).then_inc(context_in, 16)
            sp.wait_ge(context_in, 32)

        @block.vector
        def _(dve):
            own, V = Count(chain), nc.vector
            lam = k.col("lambdas")
            V.tensor_tensor(lam_prod[:, 0:1], lam[:, 0:1], lam[:, 1:2], ALU.mult)
            V.tensor_tensor(lam_prod[:, 1:2], lam[:, 2:3], lam[:, 3:4], ALU.mult).then_inc(prods, 1)
            for g, mod in enumerate((2, 5)):
                for d in range(DT):
                    V.tensor_scalar(diag[:, g, d * P:(d + 1) * P], k.cst("ident"), m[:, mod, d, 0:1], None,
                                    ALU.mult).then_inc(diags, 1)
            for n, (base, sh, sc, w) in enumerate((("norm_attn", 0, 1, 0), ("norm_attn", 0, 1, 1), ("norm_mlp", 3, 4, 0))):
                V.tensor_copy(scale[:, 2 * n + 1], m[:, sh, :, w])
                own.then_wait(dve, V.tensor_scalar(scale[:, 2 * n], m[:, sc, :, w], 1.0, None, ALU.add))
                own.then_wait(dve, V.tensor_tensor(scale[:, 2 * n], scale[:, 2 * n], k.col(base), ALU.mult))
            dve.wait_ge(exps, 1)
            own.then_wait(dve, V.tensor_tensor(k.neg_lam, lam_exp[:, 1:2], lam_exp[:, 0:1], ALU.subtract))
            V.tensor_scalar(k.neg_lam, k.neg_lam, -LAM_INIT, None, ALU.add)
            for n in range(4):
                dve.wait_ge(rows, n + 1)
                V.tensor_copy(k.gate_rows[:, n * NB:(n + 1) * NB], k.psum[:, n, :])

        @block.tensor
        def _(pe):
            pe.wait_ge(prods, 1)
            nc.tensor.matmul(k.psum[:, 4, 0:2], k.cst("ones"), lam_prod, start=True, stop=True).then_inc(sums, 1)
            for g in range(2):
                for half in range(2):
                    pe.wait_ge(diags, DT * g + 4 * half + 4)
                    nc.tensor.matmul(k.psum[:, 2 * g + half, :], k.cst("ones"), diag[:, g, half * NB:(half + 1) * NB],
                                     start=True, stop=True).then_inc(rows, 1)

        @block.scalar
        def _(act):
            act.wait_ge(sums, 1)
            nc.scalar.activation(lam_exp, k.psum[:, 4, 0:2], ACT.Exp).then_inc(exps, 1)
    return context


@stage
def blend_project(k, b):
    nc = k.nc
    first = FIRST["qa"]
    units = ([("qa", t) for t in range(ST)] + [("kva", t) for t in range(ST + CT)] + [("qb", t) for t in range(ST)]
             + [("kb", t) for t in range(ST + CT)] + [("vb", t) for t in range(ST + CT)])
    order = ("qa", "kva", "qb", "kb", "vb")
    width = {"kva": 256}
    gain_of = {"qa": 0, "kva": 1, "qb": 2, "kb": 3}
    rope = k.cst("rope2").rearrange("p (f t c) -> p f t c", f=2, t=ST)
    free = b["free"][:, 0:3584].rearrange("p (n c) -> p n c", n=7)
    late = b["ya"]
    raw = [free[:, 0], free[:, 1]]
    squares = [free[:, 2], free[:, 3]]
    staged = [free[:, 4], free[:, 5]]
    normal = free[:, 6]
    m1, m2 = late[:, 0], late[:, 1]
    small = late[:, 2, 0:96].rearrange("p (n c) -> p n c", c=8)
    ssq, mean, root, rstd = ([small[:, 2 * j], small[:, 2 * j + 1]] for j in range(4))
    normed = [n for n, (c, t) in enumerate(units) if c != "vb"]
    M = len(normed)
    names = ("product", "copied", "squared", "meaned", "rooted", "staged", "turned", "placed", "chain", "v_copied")
    product, copied, squared, meaned, rooted, staged_s, turned, placed, chain, v_copied = (k.sem(f"blend_{n}") for n in names)

    def token0(t):
        return t * P

    ends = {c: max(n for n, u in enumerate(units) if u[0] == c) + 1 for c in order}

    with nc.Block() as block:
        @block.sync
        def _(sp):
            for i, c in enumerate(order):
                sp.wait_ge(product, ends[c])
                k.load_chunk(sp, first + i + NSLOT)

        @block.tensor
        def _(pe):
            for n in range(len(units) + 2):
                if n < len(units):
                    c, t = units[n]
                    wd = width.get(c, NB)
                    w = k.chunk(pe, first + order.index(c), wd)
                    if n >= 4:
                        pe.wait_ge(copied, n - 3)
                    for d in range(DT):
                        i = nc.tensor.matmul(k.psum[:, n % 4, 0:wd], k.turned[:, d, t * P:(t + 1) * P], w[:, d, :],
                                             start=(d == 0), stop=(d == DT - 1))
                    i.then_inc(product, 1)
                m = n - 2
                if 0 <= m < M:
                    c, t = units[m]
                    pe.wait_ge(staged_s, m + 1)
                    if m >= 2:
                        pe.wait_ge(placed, m - 1)
                    for f in range(2 if c == "kva" else 4):
                        i = nc.tensor.transpose(k.psum[:, 4 + m % 2, f * P:(f + 1) * P],
                                                staged[m % 2][:, f * P:(f + 1) * P], k.cst("ident"))
                    i.then_inc(turned, 1)

        @block.scalar
        def _(act):
            for n in range(len(units) + 3):
                if n < len(units):
                    c, t = units[n]
                    act.wait_ge(product, n + 1)
                    ps = k.psum[:, n % 4, :]
                    if c == "vb":
                        nc.scalar.activation(b["vb"][:, t, :], ps, ACT.Copy).then_inc(copied, 1)
                    else:
                        wd = width.get(c, NB)
                        if n >= 2:
                            act.wait_ge(staged_s, n - 1)
                        nc.scalar.activation(raw[n % 2][:, 0:wd], ps[:, 0:wd], ACT.Copy).then_inc(copied, 1)
                        act.wait_ge(copied, n + 1)
                        wd = P if c == "kva" else NB
                        nc.scalar.activation(squares[n % 2][:, 0:wd], raw[n % 2][:, 0:wd], ACT.Square).then_inc(squared, 1)
                        act.wait_ge(meaned, n + 1)
                        nc.scalar.activation(root[n % 2][:, 0:wd // HD], mean[n % 2][:, 0:wd // HD], ACT.Sqrt).then_inc(rooted, 1)
                m = n - 3
                if 0 <= m < M:
                    c, t = units[m]
                    tiles = 2 if c == "kva" else 4
                    act.wait_ge(turned, m + 1)
                    dst = b["ka" if c == "kva" else c]
                    nc.scalar.activation(dst[:, :, token0(t):token0(t) + P],
                                         k.psum[:, 4 + m % 2, 0:tiles * P].rearrange("p (f s) -> p f s", f=tiles),
                                         ACT.Copy, scale=HD ** -0.5 if c[0] == "q" else 1.0).then_inc(placed, 1)

        @block.vector
        def _(dve):
            own, V = Count(chain), nc.vector

            def heads_of(x, heads):
                return x[:, 0:heads * HD].rearrange("p (h c) -> p h c", c=HD)

            for m in range(M + 1):
                if m < M:
                    c, t = units[m]
                    heads = 2 if c == "kva" else 8
                    dve.wait_ge(squared, m + 1)
                    own.then_wait(dve, V.tensor_reduce(ssq[m % 2][:, 0:heads], heads_of(squares[m % 2], heads), AX.X, ALU.add))
                    V.tensor_scalar(mean[m % 2][:, 0:heads], ssq[m % 2][:, 0:heads], 1.0 / HD, EPS, ALU.mult,
                                    ALU.add).then_inc(meaned, 1)
                n = m - 1
                if n < 0:
                    continue
                c, t = units[n]
                heads = 2 if c == "kva" else 8
                wide = [P, heads, HD]
                dve.wait_ge(rooted, n + 1)
                r, x, y = rstd[n % 2][:, 0:heads], heads_of(raw[n % 2], heads), heads_of(normal, heads)
                own.then_wait(dve, V.reciprocal(r, root[n % 2][:, 0:heads]))
                if n:
                    dve.wait_ge(staged_s, n)
                own.then_wait(dve, V.tensor_tensor(y, x, r.unsqueeze(2).broadcast_to(wide), ALU.mult))
                gain = k.head_gains[:, gain_of[c] * HD:(gain_of[c] + 1) * HD].unsqueeze(1).broadcast_to(wide)
                if c == "kva":
                    V.tensor_copy(b["va"][:, t, :], raw[n % 2][:, P:2 * P])
                if n >= 2:
                    dve.wait_ge(turned, n - 1)
                out = staged[n % 2]
                o = heads_of(out if c != "kva" else normal, heads)
                if t >= ST:
                    if c == "kva":
                        own.then_wait(dve, V.tensor_tensor(y, y, gain, ALU.mult))
                    else:
                        V.tensor_tensor(o, y, gain, ALU.mult).then_inc(staged_s, 1)
                else:
                    own.then_wait(dve, V.tensor_tensor(y, y, gain, ALU.mult))
                    yp = y.rearrange("p h (c two) -> p h c two", two=2)
                    a1 = heads_of(m1, heads).rearrange("p h (c two) -> p h c two", two=2)
                    a2 = heads_of(m2, heads).rearrange("p h (c two) -> p h c two", two=2)
                    op = o.rearrange("p h (c two) -> p h c two", two=2)
                    half = [P, heads, HD // 2]
                    cos = rope[:, 0, t, :].unsqueeze(1).broadcast_to(half)
                    sin = rope[:, 1, t, :].unsqueeze(1).broadcast_to(half)
                    V.tensor_tensor(a1[:, :, :, 0], yp[:, :, :, 0], cos, ALU.mult)
                    V.tensor_tensor(a1[:, :, :, 1], yp[:, :, :, 1], cos, ALU.mult)
                    V.tensor_tensor(a2[:, :, :, 0], yp[:, :, :, 1], sin, ALU.mult)
                    own.then_wait(dve, V.tensor_tensor(a2[:, :, :, 1], yp[:, :, :, 0], sin, ALU.mult))
                    V.tensor_tensor(op[:, :, :, 0], a1[:, :, :, 0], a2[:, :, :, 0], ALU.subtract)
                    j = V.tensor_tensor(op[:, :, :, 1], a1[:, :, :, 1], a2[:, :, :, 1], ALU.add)
                    if c == "kva":
                        own.then_wait(dve, j)
                    else:
                        j.then_inc(staged_s, 1)
                if c == "kva":
                    V.tensor_copy(out[:, 0:4 * HD].rearrange("p (h b c) -> p h b c", b=2, c=HD),
                                  y.unsqueeze(2).broadcast_to([P, 2, 2, HD])).then_inc(staged_s, 1)


@stage
def blend_heads_a(k, b):
    nc = k.nc
    units = [(i, h) for i in range(ST) for h in range(AH)]
    N = len(units)
    prob = b["free"][:, 0:3 * KEYS].rearrange("p (n s) -> p n s", n=3)
    prob_t = b["free"][:, 3 * KEYS:5 * KEYS].rearrange("p (n s) -> p n s", n=2)
    flat = k.psum.rearrange("p b s -> p (b s)")
    scores = lambda n: flat[:, 2 * NB * (n % 2):2 * NB * (n % 2) + KEYS]
    turned_bank = flat[:, 4 * NB:4 * NB + KEYS]
    top, total, inv = (k.stat[:, 8 * j:8 * j + 8] for j in range(3))
    names = ("score", "topped", "exp", "inverse", "scaled", "turned", "placed", "product", "kept")
    score, topped, exped, inverse, scaled, turned, placed, product, kept = (k.sem(f"branch_a_{n}") for n in names)

    with nc.Block() as block:
        @block.tensor
        def _(pe):
            for n in range(N + 3):
                if n < N:
                    i, h = units[n]
                    r = HD * (h % 2)
                    if n >= 2:
                        pe.wait_ge(exped, n - 1)
                    for lo, hi in ((0, S), (S, KEYS)):
                        j = nc.tensor.matmul(scores(n)[:, lo:hi], b["qa"][r:r + HD, h // 2, i * P:(i + 1) * P],
                                             b["ka"][r:r + HD, h // 4, lo:hi], start=True, stop=True)
                    j.then_inc(score, 1)
                m = n - 2
                if 0 <= m < N:
                    pe.wait_ge(scaled, m + 1)
                    if m >= 1:
                        pe.wait_ge(placed, m)
                    for t in range(KT2):
                        j = nc.tensor.transpose(turned_bank[:, t * P:(t + 1) * P], prob[:, m % 3, t * P:(t + 1) * P],
                                                k.cst("ident"))
                    j.then_inc(turned, 1)
                m = n - 3
                if 0 <= m < N:
                    i, h = units[m]
                    r, pair = HD * (h % 2), m // 2
                    pe.wait_ge(placed, m + 1)
                    if h % 2 == 0 and pair >= 2:
                        pe.wait_ge(kept, pair - 1)
                    for t in range(KT2):
                        j = nc.tensor.matmul(k.psum[r:r + HD, 6 + pair % 2, 0:P], b["va"][:, t, (h // 4) * HD:(h // 4 + 1) * HD],
                                             prob_t[:, m % 2, t * P:(t + 1) * P], start=(t == 0), stop=(t == KT2 - 1),
                                             tile_position=(0, r))
                    j.then_inc(product, 1)

        @block.vector
        def _(dve):
            V = nc.vector
            for n in range(N + 4):
                if n < N:
                    dve.wait_ge(score, n + 1)
                    V.tensor_reduce(top[:, n % 8:n % 8 + 1], scores(n), AX.X, ALU.max, negate=True).then_inc(topped, 1)
                if 1 <= n <= N:
                    m = n - 1
                    dve.wait_ge(exped, m + 1)
                    V.reciprocal(inv[:, m % 8:m % 8 + 1], total[:, m % 8:m % 8 + 1]).then_inc(inverse, 1)
                m = n - 4
                if 0 <= m < N and m % 2 == 1:
                    i, h = units[m]
                    dve.wait_ge(product, m + 1)
                    V.tensor_copy(b["ya"][:, h // 2, i * P:(i + 1) * P], k.psum[:, 6 + (m // 2) % 2, 0:P]).then_inc(kept, 1)

        @block.scalar
        def _(act):
            for n in range(N + 2):
                if n < N:
                    act.wait_ge(topped, n + 1)
                    if n >= 3:
                        act.wait_ge(turned, n - 2)
                    nc.scalar.activation(prob[:, n % 3, :], scores(n), ACT.Exp, bias=top[:, n % 8:n % 8 + 1],
                                         accum_out=total[:, n % 8:n % 8 + 1]).then_inc(exped, 1)
                m = n - 2
                if m >= 0:
                    act.wait_ge(turned, m + 1)
                    if m >= 2:
                        act.wait_ge(product, m - 1)
                    nc.scalar.activation(prob_t[:, m % 2, :], turned_bank, ACT.Copy).then_inc(placed, 1)

        @block.gpsimd
        def _(pool):
            for n in range(N):
                pool.wait_ge(inverse, n + 1)
                nc.gpsimd.tensor_scalar(prob[:, n % 3, :], prob[:, n % 3, :], inv[:, n % 8:n % 8 + 1], 1.0,
                                        ALU.mult, ALU.mult).then_inc(scaled, 1)


@stage
def blend_heads_b(k, b):
    nc = k.nc
    units = [(i, h) for i in range(ST) for h in range(BH)]
    N = len(units)
    prob = [x.rearrange("p (m s) -> p m s", m=2) for x in (b["free"][:, 0:2 * KEYS], b["free"][:, 2 * KEYS:4 * KEYS],
                                                           k.small[:, 0:2 * KEYS])]
    prob_t = b["free"][:, 4 * KEYS:5 * KEYS]
    flat = k.psum.rearrange("p b s -> p (b s)")
    scores = lambda m: flat[:, 2 * NB * m:2 * NB * m + KEYS]
    turned_bank = flat[:, 4 * NB:4 * NB + KEYS]
    top, total, inv = (k.stat[:, 8 * j:8 * j + 8] for j in range(3))
    names = ("score", "topped", "exp", "inverse", "weight", "scaled", "mixed", "turned", "placed", "product", "kept")
    (score, topped, exped, inverse, weight, scaled, mixed, turned, placed, product,
     kept) = (k.sem(f"branch_b_{n}") for n in names)

    def at(x, n, m):
        j = (2 * n + m) % 8
        return x[:, j:j + 1]

    with nc.Block() as block:
        @block.tensor
        def _(pe):
            for n in range(N + 3):
                if n < N:
                    i, h = units[n]
                    for m in range(2):
                        if n >= 1:
                            pe.wait_ge(exped, 2 * n - 1 + m)
                        for lo, hi in ((0, S), (S, KEYS)):
                            j = nc.tensor.matmul(scores(m)[:, lo:hi], b["qb"][HD * m:HD * (m + 1), h, i * P:(i + 1) * P],
                                                 b["kb"][HD * m:HD * (m + 1), h, lo:hi], start=True, stop=True)
                        j.then_inc(score, 1)
                m = n - 2
                if 0 <= m < N:
                    pe.wait_ge(mixed, m + 1)
                    if m >= 1:
                        pe.wait_ge(placed, m)
                    for t in range(KT2):
                        j = nc.tensor.transpose(turned_bank[:, t * P:(t + 1) * P], prob[m % 3][:, 0, t * P:(t + 1) * P],
                                                k.cst("ident"))
                    j.then_inc(turned, 1)
                m = n - 3
                if 0 <= m < N:
                    i, h = units[m]
                    pe.wait_ge(placed, m + 1)
                    if m >= 2:
                        pe.wait_ge(kept, m - 1)
                    for t in range(KT2):
                        j = nc.tensor.matmul(k.psum[:, 6 + m % 2, 0:P], b["vb"][:, t, h * P:(h + 1) * P],
                                             prob_t[:, t * P:(t + 1) * P], start=(t == 0), stop=(t == KT2 - 1))
                    j.then_inc(product, 1)

        @block.vector
        def _(dve):
            V = nc.vector
            for n in range(N + 3):
                if n < N:
                    for m in range(2):
                        dve.wait_ge(score, 2 * n + m + 1)
                        V.tensor_reduce(at(top, n, m), scores(m), AX.X, ALU.max, negate=True).then_inc(topped, 1)
                u = n - 1
                if 0 <= u < N:
                    for m in range(2):
                        dve.wait_ge(exped, 2 * u + m + 1)
                        V.reciprocal(at(inv, u, m), at(total, u, m)).then_inc(inverse, 1)
                    dve.wait_ge(inverse, 2 * u + 2)
                    V.tensor_tensor(at(inv, u, 1), at(inv, u, 1), k.neg_lam, ALU.mult).then_inc(weight, 1)
                    dve.wait_ge(weight, u + 1)
                    dve.wait_ge(scaled, u + 1)
                    V.scalar_tensor_tensor(out=prob[u % 3][:, 0, :], in0=prob[u % 3][:, 1, :], scalar=at(inv, u, 1),
                                           in1=prob[u % 3][:, 0, :], op0=ALU.mult, op1=ALU.add).then_inc(mixed, 1)
                u = n - 3
                if u >= 0:
                    i, h = units[u]
                    dve.wait_ge(product, u + 1)
                    V.tensor_copy(b["yb"][:, h, i * P:(i + 1) * P], k.psum[:, 6 + u % 2, 0:P]).then_inc(kept, 1)

        @block.scalar
        def _(act):
            for n in range(N + 2):
                if n < N:
                    for m in range(2):
                        act.wait_ge(topped, 2 * n + m + 1)
                        if n >= 3:
                            act.wait_ge(turned, n - 2)
                        nc.scalar.activation(prob[n % 3][:, m, :], scores(m), ACT.Exp, bias=at(top, n, m),
                                             accum_out=at(total, n, m)).then_inc(exped, 1)
                m = n - 2
                if m >= 0:
                    act.wait_ge(turned, m + 1)
                    if m >= 1:
                        act.wait_ge(product, m)
                    nc.scalar.activation(prob_t, turned_bank, ACT.Copy).then_inc(placed, 1)

        @block.gpsimd
        def _(pool):
            for n in range(N):
                pool.wait_ge(inverse, 2 * n + 1)
                nc.gpsimd.tensor_scalar(prob[n % 3][:, 0, :], prob[n % 3][:, 0, :], at(inv, n, 0), 1.0,
                                        ALU.mult, ALU.mult).then_inc(scaled, 1)


@stage
def blend_subnorm(k, b):
    nc = k.nc
    sq = b["free"][:, 0:2048].rearrange("p (h s) -> p h s", h=BH)
    sub = k.stat[:, 0:1]
    squared, summed, meaned, rooted, chain = (k.sem(f"subln_{n}") for n in ("squared", "summed", "meaned", "rooted", "chain"))
    with nc.Block() as block:
        @block.scalar
        def _(act):
            for h in range(BH):
                nc.scalar.activation(sq[:, h], b["yb"][:, h, :], ACT.Square).then_inc(squared, 1)
            for h in range(BH):
                act.wait_ge(meaned, h + 1)
                nc.scalar.activation(sq[:, h], sq[:, h], ACT.Sqrt).then_inc(rooted, 1)

        @block.tensor
        def _(pe):
            for h in range(BH):
                pe.wait_ge(squared, h + 1)
                nc.tensor.matmul(k.psum[:, h, :], k.cst("ones"), sq[:, h], start=True, stop=True).then_inc(summed, 1)

        @block.vector
        def _(dve):
            own, V = Count(chain), nc.vector
            own.then_wait(dve, V.tensor_scalar(sub, k.col("subln"), 1.0 - LAM_INIT, None, ALU.mult))
            for h in range(BH):
                dve.wait_ge(summed, h + 1)
                V.tensor_scalar(sq[:, h], k.psum[:, h, :], 1.0 / P, SUBLN_EPS, ALU.mult, ALU.add).then_inc(meaned, 1)
            for h in range(BH):
                dve.wait_ge(rooted, h + 1)
                own.then_wait(dve, V.reciprocal(sq[:, h], sq[:, h]))
                V.scalar_tensor_tensor(out=b["yb"][:, h, :], in0=b["yb"][:, h, :], scalar=sub, in1=sq[:, h],
                                       op0=ALU.mult, op1=ALU.mult)


@stage
def blend_merge(k, b):
    nc = k.nc
    first = FIRST["ga"]
    tiles = lambda x, n: x.rearrange("p (f s) -> p f s", f=n)
    x_high, x_low = tiles(k.arena_r[4][:, :], 8), tiles(k.arena_r[5][:, :], 8)
    merged, part = tiles(k.work[:, 8192:12288], 8), tiles(k.work[:, 12288:16384], 8)
    y, y_low, y_high = tiles(k.work[:, 16384:20480], 8), tiles(k.arena_r[8][:, :], 8), tiles(k.operand_r[:, 0:4096], 8)
    gate = tiles(k.small[:, 0:2048], 4)
    names = ("high", "low", "x_high", "x_low", "y_high", "y_low", "used", "gate_product", "product", "opened", "gated", "added")
    (high, low, x_high_ready, x_low_ready, y_high_ready, y_low_ready, used, gate_product, product, opened, gated,
     added) = (k.sem(f"merge_{n}") for n in names)
    groups = [(half, br) for half in range(2) for br in range(2)]
    M = 3 * len(groups)

    def chunk_of(m):
        return first + 2 * (m // 3) + (m % 3) // 2

    def piece(m):
        slot, at = chunk_of(m) % NSLOT, slice(PIECE, 2 * PIECE) if m % 3 == 1 else slice(0, PIECE)
        return k.ring[:, slot, at], k.arena_r[slot][:, at], k.arena_r[NSLOT][:, (m % 2) * PIECE:(m % 2 + 1) * PIECE]

    with nc.Block() as block:
        @block.sync
        def _(sp):
            for m in range(M):
                if m % 3:
                    sp.wait_ge(used, m + 1)
                    k.load_chunk(sp, chunk_of(m) + NSLOT)

        @block.tensor
        def _(pe):
            pe.wait_ge(x_low_ready, DT)
            for m in range(M):
                u, v = m // 3, m % 3
                raw, w_low, w_high = piece(m)
                w = [tiles(x, 4) for x in (w_high, w_low)]
                pe.wait_ge(low, m + 1)
                if m == 2:
                    pe.wait_ge(y_low_ready, DT)
                for f in range(4):
                    if u and v == 0:
                        pe.wait_ge(opened, 4 * (u - 1) + f + 1)
                    if u and v == 2:
                        pe.wait_ge(gated, 4 * (u - 1) + f + 1)
                    for j in range(4):
                        if v < 2:
                            right, start, stop = (x_high[:, 4 * v + j, :], x_low[:, 4 * v + j, :]), v == 0 and j == 0, v == 1 and j == 3
                        else:
                            c = 4 * (u % 2) + j
                            right, start, stop = (y_high[:, c, :], y_low[:, c, :]), j == 0, j == 3
                        i = exact_product(nc, k.psum[:, 2 * f + v // 2, :], [t[:, j, f * P:(f + 1) * P] for t in w], right,
                                          start=start, stop=stop)
                    if v:
                        i.then_inc(gate_product if v == 1 else product, 1)
                if v == 0:
                    i.then_inc(used, 1)
                else:
                    pe.wait_ge(gate_product if v == 1 else product, 4 * u + 4)
                    pe.sem_inc(used, 1)

        @block.scalar
        def _(act):
            def split_high(m):
                act.wait_ge(k.loaded[chunk_of(m) % NSLOT], 16 * (chunk_of(m) // NSLOT + 1))
                if m >= 2:
                    act.wait_ge(used, m - 1)
                raw, _, w_high = piece(m)
                nc.scalar.activation(w_high, raw, ACT.Copy).then_inc(high, 1)

            split_high(0)
            for d in range(DT):
                nc.scalar.activation(x_high[:, d, :], k.turned[:, d, 0:S], ACT.Copy).then_inc(x_high_ready, 1)
            split_high(1)
            act.wait_ge(x_low_ready, DT)
            for d in range(DT):
                nc.scalar.activation(y_high[:, d, :], y[:, d, :], ACT.Copy).then_inc(y_high_ready, 1)
            for m in range(1, M):
                if m + 1 < M:
                    split_high(m + 1)
                if m % 3 == 1:
                    for n in range(4 * (m // 3), 4 * (m // 3) + 4):
                        act.wait_ge(gate_product, n + 1)
                        if n >= 4:
                            act.wait_ge(gated, n - 3)
                        nc.scalar.activation(gate[:, n % 4], k.psum[:, 2 * (n % 4), :], ACT.Sigmoid).then_inc(opened, 1)

        @block.vector
        def _(dve):
            V = nc.vector

            def split_low(m):
                raw, w_low, w_high = piece(m)
                dve.wait_ge(high, m + 1)
                V.tensor_tensor(w_low, raw, w_high.bitcast(F32), ALU.subtract).then_inc(low, 1)

            split_low(0)
            for d in range(DT):
                dve.wait_ge(x_high_ready, d + 1)
                V.tensor_tensor(x_low[:, d, :], k.turned[:, d, 0:S], x_high[:, d, :].bitcast(F32), ALU.subtract).then_inc(x_low_ready, 1)
            split_low(1)
            for d in range(DT):
                dve.wait_ge(y_high_ready, d + 1)
                V.tensor_tensor(y_low[:, d, :], y[:, d, :], y_high[:, d, :].bitcast(F32), ALU.subtract).then_inc(y_low_ready, 1)
            for m in range(1, M):
                if m + 1 < M:
                    split_low(m + 1)
                if m % 3 == 2:
                    for n in range(4 * (m // 3), 4 * (m // 3) + 4):
                        dve.wait_ge(product, n + 1)
                        dve.wait_ge(opened, n + 1)
                        if n >= 8:
                            dve.wait_ge(added, n % 4 + 1)
                        V.tensor_tensor(part[:, n % 8], gate[:, n % 4], k.psum[:, 2 * (n % 4) + 1, :], ALU.mult).then_inc(gated, 1)

        @block.gpsimd
        def _(pool):
            for f in range(DT):
                half, ff = f // 4, f % 4
                pool.wait_ge(gated, 8 * half + ff + 5)
                nc.gpsimd.tensor_tensor(merged[:, f, :], part[:, ff], part[:, 4 + ff], ALU.add).then_inc(added, 1)
    return lambda ki: merged[:, ki, :]


EXTRA = NBLK - NE + 2
ROLES = ("gate", "up", "gate", "up", "down", "down")
PAD_ROWS = S * NK
SLOTS_E = S // CAP


PIECES = 12
NHI = 3
BY_POOL = (5, 10)


def expert_layout(k):
    e, w = {}, k.work
    piece_at = lambda n: k.arena_r[n // 2][:, n % 2 * PIECE:(n % 2 + 1) * PIECE]
    e["raw"] = k.arena[:, 0:PIECES * PIECE].rearrange("p (n c) -> p n c", n=PIECES)
    e["low"] = [piece_at(n) for n in range(PIECES)]
    at = 2 * CHUNK

    def take(name, width, dt=F32):
        nonlocal at
        e[name] = w[:, at:at + width] if dt == F32 else w[:, at:at + width].bitcast(dt)
        at += width

    e["high"] = [piece_at(PIECES + n) for n in range(NHI)]
    at += NHI * PIECE
    e["bias_high"], e["bias_low"] = (piece_at(PIECES + NHI + n)[0:NE, :] for n in range(2))
    e["bias"] = w[0:NE, at + 2 * D:at + 4 * D]
    at += 4 * D
    take("token", NE * SLOTS_E, I32)
    take("home", NE * SLOTS_E, I32)
    take("plan", 2 * (NE + EXTRA) + 2, I32)
    take("token_col", 2, I32)
    take("home_col", 2, I32)
    e["choice"] = k.arena_r[8][0:NE, at - 4 * CHUNK:at - 4 * CHUNK + CAP]
    at += CAP
    take("open", D)
    assert at <= 20480
    e["x_rows"], _, _, e["y"], e["gate"], e["up"] = (k.turned_flat[:, n * D:(n + 1) * D] for n in range(6))
    e["x_high"], e["x_low"] = (k.operand_r[:, n * D:(n + 1) * D] for n in (1, 2))
    e["hidden_high"], e["hidden_low"] = k.operand_r[:, 6 * D:7 * D], k.small_r[:, D:2 * D]
    e["weight"] = k.small[:, 0:ST * NK]
    e["spread"] = k.small[:, 64:64 + ST * NE].rearrange("p (t e) -> p t e", t=ST)
    e["spread_t"] = k.small[0:NE, 192:192 + S]
    for name, rows in (("tokens_dram", S), ("routed", PAD_ROWS + P)):
        e[name] = k.nc.dram_tensor(name, (rows, D), F32, kind="Internal").ap()
    e["list"] = k.nc.dram_tensor("assignments", (NE * S, 1), F32, kind="Internal").ap()
    e["in"] = [k.nc.alloc_semaphore(name=f"expert_weights_in_{n}") for n in range(PIECES)]
    return e


def load_expert_piece(k, e, sp, q, expert):
    role, part = q // 2, q % 2
    half = (0, 0, 1, 1, 0, 1)[role]
    src = k.io[ROLES[role]].rearrange("(e h) p (s c) -> e h s p c", h=2, s=2)
    sp.dma_start(e["raw"][:, q, :], src[expert, half, part]).then_inc(e["in"][q], 16)


@stage
def route(k, e):
    nc = k.nc
    rows = [k.work[:, 11264 + D * t:11264 + D * (t + 1)] for t in range(3)] + [k.gate_rows[:, 0:D]]
    free = k.work[:, 8192:11264]
    NA = ST * NK
    used = 0

    def take(width, **shape):
        nonlocal used
        used += width
        assert used <= free.shape[1]
        return free[:, used - width:used]

    router = take(DT * NE).rearrange("p (d e) -> p d e", d=DT)
    router_b = take(NE)
    logits = take(ST * NE).rearrange("p (t e) -> p t e", t=ST)
    best = take(ST * 8).rearrange("p (t n) -> p t n", t=ST)
    index = take(ST * 8).rearrange("p (t n) -> p t n", t=ST).bitcast(U32)
    index_f = take(NA)
    chosen = take(NA * NE).rearrange("p (a e) -> p a e", a=NA)
    spare = take(NA * NE).rearrange("p (a e) -> p a e", a=NA)
    member = take(ST * NE).rearrange("p (t e) -> p t e", t=ST)
    rank = take(ST * NE).rearrange("p (t e) -> p t e", t=ST)
    place, place_f = take(NA).bitcast(I32), take(NA)
    total, top = take(ST), take(ST)
    count, extra, end = take(NE), take(NE), take(NE)
    part = take(3 * NE).rearrange("p (n e) -> p n e", n=3)
    plan_f = take(2 * (NE + EXTRA) + 2)
    listed, value = take(P), take(P)
    weight = e["weight"].rearrange("p (t n) -> p t n", t=ST)
    NP = NE + EXTRA
    index_3d = lambda a: a.rearrange("p (t n) -> p t n", t=ST)
    names = ("inputs", "list_ready", "logits", "chain", "exp", "member", "ranked", "counted", "placed", "scattered",
             "list_in", "list_turned", "spread", "spread_turned", "rows_out", "turned_back", "copied", "bias_in", "bias_split")
    (inputs, list_ready, logits_s, chain, exped, member_s, ranked, counted, placed_s, scattered, list_in, list_turned,
     spread_s, spread_turned, rows_out, turned_back, copied, bias_in, bias_split) = (k.sem(f"route_{n}") for n in names)

    with nc.Block() as block:
        @block.sync
        def _(sp):
            sp.dma_start(e["list"].rearrange("(a b) c -> a (b c)", a=P), k.io["pad_list"].rearrange("(a b) c -> a (b c)", a=P)).then_inc(list_ready, 16)
            for q in range(PIECES):
                load_expert_piece(k, e, sp, q, 0)
            for t in range(ST):
                sp.wait_ge(copied, 2 * t + 2)
                sp.dma_start(e["tokens_dram"][t * P:(t + 1) * P, :], rows[t]).then_inc(rows_out, 16)
            sp.wait_ge(rows_out, 16 * ST)

        @block.scalar
        def _(act):
            act.dma_start(router, k.io["router"].rearrange("p (d e) -> p d e", d=DT)).then_inc(inputs, 16)
            act.dma_start(router_b, k.io["rows"][9, 0:NE].partition_broadcast(P)).then_inc(inputs, 16)
            act.dma_start(e["bias"], k.io["moe_bias"]).then_inc(bias_in, 16)
            for n in range(2 * ST):
                act.wait_ge(turned_back, n + 1)
                nc.scalar.activation(rows[n // 2][:, (n % 2) * NB:(n % 2 + 1) * NB], k.psum[:, 4 + n % 4, :],
                                     ACT.Copy).then_inc(copied, 1)
            act.wait_ge(exped, 1)
            nc.scalar.activation(weight, weight, ACT.Exp).then_inc(exped, 1)
            act.wait_ge(bias_in, 16)
            nc.scalar.activation(e["bias_high"], e["bias"], ACT.Copy).then_inc(bias_split, 1)
            act.wait_ge(scattered, 16 * NA)
            act.dma_start(listed, e["list"].rearrange("(b s) c -> b (s c)", s=CAP)).then_inc(list_in, 16)

        @block.tensor
        def _(pe):
            pe.wait_ge(inputs, 32)
            for t in range(ST):
                for d in range(DT):
                    i = nc.tensor.matmul(k.psum[:, 0, t * NE:(t + 1) * NE], k.turned[:, d, t * P:(t + 1) * P], router[:, d, :],
                                         start=(d == 0), stop=(d == DT - 1))
            i.then_inc(logits_s, 1)
            for n in range(2 * ST):
                if n >= 4:
                    pe.wait_ge(copied, n - 3)
                for d in range(4):
                    i = nc.tensor.transpose(k.psum[:, 4 + n % 4, d * P:(d + 1) * P],
                                            k.turned[:, 4 * (n % 2) + d, (n // 2) * P:(n // 2 + 1) * P], k.cst("ident"))
                i.then_inc(turned_back, 1)
            pe.wait_ge(member_s, 1)
            for t in range(ST):
                i = nc.tensor.matmul(k.psum[:, 2, 0:NE], k.cst("ones"), member[:, t, :], start=(t == 0), stop=(t == ST - 1))
            i.then_inc(counted, 1)
            for t in range(ST):
                for before in range(t + 1):
                    i = nc.tensor.matmul(k.psum[:, 1, t * NE:(t + 1) * NE], k.cst("ones" if before < t else "before"),
                                         member[:, before, :], start=(before == 0), stop=(before == t))
            i.then_inc(ranked, 1)
            pe.wait_ge(spread_s, 1)
            for t in range(ST):
                i = nc.tensor.transpose(k.psum[0:NE, 3, t * P:(t + 1) * P], e["spread"][:, t, :], k.cst("ident"))
            i.then_inc(spread_turned, 1)
            pe.wait_ge(list_in, 16)
            nc.tensor.transpose(k.psum[:, 4, 0:P], listed, k.cst("ident")).then_inc(list_turned, 1)

        @block.vector
        def _(dve):
            own, V = Count(chain), nc.vector
            then = lambda i: own.then_wait(dve, i)
            iota = k.cst("iota_e")
            dve.wait_ge(logits_s, 1)
            then(V.tensor_tensor(logits, k.psum[:, 0, 0:ST * NE].rearrange("p (t e) -> p t e", t=ST),
                                 router_b.unsqueeze(1).broadcast_to([P, ST, NE]), ALU.add))
            for t in range(ST):
                i = V.max(best[:, t, :], logits[:, t, :])
            then(i)
            for t in range(ST):
                i = V.max_index(index[:, t, :], best[:, t, :], logits[:, t, :])
            then(i)
            V.tensor_tensor(weight, best[:, :, 0:NK], best[:, :, 0:1].broadcast_to([P, ST, NK]), ALU.subtract).then_inc(exped, 1)
            then(V.tensor_copy(index_3d(index_f), index[:, :, 0:NK]))
            then(V.tensor_tensor(chosen, iota.unsqueeze(1).broadcast_to([P, NA, NE]),
                                 index_f.unsqueeze(2).broadcast_to([P, NA, NE]), ALU.is_equal))
            by_k = chosen.rearrange("p (t n) e -> p t e n", t=ST)
            V.tensor_reduce(member, by_k, AX.X, ALU.add).then_inc(member_s, 1)
            dve.wait_ge(counted, 1)
            then(V.tensor_copy(count, k.psum[:, 2, 0:NE]))
            for n in range(3):
                i = V.tensor_scalar(part[:, n, :], count, float(CAP * (n + 1)), None, ALU.is_gt)
            then(i)
            then(V.tensor_reduce(extra, part.rearrange("p n e -> p e n"), AX.X, ALU.add))
            then(V.tensor_tensor_scan(end, k.cst("ones")[:, 0:NE], extra, 0.0, ALU.mult, ALU.add))
            dve.wait_ge(ranked, 1)
            passed = spare[:, 0:NA, :]
            ordinal = iota[:, 0:EXTRA]
            expert_f, col_f = plan_f[:, 0:NP], plan_f[:, NP:2 * NP]
            V.tensor_scalar(plan_f[:, 2 * NP:2 * NP + 2], end[:, NE - 1:NE].broadcast_to([P, 2]), float(NE), None, ALU.add)
            V.tensor_copy(expert_f[:, 0:NE], iota)
            V.tensor_scalar(col_f[:, 0:NE], iota, float(SLOTS_E), None, ALU.mult)
            for lo in range(0, EXTRA, NA):
                n = min(NA, EXTRA - lo)
                then(V.tensor_tensor(passed[:, 0:n, :], ordinal[:, lo:lo + n].unsqueeze(2).broadcast_to([P, n, NE]),
                                     end.unsqueeze(1).broadcast_to([P, n, NE]), ALU.is_ge))
                then(V.tensor_reduce(expert_f[:, NE + lo:NE + lo + n], passed[:, 0:n, :], AX.X, ALU.add))
                then(V.tensor_tensor(passed[:, 0:n, :], passed[:, 0:n, :], extra.unsqueeze(1).broadcast_to([P, n, NE]), ALU.mult))
                then(V.tensor_reduce(col_f[:, NE + lo:NE + lo + n], passed[:, 0:n, :], AX.X, ALU.add))
            more_e, more_c = expert_f[:, NE:NP], col_f[:, NE:NP]
            then(V.tensor_scalar(more_e, more_e, float(NE - 1), None, ALU.min))
            then(V.tensor_tensor(more_c, ordinal, more_c, ALU.subtract))
            then(V.tensor_scalar(more_c, more_c, 1.0, float(SLOTS_E - 1), ALU.add, ALU.min))
            then(V.scalar_tensor_tensor(out=more_c, in0=more_e, scalar=float(SLOTS_E), in1=more_c, op0=ALU.mult, op1=ALU.add))
            V.tensor_copy(e["plan"], plan_f)
            then(V.tensor_copy(rank, k.psum[:, 1, 0:ST * NE].rearrange("p (t e) -> p t e", t=ST)))
            then(V.tensor_tensor(spare.rearrange("p (t n) e -> p t n e", t=ST), chosen.rearrange("p (t n) e -> p t n e", t=ST),
                                 rank.unsqueeze(2).broadcast_to([P, ST, NK, NE]), ALU.mult))
            then(V.tensor_reduce(place_f, spare, AX.X, ALU.add))
            then(V.scalar_tensor_tensor(out=place_f, in0=index_f, scalar=float(S), in1=place_f, op0=ALU.mult, op1=ALU.add))
            V.tensor_copy(place, place_f).then_inc(placed_s, 1)
            dve.wait_ge(exped, 2)
            then(V.tensor_reduce(total, weight, AX.X, ALU.add))
            then(V.reciprocal(total, total))
            then(V.tensor_tensor(weight, weight, total.unsqueeze(2).broadcast_to([P, ST, NK]), ALU.mult))
            then(V.tensor_tensor(spare, chosen, e["weight"].unsqueeze(2).broadcast_to([P, NA, NE]), ALU.mult))
            V.tensor_reduce(e["spread"], spare.rearrange("p (t n) e -> p t e n", t=ST), AX.X, ALU.add).then_inc(spread_s, 1)
            dve.wait_ge(bias_split, 1)
            V.tensor_tensor(e["bias_low"], e["bias"], e["bias_high"].bitcast(F32), ALU.subtract)
            dve.wait_ge(spread_turned, 1)
            V.tensor_copy(e["spread_t"], k.psum[0:NE, 3, :])
            dve.wait_ge(list_turned, 1)
            then(V.tensor_copy(value, k.psum[:, 4, 0:P]))
            V.tensor_copy(e["home"], value)
            then(V.tensor_scalar(value, value, 1.0 / NK, -0.375, ALU.mult, ALU.add))
            then(V.tensor_scalar(value, value, float(S - 1), ROUND, ALU.min, ALU.add))
            then(V.tensor_scalar(value, value, ROUND, None, ALU.subtract))
            V.tensor_copy(e["token"], value)

        @block.gpsimd
        def _(pool):
            pool.wait_ge(list_ready, 16)
            pool.wait_ge(placed_s, 1)
            for a in range(NA):
                pool.indirect_dma_start(e["list"], bass.IndirectOffsetOnAxis(ap=place[:, a:a + 1], axis=0),
                                        k.cst("assign")[:, a:a + 1], None).then_inc(scattered, 16)


@stage
def experts(k, e):
    nc = k.nc
    NP = NE + EXTRA
    plan, raw, low, high = e["plan"], e["raw"], e["low"], e["high"]
    half = lambda x, h: x[:, h * NB:(h + 1) * NB]
    names = ("x_in", "x_turned", "x_high_ready", "x_ready", "staged", "chosen", "used", "high_ready", "low_dve", "low_pool",
             "gate_ready", "up_ready", "opened", "gated", "hidden_ready", "hidden_turned", "hidden_high_ready", "hidden_split",
             "y_act", "y_dve", "y_out", "passed")
    (x_in, x_turned, x_high_ready, x_ready, staged, chosen, used, high_ready, low_dve, low_pool, gate_ready, up_ready,
     opened, gated, hidden_ready, hidden_turned, hidden_high_ready, hidden_split, y_act, y_dve, y_out,
     passed) = (k.sem(f"experts_{n}") for n in names)
    during = lambda b, q: PIECES * b + (q + 1)
    pool_before = lambda q: sum(p < q for p in BY_POOL)
    N_POOL = len(BY_POOL)

    def number_of_blocks(engine):
        return engine.value_load(plan[0:1, 2 * NP:2 * NP + 1], min_val=NE, max_val=NBLK)

    def gather_rows(pool):
        pool.indirect_dma_start(e["x_rows"], None, e["tokens_dram"],
                                bass.IndirectOffsetOnAxis(ap=e["token_col"][:, 0:1], axis=0)).then_inc(x_in, 16)

    def turn_rows():
        for d in range(DT):
            i = nc.tensor.transpose(k.psum[:, 4 + d // 4, (d % 4) * P:(d % 4 + 1) * P], e["x_rows"][:, d * P:(d + 1) * P],
                                    k.cst("ident"))
        i.then_inc(x_turned, 1)

    x_banks = k.psum[:, 4:6, :].rearrange("p b s -> p (b s)")

    def take_x_high():
        nc.scalar.activation(e["x_high"], x_banks, ACT.Copy).then_inc(x_high_ready, 1)

    def take_x_low():
        nc.vector.tensor_tensor(e["x_low"], x_banks, e["x_high"].bitcast(F32), ALU.subtract).then_inc(x_ready, 1)

    def take_high(act, b, q):
        act.wait_ge(e["in"][q], 16 * b + 16)
        nc.scalar.activation(high[q % NHI], raw[:, q, :], ACT.Copy).then_inc(high_ready, 1)

    def take_low(engine, compute, b, q, done):
        engine.wait_ge(high_ready, PIECES * b + (q + 1))
        compute.tensor_tensor(low[q], raw[:, q, :], high[q % NHI].bitcast(F32), ALU.subtract).then_inc(done, 1)

    with nc.Block() as block:
        @block.sync
        def _(sp):
            n = number_of_blocks(sp)
            with sp.Fori(1, NBLK) as b:
                with sp.If(b < n):
                    expert = sp.value_load(plan[0:1, bass.ds(b, 1)], min_val=0, max_val=NE - 1)
                    for q in range(PIECES):
                        sp.wait_ge(used, PIECES * b + (q + 2 - PIECES))
                        load_expert_piece(k, e, sp, q, expert)

        @block.gpsimd
        def _(pool):
            n = number_of_blocks(pool)
            column = pool.value_load(plan[0:1, NP:NP + 1], min_val=0, max_val=P - 1)
            nc.gpsimd.tensor_copy(e["token_col"][:, 0:1], e["token"][:, bass.ds(column, 1)]).then_inc(staged, 1)
            nc.gpsimd.tensor_copy(e["choice"], k.cst("ident")[0:NE, 0:1].broadcast_to([NE, CAP])).then_inc(chosen, 1)
            pool.wait_ge(staged, 1)
            gather_rows(pool)
            with pool.Fori(0, NBLK) as b:
                with pool.If(b < n):
                    column = pool.value_load(plan[0:1, bass.ds(b + NP, 1)], min_val=0, max_val=P - 1)
                    next_column = pool.value_load(plan[0:1, bass.ds(b + NP + 1, 1)], min_val=0, max_val=P - 1)
                    next_expert = pool.value_load(plan[0:1, bass.ds(b + 1, 1)], min_val=0, max_val=NE - 1)
                    pool.wait_ge(x_turned, b + 1)
                    nc.gpsimd.tensor_copy(e["token_col"][:, 0:1], e["token"][:, bass.ds(next_column, 1)]).then_inc(staged, 1)
                    pool.wait_ge(staged, 2 * b + 2)
                    pool.sem_inc(passed, 1)
                    gather_rows(pool)
                    for h in range(2):
                        if h == 1:
                            with pool.If(b > 0):
                                pool.wait_ge(y_out, 16 * b)
                            nc.gpsimd.tensor_copy(e["home_col"][:, 0:1], e["home"][:, bass.ds(column, 1)]).then_inc(staged, 1)
                        pool.wait_ge(opened, 2 * b + h + 1)
                        nc.gpsimd.tensor_tensor(half(e["open"], h), half(e["gate"], h), half(e["open"], h), ALU.mult).then_inc(gated, 1)
                        take_low(pool, nc.gpsimd, b, BY_POOL[h], low_pool)
                    pool.wait_ge(y_act, b + 1)
                    pool.wait_ge(y_dve, b + 1)
                    nc.gpsimd.tensor_copy(e["choice"], k.cst("ident")[0:NE, bass.ds(next_expert, 1)].broadcast_to([NE, CAP])).then_inc(chosen, 1)
                    pool.wait_ge(staged, 2 * b + 3)
                    pool.sem_inc(passed, 1)
                    pool.indirect_dma_start(e["routed"], bass.IndirectOffsetOnAxis(ap=e["home_col"][:, 0:1], axis=0),
                                            e["y"], None).then_inc(y_out, 16)
            pool.wait_ge(y_out, 16 * n)
            pool.wait_ge(x_in, 16 * n + 16)

        @block.tensor
        def _(pe):
            n = number_of_blocks(pe)
            pe.wait_ge(x_in, 16)
            nc.tensor.transpose(k.psum[:, 0, 0:P], k.cst("ident"), k.cst("ident")).then_inc(used, 1)
            turn_rows()

            def turn_hidden(b, h):
                pe.wait_ge(hidden_ready, 2 * b + h + 1)
                for f in range(4):
                    i = nc.tensor.transpose(k.psum[:, 2 * h, f * P:(f + 1) * P], e["gate"][:, (4 * h + f) * P:(4 * h + f + 1) * P],
                                            k.cst("ident"))
                i.then_inc(hidden_turned, 1)

            with pe.Fori(0, NBLK) as b:
                with pe.If(b < n):
                    pe.wait_ge(x_ready, b + 1)
                    for q in range(PIECES):
                        if q in BY_POOL:
                            pe.wait_ge(low_pool, N_POOL * b + (pool_before(q) + 1))
                        else:
                            pe.wait_ge(low_dve, (PIECES - N_POOL) * b + (q + 1 - pool_before(q)))
                        if q < 8:
                            r = q // 2
                            w = [x.rearrange("p (d f) -> p d f", d=4) for x in (high[q % NHI], low[q])]
                            for j in range(4):
                                d = 4 * (q % 2) + j
                                x = [t[:, d * P:(d + 1) * P] for t in (e["x_high"], e["x_low"])]
                                i = exact_product(nc, k.psum[:, r, :], x, (w[0][:, j, :], w[1][:, j, :]), start=(d == 0), stop=False)
                            if q % 2 == 1:
                                if q == 1:
                                    pe.wait_ge(chosen, b + 1)
                                at = (r % 2) * D + (r // 2) * NB
                                for bias in (e["bias_high"], e["bias_low"]):
                                    i = nc.tensor.matmul(k.psum[:, r, :], e["choice"], bias[:, at:at + NB],
                                                         start=False, stop=(bias is e["bias_low"]))
                        else:
                            w = [x.rearrange("p (f c) -> p f c", f=2) for x in (high[q % NHI], low[q])]
                            if q % 2 == 0:
                                pe.wait_ge(hidden_split, 2 * b + ((q - 8) // 2 + 1))
                            for j in range(2):
                                f = 2 * (q - 8) + j
                                x = [t[:, f * P:(f + 1) * P] for t in (e["hidden_high"], e["hidden_low"])]
                                for c in range(2):
                                    i = exact_product(nc, k.psum[:, 6 + c, :], x, [t[:, j, c * NB:(c + 1) * NB] for t in w],
                                                      start=(f == 0), stop=(f == DT - 1))
                        i.then_inc(used, 1)
                        if q == 5:
                            turn_hidden(b, 0)
                        if q == 7:
                            pe.wait_ge(x_in, 16 * b + 32)
                            turn_rows()
                        if q == 8:
                            turn_hidden(b, 1)

        @block.scalar
        def _(act):
            n = number_of_blocks(act)
            for q in range(2):
                take_high(act, 0, q)
            act.wait_ge(x_turned, 1)
            take_x_high()

            def open_gate(b, h):
                act.wait_ge(gate_ready, 2 * b + h + 1)
                nc.scalar.activation(half(e["open"], h), half(e["gate"], h), ACT.Sigmoid, scale=ALPHA).then_inc(opened, 1)

            def take_hidden_high(b, h):
                act.wait_ge(hidden_turned, 2 * b + h + 1)
                nc.scalar.activation(half(e["hidden_high"], h), k.psum[:, 2 * h, :], ACT.Copy).then_inc(hidden_high_ready, 1)

            with act.Fori(0, NBLK) as b:
                with act.If(b < n):
                    for q in range(PIECES):
                        if q == 9:
                            take_hidden_high(b, 1)
                        if q + 2 < PIECES:
                            act.wait_ge(used, during(b, q))
                            take_high(act, b, q + 2)
                        else:
                            with act.If(b + 1 < n):
                                act.wait_ge(used, during(b, q))
                                take_high(act, b + 1, q + 2 - PIECES)
                        if q == 2:
                            open_gate(b, 0)
                        if q == 6:
                            take_hidden_high(b, 0)
                            open_gate(b, 1)
                        if q == 8:
                            act.wait_ge(x_turned, b + 2)
                            take_x_high()
                    act.wait_ge(used, during(b, PIECES))
                    nc.scalar.activation(half(e["y"], 0), k.psum[:, 6, :], ACT.Copy).then_inc(y_act, 1)

        @block.vector
        def _(dve):
            V = nc.vector
            n = number_of_blocks(dve)
            for q in range(2):
                take_low(dve, V, 0, q, low_dve)
            dve.wait_ge(x_high_ready, 1)
            take_x_low()

            def clip_gate(b, h):
                dve.wait_ge(used, during(b, 4 * h + 2))
                V.tensor_scalar(half(e["gate"], h), k.psum[:, 2 * h, :], LIMIT, None, ALU.min).then_inc(gate_ready, 1)

            def hide(b, h):
                dve.wait_ge(used, during(b, 4 * h + 4))
                V.tensor_scalar(half(e["up"], h), k.psum[:, 2 * h + 1, :], LIMIT, -LIMIT, ALU.min, ALU.max).then_inc(up_ready, 1)
                dve.wait_ge(up_ready, 2 * b + h + 1)
                dve.wait_ge(gated, 2 * b + h + 1)
                V.scalar_tensor_tensor(out=half(e["gate"], h), in0=half(e["up"], h), scalar=1.0, in1=half(e["open"], h),
                                       op0=ALU.add, op1=ALU.mult).then_inc(hidden_ready, 1)

            def take_hidden_low(b, h):
                dve.wait_ge(hidden_high_ready, 2 * b + h + 1)
                V.tensor_tensor(half(e["hidden_low"], h), k.psum[:, 2 * h, :], half(e["hidden_high"], h).bitcast(F32), ALU.subtract).then_inc(hidden_split, 1)

            with dve.Fori(0, NBLK) as b:
                with dve.If(b < n):
                    for q in range(PIECES):
                        if q == 2:
                            clip_gate(b, 0)
                        if q == 4:
                            hide(b, 0)
                        if q == 6:
                            clip_gate(b, 1)
                        if q == 8:
                            hide(b, 1)
                        if q == 9:
                            take_hidden_low(b, 1)
                        if (q + 2) % PIECES not in BY_POOL:
                            if q + 2 < PIECES:
                                take_low(dve, V, b, q + 2, low_dve)
                            else:
                                with dve.If(b + 1 < n):
                                    take_low(dve, V, b + 1, q + 2 - PIECES, low_dve)
                        if q == 6:
                            take_hidden_low(b, 0)
                        if q == 8:
                            dve.wait_ge(x_high_ready, b + 2)
                            take_x_low()
                    dve.wait_ge(used, during(b, PIECES))
                    V.tensor_copy(half(e["y"], 1), k.psum[:, 7, :]).then_inc(y_dve, 1)


@stage
def combine(k, e, stored):
    nc = k.nc
    rows = k.arena[:, 0:ST * NK * D].rearrange("p (t n d) -> p t n d", t=ST, n=NK)
    diag = k.turned_flat[:, 0:2 * ST * P].rearrange("p (n s) -> p n s", n=2 * ST)
    acc = k.turned_flat[:, 2 * D:4 * D].rearrange("p (n d) -> p n d", n=2)
    b_down = k.turned_flat[0:NE, 4 * D:5 * D]
    g_m = k.gate_rows[:, D:2 * D]
    names = ("diagonals", "product", "partial", "summed", "gated", "added")
    diagonals, product, partial, summed, gated, added = (k.sem(f"combine_{n}") for n in names)
    biases_in = k.sem("combine_biases_in")
    rows_in = [k.sem(f"combine_rows_in_{t}") for t in range(ST)]

    def add_tile(V, dve, t):
        dve.wait_ge(gated, t + 1)
        V.tensor_tensor(k.resid[:, t, :], rows[:, t, 0, :], k.resid[:, t, :], ALU.add).then_inc(added, 1)

    with nc.Block() as block:
        @block.sync
        def _(sp):
            src = e["routed"][0:S * NK].rearrange("(t p n) d -> t p n d", t=ST, p=P)
            sp.dma_start(b_down, k.io["b_down"]).then_inc(biases_in, 16)
            for t in range(ST):
                sp.dma_start(rows[:, t], src[t]).then_inc(rows_in[t], 16)
            for t in range(ST):
                sp.wait_ge(added, t + 1)
                sp.dma_start(k.io["out"][t * P:(t + 1) * P, :], k.resid[:, t, :]).then_inc(stored, 16)
            sp.wait_ge(stored, 16 * ST)

        @block.tensor
        def _(pe):
            for t in range(ST):
                pe.wait_ge(rows_in[t], 16)
                pe.wait_ge(biases_in, 16)
                pe.wait_ge(diagonals, 2 * t + 2)
                for c in range(2):
                    for n in range(2):
                        nc.tensor.matmul(k.psum[:, 2 * t + c, :], diag[:, 2 * t + n, :], rows[:, t, n, c * NB:(c + 1) * NB],
                                         start=(n == 0), stop=False)
                    i = nc.tensor.matmul(k.psum[:, 2 * t + c, :], e["spread_t"][:, t * P:(t + 1) * P],
                                         b_down[:, c * NB:(c + 1) * NB], start=False, stop=True)
                i.then_inc(product, 1)

        @block.vector
        def _(dve):
            V = nc.vector
            w = lambda t, n: e["weight"][:, NK * t + n:NK * t + n + 1]
            for t in range(ST):
                for n in range(2):
                    V.tensor_scalar(diag[:, 2 * t + n, :], k.cst("ident"), w(t, n), None, ALU.mult).then_inc(diagonals, 1)
            for t in range(ST):
                dve.wait_ge(product, t + 1)
                if t >= 2:
                    dve.wait_ge(gated, t - 1)
                V.scalar_tensor_tensor(out=acc[:, t % 2], in0=rows[:, t, 2, :], scalar=w(t, 2),
                                       in1=k.psum[:, 2 * t:2 * t + 2, :].rearrange("p b s -> p (b s)"),
                                       op0=ALU.mult, op1=ALU.add).then_inc(partial, 1)
                dve.wait_ge(partial, t + 1)
                V.scalar_tensor_tensor(out=acc[:, t % 2], in0=rows[:, t, 3, :], scalar=w(t, 3), in1=acc[:, t % 2],
                                       op0=ALU.mult, op1=ALU.add).then_inc(summed, 1)
                if t >= 1:
                    add_tile(V, dve, t - 1)
            add_tile(V, dve, ST - 1)

        @block.gpsimd
        def _(pool):
            for t in range(ST):
                pool.wait_ge(summed, t + 1)
                nc.gpsimd.tensor_tensor(rows[:, t, 0, :], acc[:, t % 2], g_m, ALU.mult).then_inc(gated, 1)


def shape_constants():
    out = np.zeros((P, NCONST), np.float32)

    def put(name, a):
        at, width = CONST[name]
        out[:, at:at + width] = np.asarray(a, np.float32).reshape(P, width)

    i = np.arange(P)
    put("ident", np.eye(P))
    put("ones", np.ones((P, P)))
    put("before", i[:, None] < i[None, :])
    pos = np.arange(S, dtype=np.float32)
    half = HD // 2
    inv = np.power(np.float32(10000.0), -np.arange(half, dtype=np.float32) * np.float32(2.0) / np.float32(HD)).astype(np.float32)
    ang = (pos[:, None] * inv[None, :]).astype(np.float32)
    tiles = lambda a: a.reshape(ST, P, -1).transpose(1, 0, 2)
    put("rope1", np.stack([tiles(np.cos(ang.astype(np.float64))), tiles(np.sin(ang.astype(np.float64)))], 1))
    pairs, grid_w = HD // 4, 64
    row, col = np.repeat(np.arange(S // grid_w), grid_w), np.tile(np.arange(grid_w), S // grid_w)
    inv = (np.float32(1.0) / np.power(np.float32(10000.0), np.arange(pairs, dtype=np.float32) / np.float32(pairs))).astype(np.float32)
    ang = np.concatenate([row.astype(np.float32)[:, None] * inv, col.astype(np.float32)[:, None] * inv], -1).astype(np.float32)
    put("rope2", np.stack([tiles(np.cos(ang.astype(np.float64))), tiles(np.sin(ang.astype(np.float64)))], 1))
    put("iota_e", np.tile(np.arange(NE), (P, 1)))
    tok = np.arange(ST)[None, :, None] * P + i[:, None, None]
    put("assign", tok * NK + np.arange(NK))
    return out


def columns(a):
    return np.ascontiguousarray(np.asarray(a).reshape(-1, P).T)


def chunks_by_columns(w, width=NB):
    kk, n = w.shape
    return w.reshape(kk // P, P, n // width, width).transpose(2, 1, 0, 3).reshape(n // width, P, -1)


def lay_out(inp):
    g = {n: np.asarray(a) for n, a in inp.items()}
    cols = np.zeros((P, NCOLS), np.float32)

    def put(name, a):
        at, width = COLS[name]
        cols[:, at:at + width] = a.reshape(P, width)

    put("gains", columns(g["norm_g"].reshape(-1)))
    put("ssm_d", columns(g["ssm_d"].reshape(-1)))
    states = lambda a: a.reshape(NJ, P).T
    put("lam_re", states(g["ssm_lam_re"][0]))
    put("lam_im", states(g["ssm_lam_im"][0]))
    put("log_dt", states(np.repeat(g["ssm_log_dt"][0][:, None], 64, 1)))
    put("cond", np.stack([columns(g["c_2"].reshape(-1)), columns(g["c_ctx_2"])], 2))
    put("b_ada", columns(g["b_ada_2"][0]))
    put("norm_attn", columns(g["norm_attn_2"][0]))
    put("norm_mlp", columns(g["norm_mlp_2"][0]))
    put("subln", columns(g["subln_b_2"][0]))
    lam = np.zeros((P, 4), np.float32)
    for i, n in enumerate(("lambda_q1_2", "lambda_k1_2", "lambda_q2_2", "lambda_k2_2")):
        lam[:HD, i] = g[n][0]
    put("lambdas", lam)

    bc = np.zeros((P, 4, NJ, 32), np.float32)
    for i, n in enumerate(("ssm_b_re", "ssm_b_im")):
        b = g[n][0].reshape(NJ, 2, 64, 16)
        for gg in range(2):
            bc[64 * gg:64 * gg + 64, i, :, 16 * gg:16 * gg + 16] = b[:, gg].transpose(1, 0, 2)
    for i, n in enumerate(("ssm_c_re", "ssm_c_im")):
        c = g[n][0].reshape(NJ, 2, 16, 64)
        for gg in range(2):
            bc[64 * gg:64 * gg + 64, 2 + i, :, 16 * gg:16 * gg + 16] = c[:, gg].transpose(2, 0, 1)

    dense = np.zeros((NDENSE, P, CHUNK), np.float32)

    def fill(name, a):
        at = FIRST[name]
        dense[at:at + len(a), :, :a.shape[2]] = a

    def by_rows(w):
        return w.reshape(-1, 4, P, D).transpose(0, 2, 1, 3).reshape(-1, P, CHUNK)

    fill("ssm_in", chunks_by_columns(g["ssm_w_in"][0]))
    fill("ssm_glu", chunks_by_columns(g["ssm_w_glu"][0]))
    fill("ssm_out", by_rows(g["ssm_w_out"][0]))
    fill("ada", chunks_by_columns(g["w_ada_2"][0]))
    for i in range(2):
        fill(f"w1_{i}", chunks_by_columns(g["mlp_w1"][i]))
        fill(f"w2_{i}", by_rows(g["mlp_w2"][i]))
    fill("att_in", chunks_by_columns(g["att_w_in"][0][:, :2048]))
    fill("att_idx", chunks_by_columns(g["att_w_in"][0][:, 2048:], 72))
    fill("att_out", by_rows(g["att_w_out"][0]))
    w = g["w_in_2"][0]
    fill("qa", chunks_by_columns(w[:, 0:512]))
    fill("kva", chunks_by_columns(w[:, 512:768], 256))
    fill("qb", chunks_by_columns(w[:, 768:1280]))
    fill("kb", chunks_by_columns(w[:, 1280:1792]))
    fill("vb", chunks_by_columns(w[:, 1792:2304]))
    for h, end in enumerate(("", "1")):
        half = slice(h * NB, (h + 1) * NB)
        fill("ga" + end, chunks_by_columns(w[:, 2304:3328][:, half]))
        fill("gb" + end, chunks_by_columns(w[:, 3328:4352][:, half]))
        fill("w_oa" + end, chunks_by_columns(g["w_oa_2"][0][:, half]))
        fill("w_ob" + end, chunks_by_columns(g["w_ob_2"][0][:, half]))
    fill("w_out", by_rows(g["w_out_2"][0]))
    rows = np.zeros((12, D), np.float32)
    rows[0:8] = g["norm_g"].reshape(8, D)
    rows[8, 0:4 * HD] = np.concatenate([g[n][0] for n in ("q_norm_a_2", "k_norm_a_2", "q_norm_b_2", "k_norm_b_2")])
    rows[9, 0:NE] = g["router_b_2"][0]
    gate = g["w_gate_2"][0].reshape(NE, DT, P, 2, NB).transpose(0, 3, 2, 1, 4).reshape(NE * 2, P, CHUNK)
    up = g["w_up_2"][0].reshape(NE, DT, P, 2, NB).transpose(0, 3, 2, 1, 4).reshape(NE * 2, P, CHUNK)
    down = g["w_down_2"][0].reshape(NE, 2, 4, P, D).transpose(0, 1, 3, 2, 4).reshape(NE * 2, P, CHUNK)
    pad = np.tile(S * NK + np.arange(P, dtype=np.float32), (4 * NE, 1))
    return {
        "x": g["x"].reshape(S, D), "ctx": g["ctx_2"].reshape(CTX, D), "cols": cols, "consts": shape_constants(),
        "ssm_bc": bc.reshape(P, -1), "dense": dense, "rows": rows, "moe_bias": np.concatenate([g["b_gate_2"][0], g["b_up_2"][0]], 1),
        "router": chunks_by_columns(g["router_w_2"][0], NE)[0], "b_down": g["b_down_2"][0],
        "gate": np.ascontiguousarray(gate), "up": np.ascontiguousarray(up), "down": np.ascontiguousarray(down),
        "pad_list": pad.reshape(4 * NE * P, 1),
    }


_SHAPES = {
    "x": (S, D), "ctx": (CTX, D), "cols": (P, NCOLS), "consts": (P, NCONST), "ssm_bc": (P, 4 * NJ * 32),
    "dense": (NDENSE, P, CHUNK), "rows": (12, D), "moe_bias": (NE, 2 * D), "router": (P, DT * NE),
    "b_down": (NE, D), "gate": (2 * NE, P, CHUNK), "up": (2 * NE, P, CHUNK), "down": (2 * NE, P, CHUNK),
    "pad_list": (4 * NE * P, 1),
}


def program(nc, io):
    with ExitStack() as ctx:
        k = Kernel(nc, ctx, io)
        k.stored = nc.alloc_semaphore(name="output_stored")
        gains, row = k.col("gains"), k.io["rows"]
        gain = lambda n: gains[:, n * DT:(n + 1) * DT]
        stages(k, gain, row)


def stages(k, gain, row):
    load_inputs(k)
    norm_turned(k, "ssm_norm", k.resid, ST, 0, gain(0))
    ssm_parameters(k)
    ssm_tables(k)
    ssm_scan(k)
    lhs = ssm_gate(k)
    project_residual(k, "ssm_out", FIRST["ssm_out"], 1, lhs, row[1], True)
    norm_turned(k, "mlp0_norm", k.resid, ST, 0, gain(2), None, True, FIRST["w1_0"])
    lhs = mlp_hidden(k, "mlp0_hidden", FIRST["w1_0"])
    project_residual(k, "mlp0_out", FIRST["w2_0"], 8, lhs, row[3], True)
    norm_turned(k, "att_norm", k.resid, ST, 0, gain(4), None, True, FIRST["att_in"])
    a = attention_layout(k)
    attention_project(k, a)
    attention_select(k, a)
    lhs = attention_heads(k, a)
    project_residual(k, "att_out", FIRST["att_out"], 2, lhs, row[5], True)
    norm_turned(k, "mlp1_norm", k.resid, ST, 0, gain(6), None, True, FIRST["w1_1"])
    lhs = mlp_hidden(k, "mlp1_hidden", FIRST["w1_1"])
    project_residual(k, "mlp1_out", FIRST["w2_1"], 8, lhs, row[7], True)
    context = modulation(k)
    affine = k.affine[:, :].rearrange("p (n d) -> p n d", n=6)
    norm_turned(k, "ctx_norm", context, CT, S, affine[:, 2], affine[:, 3])
    norm_turned(k, "blend_norm", k.resid, ST, 0, affine[:, 0], affine[:, 1])
    b = blend_layout(k)
    blend_project(k, b)
    blend_heads_a(k, b)
    blend_heads_b(k, b)
    blend_subnorm(k, b)
    lhs = blend_merge(k, b)
    project_residual(k, "blend_out", FIRST["w_out"], 2, lhs, k.gate_rows[:, 0:D], False)
    norm_turned(k, "moe_norm", k.resid, ST, 0, affine[:, 4], affine[:, 5])
    e = expert_layout(k)
    route(k, e)
    experts(k, e)
    combine(k, e, k.stored)


def kernel(**inputs):
    import concourse.bacc as bacc
    from concourse.bass_utils import run_bass_kernel_spmd

    nc = bacc.Bacc("TRN2", target_bir_lowering=False, num_devices=1)
    io = {n: nc.dram_tensor(f"in_{n}", s, F32, kind="ExternalInput").ap() for n, s in _SHAPES.items()}
    io["out"] = nc.dram_tensor("out_0", (S, D), F32, kind="ExternalOutput").ap()
    program(nc, io)
    arrays = {f"in_{n}": np.ascontiguousarray(a) for n, a in lay_out(inputs).items()}
    r = run_bass_kernel_spmd(nc, [arrays], core_ids=[0])
    return r.results[0]["out_0"].reshape(1, S, D)
```
